# Optimizing a Trainium2 kernel written in Bass

```python
import math
import jax, jax.numpy as jnp
from jax import lax
import numpy as np

D_MODEL = 1024
BATCH = 1
SEQ = 256
DEPTH = 2

N_MIXERS = 2
ROPE_THETA = 500000.0
ROT_DIM = 16
Q_BLOCK = 128
NORM_EPS = 1e-6
NEG_INF = -1e30

DA_HEAD_DIM = 64
DA_V_DIM = 2 * DA_HEAD_DIM
DA_HEADS = D_MODEL // DA_V_DIM

NSA_HEAD_DIM = 64
NSA_HEADS = D_MODEL // NSA_HEAD_DIM
NSA_KV_GROUPS = 2
NSA_HEADS_PER_GROUP = NSA_HEADS // NSA_KV_GROUPS
NSA_CMP_BLOCK = 32
NSA_CMP_STRIDE = 16
NSA_CMP_HIDDEN = 4 * NSA_HEAD_DIM
NSA_SEL_BLOCK = 64
NSA_TOP_N = 16
NSA_WINDOW = 512
NSA_FORCE = 1e4
NSA_IN_DIM = NSA_HEADS * NSA_HEAD_DIM + 6 * NSA_KV_GROUPS * NSA_HEAD_DIM + 3 * NSA_HEADS

MOE_GROUPS = 4
MOE_EXPERTS_PER_GROUP = 8
MOE_EXPERTS = MOE_GROUPS * MOE_EXPERTS_PER_GROUP
MOE_TOP_K = 2
MOE_HIDDEN = D_MODEL // 4


def _rmsnorm(x, g):
    xf = x.astype(jnp.float32)
    y = xf * lax.rsqrt(jnp.mean(xf * xf, axis=-1, keepdims=True) + NORM_EPS)
    return (y * g.astype(jnp.float32)).astype(x.dtype)

def _rope_tables(positions):
    inv_freq = ROPE_THETA ** (-jnp.arange(0, ROT_DIM, 2, dtype=jnp.float32) / ROT_DIM)
    ang = positions.astype(jnp.float32)[..., None] * inv_freq
    return jnp.cos(ang)[:, :, None, :], jnp.sin(ang)[:, :, None, :]

def _rotary(x, cos, sin):
    half = ROT_DIM // 2
    xr = x[..., :ROT_DIM].astype(jnp.float32)
    x1, x2 = xr[..., :half], xr[..., half:]
    rot = jnp.concatenate([x1 * cos - x2 * sin, x2 * cos + x1 * sin], axis=-1).astype(x.dtype)
    return jnp.concatenate([rot, x[..., ROT_DIM:]], axis=-1)

def _masked_softmax(s, mask):
    s = jnp.where(mask, s.astype(jnp.float32), NEG_INF)
    p = jnp.where(mask, jnp.exp(s - jnp.max(s, axis=-1, keepdims=True)), 0.0)
    return p / jnp.maximum(jnp.sum(p, axis=-1, keepdims=True), 1e-30)

def diff_attention(h, cos, sin, w_in, w_out, lam, subln_g, lambda_init):
    B, S, D = h.shape
    H, d = DA_HEADS, DA_HEAD_DIM
    q, k, v = jnp.split(h @ w_in, 3, axis=-1)
    q = _rotary(q.reshape(B, S, 2 * H, d), cos, sin).reshape(B, S, H, 2, d).transpose(3, 0, 2, 1, 4)
    k = _rotary(k.reshape(B, S, 2 * H, d), cos, sin).reshape(B, S, H, 2, d).transpose(3, 0, 2, 1, 4)
    v = v.reshape(B, S, H, DA_V_DIM).transpose(0, 2, 1, 3)
    lam = lam.astype(jnp.float32)
    lam_full = jnp.exp(jnp.sum(lam[0] * lam[1])) - jnp.exp(jnp.sum(lam[2] * lam[3])) + lambda_init
    scale = d ** -0.5
    k_pos = jnp.arange(S)

    def block(i):
        q0 = i * Q_BLOCK
        qb = lax.dynamic_slice_in_dim(q, q0, Q_BLOCK, axis=3)
        s = jnp.einsum('cbhqd,cbhkd->cbhqk', qb, k) * scale
        mask = k_pos[None, :] <= (q0 + jnp.arange(Q_BLOCK))[:, None]
        p = _masked_softmax(s, mask)
        a = p[0] - lam_full * p[1]
        return jnp.einsum('bhqk,bhkv->bhqv', a.astype(v.dtype), v)

    o = lax.map(block, jnp.arange(S // Q_BLOCK))
    o = o.transpose(1, 0, 3, 2, 4).reshape(B, S, H, DA_V_DIM)
    o = _rmsnorm(o, subln_g) * (1.0 - lambda_init)
    return o.reshape(B, S, D) @ w_out

def _nsa_compress(t, pos_emb, w1, b1, w2):
    B, G, S, d = t.shape
    ch = t.reshape(B, G, S // NSA_CMP_STRIDE, NSA_CMP_STRIDE, d)
    blk = jnp.concatenate([ch[:, :, :-1], ch[:, :, 1:]], axis=3) + pos_emb
    blk = blk.reshape(B, G, blk.shape[2], NSA_CMP_BLOCK * d)
    return jax.nn.gelu(blk @ w1 + b1) @ w2

def nsa_attention(h, cos, sin, w_in, w_out, cmp_pos, cmp_w1, cmp_b1, cmp_w2):
    B, S, D = h.shape
    H, G, Hg, d = NSA_HEADS, NSA_KV_GROUPS, NSA_HEADS_PER_GROUP, NSA_HEAD_DIM
    kvw = G * d
    proj = h @ w_in
    bounds = [H * d + j * kvw for j in range(7)]
    q, k_c, v_c, k_s, v_s, k_w, v_w, g_raw = jnp.split(proj, bounds, axis=-1)
    q = _rotary(q.reshape(B, S, H, d), cos, sin).reshape(B, S, G, Hg, d).transpose(0, 2, 3, 1, 4)

    def kv(t, rope):
        t = t.reshape(B, S, G, d)
        if rope:
            t = _rotary(t, cos, sin)
        return t.transpose(0, 2, 1, 3)

    k_c, v_c = kv(k_c, False), kv(v_c, False)
    k_s, v_s = kv(k_s, True), kv(v_s, True)
    k_w, v_w = kv(k_w, True), kv(v_w, True)
    gates = jax.nn.sigmoid(g_raw.astype(jnp.float32)).reshape(B, S, G, Hg, 3).transpose(0, 2, 3, 1, 4)

    k_cmp = _nsa_compress(k_c, cmp_pos[0], cmp_w1[0], cmp_b1[0], cmp_w2[0])
    v_cmp = _nsa_compress(v_c, cmp_pos[1], cmp_w1[1], cmp_b1[1], cmp_w2[1])
    n_cmp = k_cmp.shape[2]
    n_sel = S // NSA_SEL_BLOCK
    n_top = min(NSA_TOP_N, n_sel)
    cmp_start = jnp.arange(n_cmp) * NSA_CMP_STRIDE
    cmp_end = cmp_start + NSA_CMP_BLOCK - 1
    sel_start = jnp.arange(n_sel) * NSA_SEL_BLOCK
    cmp_to_sel = ((cmp_start[:, None] < sel_start[None, :] + NSA_SEL_BLOCK)
                  & (cmp_start[:, None] + NSA_CMP_BLOCK > sel_start[None, :])).astype(jnp.float32)
    k_blocks = k_s.reshape(B, G, n_sel, NSA_SEL_BLOCK, d)
    v_blocks = v_s.reshape(B, G, n_sel, NSA_SEL_BLOCK, d)
    pad = ((0, 0), (0, 0), (NSA_WINDOW, 0), (0, 0))
    k_w_pad, v_w_pad = jnp.pad(k_w, pad), jnp.pad(v_w, pad)
    b_ix = jnp.arange(B)[:, None, None, None]
    g_ix = jnp.arange(G)[None, :, None, None]
    blk_off = jnp.arange(NSA_SEL_BLOCK)
    sel_ids = jnp.arange(n_sel)
    scale = d ** -0.5

    def block(i):
        q0 = i * Q_BLOCK
        tq = q0 + jnp.arange(Q_BLOCK)
        qb = lax.dynamic_slice_in_dim(q, q0, Q_BLOCK, axis=3)
        s_c = jnp.einsum('bghqd,bgnd->bghqn', qb, k_cmp) * scale
        p_c = _masked_softmax(s_c, cmp_end[None, :] <= tq[:, None])
        o_c = jnp.einsum('bghqn,bgnd->bghqd', p_c.astype(v_cmp.dtype), v_cmp)
        imp = jnp.einsum('bgqn,ns->bgqs', p_c.sum(axis=2), cmp_to_sel)
        q_blk = tq // NSA_SEL_BLOCK
        forced = ((sel_ids[None, :] == 0) | (sel_ids[None, :] == q_blk[:, None])
                  | (sel_ids[None, :] == q_blk[:, None] - 1))
        causal = sel_ids[None, :] <= q_blk[:, None]
        imp = jnp.where(forced, NSA_FORCE, jnp.where(causal, imp, -NSA_FORCE))
        _, sel = lax.top_k(imp, n_top)
        k_sel = k_blocks[b_ix, g_ix, sel].reshape(B, G, Q_BLOCK, n_top * NSA_SEL_BLOCK, d)
        v_sel = v_blocks[b_ix, g_ix, sel].reshape(B, G, Q_BLOCK, n_top * NSA_SEL_BLOCK, d)
        tok = (sel[..., None] * NSA_SEL_BLOCK + blk_off).reshape(B, G, Q_BLOCK, n_top * NSA_SEL_BLOCK)
        s_s = jnp.einsum('bghqd,bgqkd->bghqk', qb, k_sel) * scale
        p_s = _masked_softmax(s_s, tok[:, :, None] <= tq[:, None])
        o_s = jnp.einsum('bghqk,bgqkd->bghqd', p_s.astype(v_sel.dtype), v_sel)
        k_win = lax.dynamic_slice_in_dim(k_w_pad, q0, Q_BLOCK + NSA_WINDOW, axis=2)
        v_win = lax.dynamic_slice_in_dim(v_w_pad, q0, Q_BLOCK + NSA_WINDOW, axis=2)
        tk = q0 - NSA_WINDOW + jnp.arange(Q_BLOCK + NSA_WINDOW)
        dist = tq[:, None] - tk[None, :]
        mask_w = (tk[None, :] >= 0) & (dist >= 0) & (dist < NSA_WINDOW)
        s_w = jnp.einsum('bghqd,bgkd->bghqk', qb, k_win) * scale
        p_w = _masked_softmax(s_w, mask_w)
        o_w = jnp.einsum('bghqk,bgkd->bghqd', p_w.astype(v_win.dtype), v_win)
        gb = lax.dynamic_slice_in_dim(gates, q0, Q_BLOCK, axis=3)
        o = gb[..., 0:1] * o_c + gb[..., 1:2] * o_s + gb[..., 2:3] * o_w
        return o.astype(h.dtype)

    o = lax.map(block, jnp.arange(S // Q_BLOCK))
    o = o.transpose(1, 0, 4, 2, 3, 5).reshape(B, S, D)
    return o @ w_out

def hier_moe(h, w_grp, b_grp, w_exp, b_exp, w_gate, w_up, w_down):
    B, S, D = h.shape
    t = h.reshape(B * S, D)
    T = t.shape[0]
    pg = jax.nn.softmax((t @ w_grp).astype(jnp.float32) + b_grp, axis=-1)
    p_top, grp = lax.top_k(pg, 1)
    le = jnp.einsum('td,gde->tge', t, w_exp).astype(jnp.float32) + b_exp
    le_sel = le[jnp.arange(T), grp[:, 0]]
    val, idx = lax.top_k(le_sel, MOE_TOP_K)
    wts = jax.nn.softmax(val, axis=-1) * p_top
    eid = grp * MOE_EXPERTS_PER_GROUP + idx
    combine = jnp.sum(jax.nn.one_hot(eid, MOE_EXPERTS, dtype=jnp.float32) * wts[..., None], axis=1)
    y = jnp.zeros_like(t)
    for gi in range(MOE_GROUPS):
        sl = slice(gi * MOE_EXPERTS_PER_GROUP, (gi + 1) * MOE_EXPERTS_PER_GROUP)
        a = jax.nn.silu(jnp.einsum('td,edh->teh', t, w_gate[sl])) * jnp.einsum('td,edh->teh', t, w_up[sl])
        a = a * combine[:, sl, None].astype(a.dtype)
        y = y + jnp.einsum('teh,ehd->td', a, w_down[sl]).astype(t.dtype)
    return y.reshape(B, S, D)

def first_inputs(seed: int = 0) -> dict:
    key = jax.random.key(seed)
    ks = iter(jax.random.split(key, 32))
    D = D_MODEL
    n_a = (DEPTH + N_MIXERS - 1) // N_MIXERS
    n_b = DEPTH // N_MIXERS

    def nrm(shape, scale):
        return jax.random.normal(next(ks), shape, jnp.float32) * scale

    return {
        'x': nrm((BATCH, SEQ, D), 1.0),
        'c': nrm((BATCH, D), 1.0),
        'positions': (jax.random.randint(next(ks), (BATCH, 1), 0, 4096) + jnp.arange(SEQ)[None, :]).astype(jnp.int32),
        'ada_w': nrm((DEPTH, D, 6 * D), 0.5 * D ** -0.5),
        'ada_b': nrm((DEPTH, 6 * D), 0.02),
        'norm_g': 1.0 + nrm((DEPTH, 2, D), 0.02),
        'final_g': 1.0 + nrm((D,), 0.02),
        'diff_w_in': nrm((n_a, D, 3 * D), D ** -0.5),
        'diff_w_out': nrm((n_a, D, D), D ** -0.5),
        'diff_lambda': nrm((n_a, 4, DA_HEAD_DIM), 0.1),
        'diff_subln_g': 1.0 + nrm((n_a, DA_V_DIM), 0.02),
        'nsa_w_in': nrm((n_b, D, NSA_IN_DIM), D ** -0.5),
        'nsa_w_out': nrm((n_b, D, D), D ** -0.5),
        'nsa_cmp_pos': nrm((n_b, 2, NSA_CMP_BLOCK, NSA_HEAD_DIM), 0.02),
        'nsa_cmp_w1': nrm((n_b, 2, NSA_CMP_BLOCK * NSA_HEAD_DIM, NSA_CMP_HIDDEN), (NSA_CMP_BLOCK * NSA_HEAD_DIM) ** -0.5),
        'nsa_cmp_b1': nrm((n_b, 2, NSA_CMP_HIDDEN), 0.02),
        'nsa_cmp_w2': nrm((n_b, 2, NSA_CMP_HIDDEN, NSA_HEAD_DIM), NSA_CMP_HIDDEN ** -0.5),
        'moe_w_group': nrm((DEPTH, D, MOE_GROUPS), D ** -0.5),
        'moe_b_group': nrm((DEPTH, MOE_GROUPS), 0.01),
        'moe_w_expert': nrm((DEPTH, MOE_GROUPS, D, MOE_EXPERTS_PER_GROUP), D ** -0.5),
        'moe_b_expert': nrm((DEPTH, MOE_GROUPS, MOE_EXPERTS_PER_GROUP), 0.01),
        'moe_w_gate': nrm((DEPTH, MOE_EXPERTS, D, MOE_HIDDEN), D ** -0.5),
        'moe_w_up': nrm((DEPTH, MOE_EXPERTS, D, MOE_HIDDEN), D ** -0.5),
        'moe_w_down': nrm((DEPTH, MOE_EXPERTS, MOE_HIDDEN, D), MOE_HIDDEN ** -0.5),
    }

def first_block(x, c, positions, ada_w, ada_b, norm_g, final_g,
              diff_w_in, diff_w_out, diff_lambda, diff_subln_g,
              nsa_w_in, nsa_w_out, nsa_cmp_pos, nsa_cmp_w1, nsa_cmp_b1, nsa_cmp_w2,
              moe_w_group, moe_b_group, moe_w_expert, moe_b_expert,
              moe_w_gate, moe_w_up, moe_w_down):
    cos, sin = _rope_tables(positions)
    c_act = jax.nn.silu(c)
    for i in range(DEPTH):
        mod = c_act @ ada_w[i] + ada_b[i]
        sh1, sc1, g1, sh2, sc2, g2 = jnp.split(mod[:, None, :], 6, axis=-1)
        h = _rmsnorm(x, norm_g[i, 0]) * (1.0 + sc1) + sh1
        j = i // N_MIXERS
        if i % N_MIXERS == 0:
            lambda_init = 0.8 - 0.6 * math.exp(-0.3 * i)
            mix = diff_attention(h, cos, sin, diff_w_in[j], diff_w_out[j], diff_lambda[j],
                                 diff_subln_g[j], lambda_init)
        else:
            mix = nsa_attention(h, cos, sin, nsa_w_in[j], nsa_w_out[j], nsa_cmp_pos[j],
                                nsa_cmp_w1[j], nsa_cmp_b1[j], nsa_cmp_w2[j])
        x = x + g1 * mix
        h = _rmsnorm(x, norm_g[i, 1]) * (1.0 + sc2) + sh2
        x = x + g2 * hier_moe(h, moe_w_group[i], moe_b_group[i], moe_w_expert[i], moe_b_expert[i],
                              moe_w_gate[i], moe_w_up[i], moe_w_down[i])
    return _rmsnorm(x, final_g)


N_MEM = 256
MLSTM_HEADS = 4
MLSTM_HEAD_DIM = D_MODEL // 16
MLSTM_WIDTH = MLSTM_HEADS * MLSTM_HEAD_DIM
MLSTM_CHUNK = 64
MLSTM_CONV = 4
CONF_CHANNELS = D_MODEL // 4
CONF_KERNEL = 31
FOX_HEADS = 8
FOX_HEAD_DIM = D_MODEL // 16
FOX_WIDTH = FOX_HEADS * FOX_HEAD_DIM
FOX_BLOCK = 128
MIX_WIDTH = MLSTM_WIDTH + CONF_CHANNELS + FOX_WIDTH
XATTN_HEADS = 4
XATTN_HEAD_DIM = D_MODEL // 8
XATTN_WIDTH = XATTN_HEADS * XATTN_HEAD_DIM
D_FF = ((8 * D_MODEL // 3) + 255) // 256 * 256
N_EXPERTS = 8
TOP_K = 2
EXPERT_FF = D_FF
N_DENSE_LAYERS = (DEPTH + 1) // 2
N_MOE_LAYERS = DEPTH // 2
EPS = 1e-6

IN_SPLITS = (2 * MLSTM_WIDTH, MLSTM_WIDTH, MLSTM_WIDTH, MLSTM_HEADS, MLSTM_HEADS,
             2 * CONF_CHANNELS, FOX_WIDTH, FOX_WIDTH, FOX_WIDTH, FOX_HEADS)
IN_WIDTH = sum(IN_SPLITS)
IN_SPLIT_IDX = tuple(int(i) for i in np.cumsum(IN_SPLITS)[:-1])


def rmsnorm(x, w):
    xf = x.astype(jnp.float32)
    y = xf * lax.rsqrt(jnp.mean(xf * xf, axis=-1, keepdims=True) + EPS)
    return (y * w.astype(jnp.float32)).astype(x.dtype)

def layernorm_f32(x, w, b):
    mu = jnp.mean(x, axis=-1, keepdims=True)
    xc = x - mu
    var = jnp.mean(xc * xc, axis=-1, keepdims=True)
    return xc * lax.rsqrt(var + EPS) * w.astype(jnp.float32) + b.astype(jnp.float32)

def causal_dwconv(x, w, b):
    K, C = w.shape
    y = lax.conv_general_dilated(
        x, w.astype(jnp.float32)[:, None, :], window_strides=(1,), padding=[(K - 1, 0)],
        dimension_numbers=("NWC", "WIO", "NWC"), feature_group_count=C)
    return y + b.astype(jnp.float32)

def mlstm_chunkwise(q, k, v, i_pre, f_pre):
    B, S, H, Dh = q.shape
    L = MLSTM_CHUNK
    nc = S // L
    log_f = jax.nn.log_sigmoid(f_pre)
    log_i = i_pre

    def chunks(t):
        return t.reshape(B, nc, L, H, Dh).transpose(1, 0, 3, 2, 4)

    def gchunks(t):
        return t.reshape(B, nc, L, H).transpose(1, 0, 3, 2)

    causal = jnp.tril(jnp.ones((L, L), dtype=bool))

    def step(carry, xs):
        C, n, m = carry
        qc, kc, vc, lic, lfc = xs
        b = jnp.cumsum(lfc, axis=-1)
        d_log = b[..., :, None] - b[..., None, :] + lic[..., None, :]
        d_log = jnp.where(causal, d_log, -jnp.inf)
        inter = b + m[..., None]
        m_t = jnp.maximum(jnp.max(d_log, axis=-1), inter)
        s = jnp.einsum("bhtd,bhsd->bhts", qc, kc) * jnp.exp(d_log - m_t[..., None])
        w_inter = jnp.exp(inter - m_t)
        num = (jnp.einsum("bhts,bhsd->bhtd", s, vc)
               + w_inter[..., None] * jnp.einsum("bhtk,bhkv->bhtv", qc, C))
        den = jnp.sum(s, axis=-1) + w_inter * jnp.einsum("bhtk,bhk->bht", qc, n)
        h = num / jnp.maximum(jnp.abs(den), jnp.exp(-m_t))[..., None]
        b_tot = b[..., -1]
        g = b_tot[..., None] - b + lic
        m_new = jnp.maximum(b_tot + m, jnp.max(g, axis=-1))
        wg = jnp.exp(g - m_new[..., None])
        decay = jnp.exp(b_tot + m - m_new)
        C_new = decay[..., None, None] * C + jnp.einsum("bhsk,bhsv->bhkv", kc * wg[..., None], vc)
        n_new = decay[..., None] * n + jnp.einsum("bhs,bhsk->bhk", wg, kc)
        return (C_new, n_new, m_new), h

    init = (jnp.zeros((B, H, Dh, Dh), jnp.float32), jnp.zeros((B, H, Dh), jnp.float32),
            jnp.zeros((B, H), jnp.float32))
    _, hs = lax.scan(step, init, (chunks(q), chunks(k), chunks(v), gchunks(log_i), gchunks(log_f)))
    return hs.transpose(1, 0, 3, 2, 4).reshape(B, S, H, Dh)

def forgetting_attention(q, k, v, log_f):
    B, S, H, Dh = q.shape
    nb = S // FOX_BLOCK
    c = jnp.cumsum(log_f, axis=1).transpose(0, 2, 1)
    kh = k.transpose(0, 2, 1, 3)
    vh = v.transpose(0, 2, 1, 3)
    qb = (q * (Dh ** -0.5)).reshape(B, nb, FOX_BLOCK, H, Dh).transpose(1, 0, 3, 2, 4)
    cb = c.reshape(B, H, nb, FOX_BLOCK).transpose(2, 0, 1, 3)
    qpos = jnp.arange(S).reshape(nb, FOX_BLOCK)
    kpos = jnp.arange(S)

    def one_block(args):
        qi, ci, pi = args
        logits = jnp.einsum("bhqd,bhkd->bhqk", qi, kh) + ci[..., None] - c[:, :, None, :]
        logits = jnp.where(pi[:, None] >= kpos[None, :], logits, -jnp.inf)
        p = jax.nn.softmax(logits, axis=-1)
        return jnp.einsum("bhqk,bhkd->bhqd", p, vh)

    o = lax.map(one_block, (qb, cb, qpos))
    return o.transpose(1, 0, 3, 2, 4).reshape(B, S, H * Dh)

def hybrid_mixer(h, w_in, mlstm_conv_w, mlstm_conv_b, mlstm_b_i, mlstm_b_f, mlstm_norm_w,
                 conf_conv_w, conf_conv_b, conf_ln_w, conf_ln_b, fox_b_f, w_out):
    B, S, _ = h.shape
    z = jnp.einsum("bsd,de->bse", h, w_in).astype(jnp.float32)
    m_qk, m_v, m_o, m_i, m_f, c_glu, f_q, f_k, f_v, f_f = jnp.split(z, IN_SPLIT_IDX, axis=-1)

    qk = jax.nn.silu(causal_dwconv(m_qk, mlstm_conv_w, mlstm_conv_b))
    mq, mk = jnp.split(qk, 2, axis=-1)
    hd = (B, S, MLSTM_HEADS, MLSTM_HEAD_DIM)
    hm = mlstm_chunkwise(mq.reshape(hd), mk.reshape(hd) * (MLSTM_HEAD_DIM ** -0.5), m_v.reshape(hd),
                         m_i + mlstm_b_i.astype(jnp.float32), m_f + mlstm_b_f.astype(jnp.float32))
    hm = hm * lax.rsqrt(jnp.mean(hm * hm, axis=-1, keepdims=True) + EPS)
    hm = hm.reshape(B, S, MLSTM_WIDTH) * mlstm_norm_w.astype(jnp.float32) * jax.nn.sigmoid(m_o)

    a, g = jnp.split(c_glu, 2, axis=-1)
    hc = causal_dwconv(a * jax.nn.sigmoid(g), conf_conv_w, conf_conv_b)
    hc = jax.nn.silu(layernorm_f32(hc, conf_ln_w, conf_ln_b))

    fd = (B, S, FOX_HEADS, FOX_HEAD_DIM)
    log_f = jax.nn.log_sigmoid(f_f + fox_b_f.astype(jnp.float32))
    hf = forgetting_attention(f_q.reshape(fd), f_k.reshape(fd), f_v.reshape(fd), log_f)

    cat = jnp.concatenate([hm, hc, hf], axis=-1).astype(h.dtype)
    return jnp.einsum("bse,ed->bsd", cat, w_out)

def memory_cross_attention(h, mem_n, w_q, w_kv, w_o):
    B, S, _ = h.shape
    q = jnp.einsum("bsd,de->bse", h, w_q).reshape(B, S, XATTN_HEADS, XATTN_HEAD_DIM)
    kv = jnp.einsum("bmd,de->bme", mem_n, w_kv)
    k, v = jnp.split(kv, 2, axis=-1)
    k = k.reshape(B, N_MEM, XATTN_HEADS, XATTN_HEAD_DIM)
    v = v.reshape(B, N_MEM, XATTN_HEADS, XATTN_HEAD_DIM)
    logits = jnp.einsum("bshd,bmhd->bhsm", q.astype(jnp.float32), k.astype(jnp.float32))
    p = jax.nn.softmax(logits * (XATTN_HEAD_DIM ** -0.5), axis=-1)
    o = jnp.einsum("bhsm,bmhd->bshd", p, v.astype(jnp.float32)).reshape(B, S, XATTN_WIDTH)
    return jnp.einsum("bse,ed->bsd", o.astype(h.dtype), w_o)

def swiglu(h, w_gate, w_up, w_down):
    a = jnp.einsum("bsd,df->bsf", h, w_gate)
    u = jnp.einsum("bsd,df->bsf", h, w_up)
    return jnp.einsum("bsf,fd->bsd", jax.nn.silu(a) * u, w_down)

def moe_swiglu(h, router_w, w_gate, w_up, w_down):
    logits = jnp.einsum("bsd,de->bse", h, router_w).astype(jnp.float32)
    top_v, top_i = lax.top_k(logits, TOP_K)
    top_w = jax.nn.softmax(top_v, axis=-1)
    gates = jnp.sum(jax.nn.one_hot(top_i, N_EXPERTS, dtype=jnp.float32) * top_w[..., None], axis=-2)
    y = jnp.zeros(h.shape, jnp.float32)
    for e in range(N_EXPERTS):
        y = y + gates[..., e:e + 1] * swiglu(h, w_gate[e], w_up[e], w_down[e]).astype(jnp.float32)
    return y.astype(h.dtype)

def second_inputs(seed: int = 0) -> dict:
    key = jax.random.key(seed)
    ks = jax.random.split(key, 32)

    def nrm(k, shape, scale):
        return jax.random.normal(k, shape, jnp.float32) * scale

    D, L = D_MODEL, DEPTH
    return {
        "x": nrm(ks[0], (BATCH, SEQ, D), 1.0),
        "mem": nrm(ks[1], (BATCH, N_MEM, D), 1.0),
        "norm_mix_w": 1.0 + nrm(ks[2], (L, D), 0.02),
        "w_in": nrm(ks[3], (L, D, IN_WIDTH), D ** -0.5),
        "mlstm_conv_w": nrm(ks[4], (L, MLSTM_CONV, 2 * MLSTM_WIDTH), MLSTM_CONV ** -0.5),
        "mlstm_conv_b": nrm(ks[5], (L, 2 * MLSTM_WIDTH), 0.02),
        "mlstm_b_i": nrm(ks[6], (L, MLSTM_HEADS), 0.1),
        "mlstm_b_f": 3.0 + nrm(ks[7], (L, MLSTM_HEADS), 0.5),
        "mlstm_norm_w": 1.0 + nrm(ks[8], (L, MLSTM_WIDTH), 0.02),
        "conf_conv_w": nrm(ks[9], (L, CONF_KERNEL, CONF_CHANNELS), CONF_KERNEL ** -0.5),
        "conf_conv_b": nrm(ks[10], (L, CONF_CHANNELS), 0.02),
        "conf_ln_w": 1.0 + nrm(ks[11], (L, CONF_CHANNELS), 0.02),
        "conf_ln_b": nrm(ks[12], (L, CONF_CHANNELS), 0.02),
        "fox_b_f": 2.0 + nrm(ks[13], (L, FOX_HEADS), 0.5),
        "w_out": nrm(ks[14], (L, MIX_WIDTH, D), MIX_WIDTH ** -0.5),
        "norm_xattn_w": 1.0 + nrm(ks[15], (L, D), 0.02),
        "norm_mem_w": 1.0 + nrm(ks[16], (L, D), 0.02),
        "xattn_w_q": nrm(ks[17], (L, D, XATTN_WIDTH), D ** -0.5),
        "xattn_w_kv": nrm(ks[18], (L, D, 2 * XATTN_WIDTH), D ** -0.5),
        "xattn_w_o": nrm(ks[19], (L, XATTN_WIDTH, D), XATTN_WIDTH ** -0.5),
        "norm_ffn_w": 1.0 + nrm(ks[20], (L, D), 0.02),
        "ffn_w_gate": nrm(ks[21], (N_DENSE_LAYERS, D, D_FF), D ** -0.5),
        "ffn_w_up": nrm(ks[22], (N_DENSE_LAYERS, D, D_FF), D ** -0.5),
        "ffn_w_down": nrm(ks[23], (N_DENSE_LAYERS, D_FF, D), D_FF ** -0.5),
        "router_w": nrm(ks[24], (N_MOE_LAYERS, D, N_EXPERTS), D ** -0.5),
        "moe_w_gate": nrm(ks[25], (N_MOE_LAYERS, N_EXPERTS, D, EXPERT_FF), D ** -0.5),
        "moe_w_up": nrm(ks[26], (N_MOE_LAYERS, N_EXPERTS, D, EXPERT_FF), D ** -0.5),
        "moe_w_down": nrm(ks[27], (N_MOE_LAYERS, N_EXPERTS, EXPERT_FF, D), EXPERT_FF ** -0.5),
        "norm_final_w": 1.0 + nrm(ks[28], (D,), 0.02),
    }

def second_block(x, mem, norm_mix_w, w_in, mlstm_conv_w, mlstm_conv_b, mlstm_b_i, mlstm_b_f,
              mlstm_norm_w, conf_conv_w, conf_conv_b, conf_ln_w, conf_ln_b, fox_b_f, w_out,
              norm_xattn_w, norm_mem_w, xattn_w_q, xattn_w_kv, xattn_w_o, norm_ffn_w,
              ffn_w_gate, ffn_w_up, ffn_w_down, router_w, moe_w_gate, moe_w_up, moe_w_down,
              norm_final_w):
    for l in range(DEPTH):
        h = rmsnorm(x, norm_mix_w[l])
        x = x + hybrid_mixer(h, w_in[l], mlstm_conv_w[l], mlstm_conv_b[l], mlstm_b_i[l], mlstm_b_f[l],
                             mlstm_norm_w[l], conf_conv_w[l], conf_conv_b[l], conf_ln_w[l],
                             conf_ln_b[l], fox_b_f[l], w_out[l])
        h = rmsnorm(x, norm_xattn_w[l])
        mem_n = rmsnorm(mem, norm_mem_w[l])
        x = x + memory_cross_attention(h, mem_n, xattn_w_q[l], xattn_w_kv[l], xattn_w_o[l])
        h = rmsnorm(x, norm_ffn_w[l])
        if l % 2 == 0:
            j = l // 2
            x = x + swiglu(h, ffn_w_gate[j], ffn_w_up[j], ffn_w_down[j])
        else:
            j = l // 2
            x = x + moe_swiglu(h, router_w[j], moe_w_gate[j], moe_w_up[j], moe_w_down[j])
    return rmsnorm(x, norm_final_w)


def setup_inputs(seed=0):
    out = dict(first_inputs(seed))
    for name, value in second_inputs(seed + 1).items():
        if name != "x":
            out[name + "_2"] = value
    return out


def reference(
    x, c, positions, ada_w, ada_b, norm_g, final_g, diff_w_in, diff_w_out, diff_lambda,
    diff_subln_g, nsa_w_in, nsa_w_out, nsa_cmp_pos, nsa_cmp_w1, nsa_cmp_b1, nsa_cmp_w2,
    moe_w_group, moe_b_group, moe_w_expert, moe_b_expert, moe_w_gate, moe_w_up, moe_w_down,
    mem_2, norm_mix_w_2, w_in_2, mlstm_conv_w_2, mlstm_conv_b_2, mlstm_b_i_2, mlstm_b_f_2,
    mlstm_norm_w_2, conf_conv_w_2, conf_conv_b_2, conf_ln_w_2, conf_ln_b_2, fox_b_f_2, w_out_2,
    norm_xattn_w_2, norm_mem_w_2, xattn_w_q_2, xattn_w_kv_2, xattn_w_o_2, norm_ffn_w_2,
    ffn_w_gate_2, ffn_w_up_2, ffn_w_down_2, router_w_2, moe_w_gate_2, moe_w_up_2, moe_w_down_2,
    norm_final_w_2,
):
    x = first_block(
        x, c, positions, ada_w, ada_b, norm_g, final_g, diff_w_in, diff_w_out, diff_lambda,
        diff_subln_g, nsa_w_in, nsa_w_out, nsa_cmp_pos, nsa_cmp_w1, nsa_cmp_b1, nsa_cmp_w2,
        moe_w_group, moe_b_group, moe_w_expert, moe_b_expert, moe_w_gate, moe_w_up, moe_w_down,
    )
    return second_block(
        x, mem_2, norm_mix_w_2, w_in_2, mlstm_conv_w_2, mlstm_conv_b_2, mlstm_b_i_2,
        mlstm_b_f_2, mlstm_norm_w_2, conf_conv_w_2, conf_conv_b_2, conf_ln_w_2, conf_ln_b_2,
        fox_b_f_2, w_out_2, norm_xattn_w_2, norm_mem_w_2, xattn_w_q_2, xattn_w_kv_2,
        xattn_w_o_2, norm_ffn_w_2, ffn_w_gate_2, ffn_w_up_2, ffn_w_down_2, router_w_2,
        moe_w_gate_2, moe_w_up_2, moe_w_down_2, norm_final_w_2,
    )


_drawn_inputs = setup_inputs


def setup_inputs(seed=0):
    import zlib

    import numpy as np

    out = dict(_drawn_inputs(seed))
    spreads = {}
    factors = {'nsa_cmp_pos': 4.171,
     'nsa_cmp_b1': 8.0,
     'moe_b_group': 4.867,
     'moe_b_expert': 2.715,
     'mlstm_conv_b_2': 3.1,
     'mlstm_b_i_2': 64.0,
     'conf_ln_w_2': 3.873,
     'conf_ln_b_2': 2.941,
     'norm_xattn_w_2': 4.175,
     'norm_mem_w_2': 3.564,
     'norm_final_w_2': 8.416,
     'norm_ffn_w_2': 3.726}
    for name, (base, spread) in spreads.items():
        noise = np.random.default_rng([zlib.crc32(name.encode()), seed]).standard_normal(out[name].shape)
        drawn = base * np.exp(spread * noise) if base else spread * noise
        out[name] = __import__('jax').numpy.asarray(drawn.astype(out[name].dtype))
    for name, factor in factors.items():
        out[name] = (out[name] * factor).astype(out[name].dtype)
    return out
```

```python
import math
from contextlib import ExitStack

import numpy as np

import concourse.bass as bass
from concourse import mybir

P = 128
D = 1024
T = 256
KC = D // P
NTILE = 256
HID = 256
NEG = -1e30
EPS = 1e-6
RING_A = 3
RING_F = 3
E1 = 32
E2 = 8
FF2 = 2816
M2 = FF2 // HID
NFREE = 2048

F32 = mybir.dt.float32
I32 = mybir.dt.int32
ALU = mybir.AluOpType
ACT = mybir.ActivationFunctionType
AX = mybir.AxisListType

ROW_TILES = [
    [("ada_b", 96), ("c", 8), ("cmp_b1", 4), ("subln", 1)],
    [("norm_g", 32), ("final_g", 8), ("norm_mix", 16), ("norm_x", 16), ("norm_mem", 16),
     ("norm_ffn", 16), ("norm_final", 8)],
    [("conf_w", 124)],
    [("ml_w", 32), ("ml_b", 8), ("conf_b", 4), ("ln_w", 4), ("ln_b", 4), ("ml_norm", 4),
     ("cmp_pos", 32)],
]
COL = {}
for _t, _rows in enumerate(ROW_TILES):
    _at = 0
    for _name, _n in _rows:
        COL[_name] = _t * P + _at
        _at += _n

CONSTS = [("ident", P), ("mean_d", P), ("mean_128", P), ("mean_64", P), ("mean_256", P),
          ("rope", P), ("causal", 3 * P), ("zero", 2 * P), ("cmp_mask", 32), ("cmp_valid", 2),
          ("iota", 32), ("invfreq", 1), ("eps", 1), ("halfpi", 1), ("one", 1), ("sel", 8 * P)]
CAT = {}
_at = 0
for _name, _n in CONSTS:
    CAT[_name] = _at
    _at += _n
NCONST = _at

SMALL = [("gates", 48), ("route0", 36), ("route1", 36), ("route2", 8), ("pre0", 16), ("pre1", 16)]
SAT = {}
_at = 0
for _name, _n in SMALL:
    SAT[_name] = (_at, _n)
    _at += KC * _n
NSMALL = _at

GROUPS = [("ada", 48, None), ("diff_q", 4, "act"), ("diff_k", 4, "act"), ("diff_v", 4, "act"),
          ("diff_o", 4, "dve"), ("nsa_q", 4, "act"), ("nsa_kv", 3, "act"), ("cmp", 4, None),
          ("nsa_o", 4, "dve")]
for _l in range(2):
    GROUPS += [(f"mix_in{_l}", 12, "act"), (f"mix_o{_l}", 4, "dve"), (f"x_q{_l}", 2, "act"),
               (f"x_k{_l}", 2, "act"), (f"x_v{_l}", 2, "act"), (f"x_o{_l}", 4, "dve")]
TILE0, LIN0, OWNER = {}, {}, []
_n = 0
for _name, _k, _who in GROUPS:
    TILE0[_name] = _n
    LIN0[_name] = len(OWNER)
    _n += _k
    if _who:
        OWNER += [_who] * _k
NT = _n
NTILES = {g[0]: g[1] for g in GROUPS}
WA_AT, XO_AT = {}, {}
for _name, _k, _who in GROUPS:
    for _i in range(_k):
        if _name.startswith("x_o"):
            XO_AT[TILE0[_name] + _i] = len(XO_AT)
        else:
            WA_AT[TILE0[_name] + _i] = len(WA_AT)


def emptied(who, lin):
    return sum(1 for w in OWNER[:lin + 1] if w == who)


def build(nc, t):
    ctx = ExitStack()
    with ctx:
        def sb(name, shape, dt=F32):
            return ctx.enter_context(nc.sbuf_tensor(name, shape, dt))

        sems = {}

        def S(name):
            if name not in sems:
                sems[name] = ctx.enter_context(nc.semaphore(name))
            return sems[name]

        CON = sb("CON", [P, NCONST])
        SMW = sb("SMW", [P, NSMALL])
        COLS = sb("COLS", [P, 4 * P])
        WA = [sb(f"WA{i}", [P, NFREE]) for i in range(RING_A)]
        WF = [sb(f"WF{i}", [P, 3, NFREE]) for i in range(RING_F)]
        X = sb("X", [P, KC, T])
        H = sb("H", [P, KC, T])
        MEM = sb("MEM", [P, KC, T])
        BIG = sb("BIG", [P, 4 * KC, T])
        Q = BIG[:, 0:KC, :]
        K = BIG[:, KC:2 * KC, :]
        V = BIG[:, 2 * KC:3 * KC, :].rearrange("p (s c) t -> p s (c t)", s=2)
        O = BIG[:, 3 * KC:4 * KC, :]
        OTOK = O.rearrange("p (s c) t -> p s (c t)", s=2)
        YTOK = Q.rearrange("p (s c) t -> p s (c t)", s=2)
        CB = BIG
        SQ = sb("SQ", [P, KC, T])
        SM = sb("SM", [P, 2, 2, T])
        PR = sb("PR", [P, 2, 2, T])
        PN = sb("PN", [P, 2, 2, T])
        PT = sb("PT", [P, 2, 2, T])
        A1 = PR
        A2 = PN
        A3 = PT
        COS = sb("COS", [P, T])
        SIN = sb("SIN", [P, T])
        RS = sb("RS", [P, 2, T])
        MODS = sb("MODS", [P, 96])
        AG = sb("AG", [P, 4, KC])
        CACT = sb("CACT", [P, KC])
        LAM = sb("LAM", [P, 16])
        LAMR = sb("LAMR", [P, 4 * 64])
        GATE = sb("GATE", [P, 2, 48])
        KVT = sb("KVT", [P, 2, 2, P])
        ST = sb("ST", [P, 32])
        MX, NM, SUM, FAC = (ST[:, 4 * i:4 * i + 4].rearrange("p (j q) -> p j q", j=2) for i in range(4))
        RB = sb("RB", [P, 3, 36])
        LG = sb("LG", [P, 2, 36])
        R1, R2, R3, R4, R5 = (sb(f"R{i}", [P, 2, 32]) for i in range(1, 6))
        RV = sb("RV", [P, 12, 2])
        CTOK = sb("CTOK", [P, 2, 32])
        COMBT = sb("COMBT", [32, T])
        PB = sb("PB", [8, 6])
        PRE = sb("PRE", [8, 10, T])
        MCOL = sb("MCOL", [P, 2, 2, 4])
        H1 = sb("H1", [P, 2, 2, 31])
        H1G = sb("H1G", [P, 2, 2, 30])
        CMPZ = SM
        KCMP = sb("KCMP", [P, 16])
        VCMP = sb("VCMP", [16, 2, 64])
        W2D = sb("W2D", [P, 2, 2, P])
        LNM = sb("LNM", [P, 2, T])
        PSB = [ctx.enter_context(nc.psum_tensor(f"B{i}", [P, 512], F32)) for i in range(8)]

        OBANK = [PSB[7], PSB[3]]

        def con(name, n=None, rows=P):
            a = CAT[name]
            return CON[0:rows, a:a + (n or dict(CONSTS)[name])]

        def col(name, i=0):
            return COLS[:, COL[name] + i:COL[name] + i + 1]

        ident = con("ident")
        COMBD = nc.dram_tensor("comb_rows", (3, 32, T), F32, kind="Internal").ap()

        def two(ap):
            return ap.rearrange("p (s t) -> p s t", s=2)

        def over2(ap):
            return ap.unsqueeze(1).to_broadcast([P, 2, T])

        causal = [con("causal")[:, 0:P], con("causal")[:, P:3 * P]]
        nomask = [con("zero"), con("zero")]

        def job(**kw):
            j = dict(kind="std", scale=0.125, mask=causal, keys=[128, 256], tr=True, part=0, dv=64,
                     rows=[128, 128], first=True, last=True, gate=None)
            j.update(kw)
            return j

        def diff_jobs():
            out = []
            for h in range(8):
                for c in range(2):
                    a = slice(64 * c, 64 * c + 64)
                    out.append(job(kind=f"diff{c}", q=Q[a, h, :], k=K[a, h, :], tr=c == 1, dv=128,
                                   v=[V[:, kt, 128 * h:128 * h + 128] for kt in range(2)], out=h,
                                   close=True))
            return out

        def nsa_jobs():
            out = []
            for c in range(8):
                for g in range(2):
                    h = 8 * g + c
                    a = slice(64 * g, 64 * g + 64)
                    for b in range(3):
                        kw = dict(kind="nsa", q=Q[a, c, :], part=64 * g, out=c, first=b == 0,
                                  last=b == 2, gate=3 * h + b, close=g == 1 and b == 2)
                        if b == 0:
                            kw.update(kind="cmp", k=KCMP[a, 0:15], keys=[15, 15], rows=[15],
                                      mask=[con("cmp_mask")[:, 0:15], con("cmp_mask")[:, 16:31]],
                                      v=[VCMP[0:15, g, :]])
                        else:
                            kw.update(k=K[a, 2 + 2 * (b - 1), :],
                                      v=[KVT[:, b - 1, kt, 64 * g:64 * g + 64] for kt in range(2)])
                        out.append(job(**kw))
            return out

        def ml_jobs():
            out = []
            for h in range(4):
                a = slice(64 * (h % 2), 64 * (h % 2) + 64)
                out.append(job(kind="ml", h=h, q=Q[a, h // 2, :], k=K[a, h // 2, :], part=64 * (h % 2),
                               v=[V[:, kt, 64 * h:64 * h + 64] for kt in range(2)], out=h // 2,
                               close=h % 2 == 1))
            return out

        def fox_jobs():
            out = []
            for h in range(8):
                a = slice(64 * (h % 2), 64 * (h % 2) + 64)
                out.append(job(kind="fox", h=h, q=Q[a, 4 + h // 2, :], k=K[a, 4 + h // 2, :],
                               part=64 * (h % 2), out=4 + h // 2, close=h % 2 == 1,
                               v=[V[:, kt, 512 + 64 * h:576 + 64 * h] for kt in range(2)]))
            return out

        def x_jobs():
            return [job(q=Q[:, h, :], k=K[:, h, :], mask=nomask, keys=[256, 256], dv=128,
                        scale=128 ** -0.5, v=[V[:, kt, 128 * h:128 * h + 128] for kt in range(2)],
                        out=h, close=True) for h in range(4)]

        def n_tr(jobs, j):
            return sum(1 for x in jobs[:j + 1] if x["tr"])

        def n_closed(jobs, j):
            return sum(1 for x in jobs[:j + 1] if x["tr"] and x["close"])

        STAGES = [("a0", diff_jobs()), ("a1", nsa_jobs()), ("mix0", ml_jobs() + fox_jobs()), ("xt0", x_jobs()),
                  ("mix1", ml_jobs() + fox_jobs()), ("xt1", x_jobs())]
        JOBS = dict(STAGES)
        BEFORE, so_far = {}, (0, 0, 0)
        for name, jobs in STAGES:
            BEFORE[name] = so_far
            so_far = (so_far[0] + len(jobs), so_far[1] + n_tr(jobs, len(jobs)), so_far[2] + n_closed(jobs, len(jobs)))

        def outputs_of(tag, n):
            return BEFORE[tag][2] + n

        def full(j, kt, qt):
            return j["keys"][qt] > 128 * kt

        def rope_pairs(layer):
            if layer == 0:
                return ([(Q[:, 2 * i:2 * i + 2, :], emptied("act", LIN0["diff_q"] + i)) for i in range(4)]
                        + [(K[:, 2 * i:2 * i + 2, :], emptied("act", LIN0["diff_k"] + i)) for i in range(4)])
            return ([(Q[:, 2 * i:2 * i + 2, :], emptied("act", LIN0["nsa_q"] + i)) for i in range(4)]
                    + [(K[:, 2 * i:2 * i + 2, :], emptied("act", LIN0["nsa_kv"] + i)) for i in (1, 2)])

        def mods(layer, part, c=None):
            a = layer * 48 + part * KC
            return MODS[:, a:a + KC] if c is None else MODS[:, a + c:a + c + 1]

        def cols8(name, l=0):
            return COLS[:, COL[name] + l * KC:COL[name] + l * KC + KC]

        NORMS = {"n0": (X, H, AG[:, 0, :], mods(0, 0)), "m0": (X, H, AG[:, 1, :], mods(0, 3)),
                 "n1": (X, H, AG[:, 2, :], mods(1, 0)), "m1": (X, H, AG[:, 3, :], mods(1, 3)),
                 "f1": (X, X, cols8("final_g"), None), "y": (X, H, cols8("norm_final"), None),
                 "d0": (X, H, cols8("norm_ffn", 0), None), "m2": (X, H, cols8("norm_ffn", 1), None)}
        for l in range(2):
            NORMS[f"x{l}"] = (X, H, cols8("norm_mix", l), None)
            NORMS[f"xa{l}"] = (X, H, cols8("norm_x", l), None)
            NORMS[f"mem{l}"] = (MEM, O, cols8("norm_mem", l), None)
        ORDER = ["n0", "m0", "n1", "m1", "f1", "x0", "mem0", "xa0", "d0", "x1", "mem1", "xa1", "m2", "y"]

        def nth(tag):
            return ORDER.index(tag) + 1

        def shifted(tag):
            return KC * sum(1 for n in ORDER[:nth(tag) - 1] if NORMS[n][3] is not None)

        SQF = SQ[:, :, :].rearrange("p c t -> p (c t)")
        RAW = SQF[:, 0:4 * 260].rearrange("p (c t) -> p c t", c=4)
        CPAD = SQF[:, 1040:1040 + 2 * 286].rearrange("p (c t) -> p c t", c=2)

        block = ctx.enter_context(nc.Block())

        @block.sync
        def _(sp):
            sp.dma_start(CON[:, :], t["consts"]).then_inc(S("con_in"), 16)
            for i in range(4):
                n = sum(k for _, k in ROW_TILES[i])
                sp.dma_start(SQ[0:n, i, 0:P], t[f"rows{i}"]).then_inc(S("rows_in"), 16)
            sp.dma_start(BIG[:, 16:24, :].rearrange("p (s c) t -> p s (c t)", s=2),
                         t["x"].rearrange("(s p) d -> p s d", p=P)).then_inc(S("x_in"), 16)
            sp.dma_start(BIG[:, 24:32, :].rearrange("p (s c) t -> p s (c t)", s=2),
                         t["mem"].rearrange("(s p) d -> p s d", p=P)).then_inc(S("x_in"), 16)

            def load_a(n):
                if n >= RING_A:
                    sp.wait_ge(S("a_used"), n - RING_A + 1)
                if n in XO_AT:
                    sp.dma_start(WA[n % RING_A][:, 0:1024], t["xo"][XO_AT[n]]).then_inc(
                        S(f"a_in{n % RING_A}"), 16)
                else:
                    sp.dma_start(WA[n % RING_A][:, :], t["wa"][WA_AT[n]]).then_inc(
                        S(f"a_in{n % RING_A}"), 16)

            for n in range(RING_A):
                load_a(n)
            sp.dma_start(SMW[:, :], t["small"]).then_inc(S("small_in"), 16)
            sp.dma_start(LAMR[:, :], t["lam"].to_broadcast([P, 256])).then_inc(S("small_in"), 16)
            sp.dma_start(SM[:, 0, 0, :].bitcast(I32), t["pos"].to_broadcast([P, T])).then_inc(S("small_in"), 16)
            sp.dma_start(RB[:, :, :].rearrange("p a b -> p (a b)"), t["route_b"].to_broadcast([P, 108])).then_inc(S("small_in"), 16)
            sp.dma_start(PB[:, :], t["pre_b"]).then_inc(S("small_in"), 16)
            sp.dma_start(W2D[:, :, :, :].rearrange("p a b c -> p (a b c)"), t["cmp_w2"]).then_inc(S("small_in"), 16)
            with sp.Fori(1, 48 // RING_A) as i:
                for j in range(RING_A):
                    sp.wait_ge(S("a_used"), (i - 1) * RING_A + j + 1)
                    sp.dma_start(WA[j][:, :], t["wa"][bass.ds(i * RING_A + j, 1)].rearrange(
                        "a p n -> p (a n)")).then_inc(S(f"a_in{j}"), 16)

            def load_group(name):
                for i in range(NTILES[name]):
                    load_a(TILE0[name] + i)

            def load_ffn(tag, src, n, before):
                if before:
                    sp.wait_ge(S(f"f_used_{before[0]}"), before[1])
                for c in range(min(RING_F, n)):
                    sp.dma_start(WF[c][:, :, :].rearrange("p a n -> p (a n)"), src[c]).then_inc(
                        S(f"f_in_{tag}{c}"), 16)
                rounds = n // RING_F
                with sp.Fori(1, rounds) as i:
                    for j in range(RING_F):
                        sp.wait_ge(S(f"f_used_{tag}"), (i - 1) * RING_F + j + 1)
                        sp.dma_start(WF[j][:, :, :].rearrange("p a n -> p (a n)"),
                                     src[bass.ds(i * RING_F + j, 1)].rearrange("a p n -> p (a n)")
                                     ).then_inc(S(f"f_in_{tag}{j}"), 16)
                for c in range(rounds * RING_F, n):
                    sp.wait_ge(S(f"f_used_{tag}"), c - RING_F + 1)
                    sp.dma_start(WF[c % RING_F][:, :, :].rearrange("p a n -> p (a n)"),
                                 src[c]).then_inc(S(f"f_in_{tag}{c % RING_F}"), 16)

            for name in ("diff_q", "diff_k", "diff_v", "diff_o"):
                load_group(name)
            load_ffn("m0", t["wf0"], E1, None)
            for name in ("nsa_q", "nsa_kv", "cmp", "nsa_o"):
                load_group(name)
            load_ffn("m1", t["wf1"], E1, ("m0", E1))
            for name in ("mix_in0", "mix_o0", "x_q0", "x_k0", "x_v0", "x_o0"):
                load_group(name)
            load_ffn("d0", t["wf2"], M2, ("m1", E1))
            for name in ("mix_in1", "mix_o1", "x_q1", "x_k1", "x_v1", "x_o1"):
                load_group(name)
            load_ffn("m2", t["wf3"], E2 * M2, ("d0", M2))
            sp.wait_ge(S("y_out"), 4)
            sp.dma_start(t["out"].rearrange("(s p) d -> p s d", p=P),
                         BIG[:, 0:8, :].rearrange("p (s c) t -> p s (c t)", s=2)).then_inc(S("out_done"), 16)
            sp.wait_ge(S("out_done"), 16)

        @block.tensor
        def _(pe):
            def mm(out, lhsT, rhs, start, stop, **kw):
                return nc.tensor.matmul(out, lhsT, rhs, start=start, stop=stop, **kw)

            pe.wait_ge(S("con_in"), 16)
            pe.wait_ge(S("rows_in"), 64)
            for i in range(4):
                n = sum(k for _, k in ROW_TILES[i])
                last = nc.tensor.transpose(PSB[3][:, i * P:i * P + n], SQ[0:n, i, 0:P], ident[0:n, 0:n])
            last.then_inc(S("cols_mm"), 1)
            pe.wait_ge(S("x_in"), 32)
            for r in range(8):
                if r >= 4:
                    pe.wait_ge(S("x_cp"), r - 3)
                src = V if r < 4 else OTOK
                for c in range(2):
                    for s in range(2):
                        cc = 2 * (r % 4) + c
                        last = nc.tensor.transpose(PSB[4 + r % 4][:, c * T + s * P:c * T + s * P + P],
                                                   src[:, s, cc * P:cc * P + P], ident)
                last.then_inc(S("x_tr"), 1)
            pe.wait_ge(S("cact"), 1)
            with pe.Fori(0, 48 // RING_A) as i:
                for j in range(RING_A):
                    pe.wait_ge(S(f"a_in{j}"), i * 16 + 16)
                    w = WA[j][:, :].rearrange("p (k n) -> p k n", k=KC)
                    for s in range(2):
                        for k in range(KC):
                            last = mm(PSB[2][:, bass.ds(i * (2 * RING_A) + 2 * j + s, 1)],
                                      w[:, k, s * P:s * P + P], CACT[:, k:k + 1], k == 0, k == KC - 1)
                    last.then_inc(S("a_used"), 1)

            def tile(name, i, src, tokens=False, nk=KC):
                n, q = TILE0[name] + i, LIN0[name] + i
                pe.wait_ge(S(f"a_in{n % RING_A}"), 16 * (n // RING_A + 1))
                if q >= 2:
                    pe.wait_ge(S(f"lin_{OWNER[q - 2]}"), emptied(OWNER[q - 2], q - 2))
                w = WA[n % RING_A][:, 0:nk * NTILE].rearrange("p (k n) -> p k n", k=nk)
                for s in range(2):
                    for k in range(nk):
                        o = PSB[q % 2][:, s * T:s * T + T]
                        if tokens:
                            last = mm(o, src[:, k, s * P:s * P + P], w[:, k, :], k == 0, k == nk - 1)
                        else:
                            last = mm(o, w[:, k, s * P:s * P + P], src[:, k, :], k == 0, k == nk - 1)
                last.then_inc(S("a_used"), 1)

            def linear(name, src, tokens=False, nk=KC):
                for i in range(NTILES[name]):
                    tile(name, i, src, tokens, nk)

            def norm(tag):
                pe.wait_ge(S("squares"), nth(tag))
                for k in range(KC):
                    last = mm(PSB[3][:, 0:T], con("mean_d"), SQ[:, k, :], k == 0, k == KC - 1)
                last.then_inc(S("mean_sq"), 1)

            def rope(tag, pairs):
                for r, (x, ready) in enumerate(pairs):
                    pe.wait_ge(S("lin_act"), ready)
                    if r >= 2:
                        pe.wait_ge(S(f"rope_use_{tag}"), r - 1)
                    mm(PSB[4 + r % 2][:, :], con("rope"), x.rearrange("p c t -> p (c t)"), True, True).then_inc(
                        S(f"rope_mm_{tag}"), 1)

            def attend(tag):
                jobs = JOBS[tag]
                j0, t0, o0 = BEFORE[tag]
                n = len(jobs)

                def scores(j):
                    x = jobs[j]
                    if j >= 2:
                        pe.wait_ge(S("weights" if jobs[j - 2]["kind"] == "ml" else "masked"), j0 + j - 1)
                    bank = PSB[4 + j % 2]
                    for qt in range(2):
                        kk = x["keys"][qt]
                        last = mm(bank[:, qt * T:qt * T + kk], x["q"][:, qt * P:qt * P + P],
                                  x["k"][:, 0:kk], True, x["kind"] != "fox")
                        if x["kind"] == "fox":
                            last = mm(bank[:, qt * T:qt * T + kk], con("sel", rows=8)[:, x["h"] * P:x["h"] * P + P],
                                      PRE[0:8, 9, 0:kk], False, True)
                    if x["kind"] == "ml":
                        if j >= 1:
                            pe.wait_ge(S("masked"), j0 + j)
                        last = mm(PSB[0][:, 0:T], con("sel", rows=4)[:, x["h"] * P:x["h"] * P + P],
                                  PRE[0:4, 4, :], True, True)
                    last.then_inc(S("scores"), 1)

                def values(j):
                    x = jobs[j]
                    if not x["tr"]:
                        return
                    t_n = n_tr(jobs, j)
                    pe.wait_ge(S("weights"), j0 + j + 1)
                    if t_n > 2:
                        pe.wait_ge(S("turned_out"), t0 + t_n - 2)
                    bank = [PSB[6], PSB[2]][t_n % 2]
                    for kt, kr in enumerate(x["rows"]):
                        for qt in range(2):
                            if full(x, kt, qt):
                                last = nc.tensor.transpose(bank[0:kr, kt * T + qt * P:kt * T + qt * P + P],
                                                           PN[:, j % 2, qt, kt * P:kt * P + kr], ident)
                    last.then_inc(S("turned"), 1)
                    pe.wait_ge(S("turned_out"), t0 + t_n)
                    g = n_closed(jobs, j - 1) if j else 0
                    if x["first"] and g >= 2:
                        pe.wait_ge(S("outputs"), o0 + g - 1)
                    for kt, kr in enumerate(x["rows"]):
                        q0 = 0 if full(x, kt, 0) else P
                        last = mm(OBANK[g % 2][x["part"]:x["part"] + x["dv"], q0:T],
                                  x["v"][kt], PT[0:kr, t_n % 2, kt, q0:T], x["first"] and kt == 0,
                                  x["last"] and kt == len(x["rows"]) - 1)
                    last.then_inc(S("mixed"), 1)

                scores(0)
                for j in range(n):
                    if j + 1 < n:
                        scores(j + 1)
                    values(j)

            def group_mean(tag, matrix, n):
                for r in range(n):
                    pe.wait_ge(S(f"gsq_{tag}"), r + 1)
                    if r >= 1:
                        pe.wait_ge(S(f"gr_{tag}"), r)
                    mm(PSB[3][:, :], con(matrix), SQ[:, 2 * r:2 * r + 2, :].rearrange("p c t -> p (c t)"),
                       True, True).then_inc(S(f"gms_{tag}"), 1)

            def route(tag, small):
                pe.wait_ge(S("normed"), nth(tag))
                a, w = SAT[small]
                for s in range(2):
                    for k in range(KC):
                        last = mm(PSB[2][:, s * 64:s * 64 + w], H[:, k, s * P:s * P + P],
                                  SMW[:, a + k * w:a + k * w + w], k == 0, k == KC - 1)
                last.then_inc(S(f"rl_{tag}"), 1)

            def route_rows(tag, ne):
                pe.wait_ge(S(f"comb_{tag}"), 1)
                for s in range(2):
                    last = nc.tensor.transpose(PSB[3][0:ne, s * P:s * P + P], CTOK[:, s, 0:ne], ident)
                last.then_inc(S(f"combt_{tag}"), 1)

            def ffn(tag, n, routed):
                def products(slot, par):
                    w = WF[slot]
                    for half in range(2):
                        ww = w[:, half, :].rearrange("p (k n) -> p k n", k=KC)
                        bank = PSB[2 * par + half]
                        for s in range(2):
                            for k in range(KC):
                                last = mm(bank[:, s * T:s * T + T], ww[:, k, s * P:s * P + P],
                                          H[:, k, :], k == 0, k == KC - 1)
                    last.then_inc(S(f"gu_{tag}"), 1)

                def down(slot, par):
                    w = WF[slot][:, 2, :].rearrange("p (s n) -> p s n", s=2)
                    for dch in range(KC):
                        for s in range(2):
                            last = mm(PSB[4 + dch // 2][:, (dch % 2) * T:(dch % 2) * T + T],
                                      w[:, s, dch * P:dch * P + P], (A3 if routed else A2)[:, par, s, :],
                                      False, False, skip_group_check=True)
                    last.then_inc(S(f"f_used_{tag}"), 1)

                zero = con("zero")
                for b in range(4):
                    for s in range(2):
                        last = mm(PSB[4 + b][:, s * T:s * T + T], zero[:, 0:P], zero, s == 0, False,
                                  skip_group_check=True)

                def step(c, j, last):
                    if not last:
                        pe.wait_ge(S(f"f_in_{tag}{(j + 1) % RING_F}"),
                                   (c[0] + (j + 1) // RING_F) * 16 + 16)
                        if j >= 1:
                            pe.wait_ge(S(f"up_{tag}"), c[1])
                        products((j + 1) % RING_F, (j + 1) % 2)
                    pe.wait_ge(S(f"a3_{tag}" if routed else f"up_{tag}"), c[1] + 1)
                    down(j % RING_F, j % 2)

                pe.wait_ge(S("normed"), nth(tag))
                pe.wait_ge(S(f"f_in_{tag}0"), 16)
                products(0, 0)
                if routed:
                    pe.wait_ge(S(f"combr_{tag}"), 1)
                step((0, 0), 0, False)
                body = 2 * RING_F
                loops = (n - 2) // body
                with pe.Fori(0, loops) as i:
                    for j in range(1, body + 1):
                        step((i * (body // RING_F), i * body + j), j, False)
                for c in range(1 + loops * body, n):
                    base = loops * body
                    step((base // RING_F, c), c - base, c == n - 1)

            def cmp_mlps():
                pe.wait_ge(S("cmpz"), 2)
                for kv in range(2):
                    for half in range(2):
                        n = TILE0["cmp"] + 2 * kv + half
                        pe.wait_ge(S(f"a_in{n % RING_A}"), 16 * (n // RING_A + 1))
                    for s in range(2):
                        for m in range(16):
                            n = TILE0["cmp"] + 2 * kv + m // 8
                            w = WA[n % RING_A][:, :].rearrange("p (k n) -> p k n", k=KC)
                            last = mm(PSB[6][:, (2 * kv + s) * 32:(2 * kv + s) * 32 + 31],
                                      w[:, m % 8, s * P:s * P + P],
                                      CMPZ[:, kv].rearrange("p a t -> p (a t)")[:, 0:496].rearrange(
                                          "p (m n) -> p m n", m=16)[:, m, :], m == 0, m == 15)
                            if s == 1 and m in (7, 15):
                                last.then_inc(S("a_used"), 1)
                pe.wait_ge(S("h1g"), 1)
                for s in range(2):
                    last = mm(PSB[3][:, 0:30], W2D[:, 0, s, :], H1G[:, 0, s, :], s == 0, s == 1)
                for g in range(2):
                    for s in range(2):
                        last = mm(PSB[3][0:15, 64 + 64 * g:128 + 64 * g], H1G[:, 1, s, 15 * g:15 * g + 15],
                                  W2D[:, 1, s, 0:64], s == 0, s == 1)
                last.then_inc(S("cmp_out"), 1)

            norm("n0")
            pe.wait_ge(S("normed"), nth("n0"))
            linear("diff_q", H)
            linear("diff_k", H)
            linear("diff_v", H, tokens=True)
            rope("r0", rope_pairs(0))
            pe.wait_ge(S("rope_use_r0"), 8)
            pe.wait_ge(S("lin_act"), emptied("act", LIN0["diff_v"] + 3))
            attend("a0")
            group_mean("g0", "mean_128", 4)
            pe.wait_ge(S("gd_g0"), 4)
            linear("diff_o", O)
            norm("m0")
            route("m0", "route0")
            route_rows("m0", E1)
            ffn("m0", E1, True)
            norm("n1")
            pe.wait_ge(S("normed"), nth("n1"))
            linear("nsa_q", H)
            linear("nsa_kv", H)
            a, w = SAT["gates"]
            for s in range(2):
                for k in range(KC):
                    last = mm(PSB[2][:, s * 64:s * 64 + w], H[:, k, s * P:s * P + P],
                              SMW[:, a + k * w:a + k * w + w], k == 0, k == KC - 1)
            last.then_inc(S("gates_mm"), 1)
            rope("r1", rope_pairs(1))
            pe.wait_ge(S("rope_use_r1"), 6)
            for b in range(2):
                for kt in range(2):
                    last = nc.tensor.transpose(PSB[7][:, (2 * b + kt) * P:(2 * b + kt) * P + P],
                                               K[:, 3 + 2 * b, kt * P:kt * P + P], ident)
            last.then_inc(S("kvt_mm"), 1)
            cmp_mlps()
            pe.wait_ge(S("cmp_kv"), 2)
            pe.wait_ge(S("kvt"), 1)
            attend("a1")
            pe.wait_ge(S("outputs"), outputs_of("a1", 8))
            linear("nsa_o", O)
            norm("m1")
            route("m1", "route1")
            route_rows("m1", E1)
            ffn("m1", E1, True)
            norm("f1")
            for l in range(2):
                norm(f"x{l}")
                pe.wait_ge(S("normed"), nth(f"x{l}"))
                for i in range(12):
                    tile(f"mix_in{l}", i, H, tokens=i in (2, 10, 11))
                a, w = SAT[f"pre{l}"]
                for r, (c0, c1) in enumerate(((0, 4), (4, 8), (8, 16))):
                    o = [PSB[2][0:4, 0:T], PSB[2][0:4, T:2 * T], PSB[3][0:8, 0:T]][r]
                    for k in range(KC):
                        last = mm(o, SMW[:, a + k * w + c0:a + k * w + c1], H[:, k, :], k == 0, k == KC - 1)
                last.then_inc(S(f"pre_mm{l}"), 1)
                pe.wait_ge(S(f"pre_rows{l}"), 1)
                for r in range(2):
                    for s in range(2):
                        last = nc.tensor.transpose(PSB[6][:, (2 * r + s) * 4:(2 * r + s) * 4 + 4],
                                                   PRE[0:4, 5 + r, s * P:s * P + P], ident[0:4, 0:4])
                last.then_inc(S(f"mcol_mm{l}"), 1)
                pe.wait_ge(S(f"mcol{l}"), 2)
                pe.wait_ge(S(f"qk_ml{l}"), 4)
                pe.wait_ge(S("lin_act"), emptied("act", LIN0[f"mix_in{l}"] + 11))
                attend(f"mix{l}")
                pe.wait_ge(S("outputs"), outputs_of(f"mix{l}", 6))
                group_mean(f"gm{l}", "mean_64", 1)
                pe.wait_ge(S(f"conv{l}"), 1)
                for c in range(2):
                    last = mm(PSB[6][:, 0:T], con("mean_256"), LNM[:, c, :], c == 0, c == 1)
                last.then_inc(S(f"ln_mm{l}"), 1)
                pe.wait_ge(S(f"ln_sq{l}"), 1)
                for c in range(2):
                    last = mm(PSB[2][:, 0:T], con("mean_256"), SQ[:, 6 + c, :], c == 0, c == 1)
                last.then_inc(S(f"ln_mm{l}"), 1)
                pe.wait_ge(S(f"cat{l}"), 2)
                linear(f"mix_o{l}", O)
                norm(f"mem{l}")
                norm(f"xa{l}")
                pe.wait_ge(S("normed"), nth(f"xa{l}"))
                linear(f"x_q{l}", H)
                pe.wait_ge(S("normed"), nth(f"mem{l}"))
                linear(f"x_k{l}", O)
                linear(f"x_v{l}", O, tokens=True)
                pe.wait_ge(S("lin_act"), emptied("act", LIN0[f"x_v{l}"] + 1))
                attend(f"xt{l}")
                pe.wait_ge(S("outputs"), outputs_of(f"xt{l}", 4))
                linear(f"x_o{l}", O, nk=4)
                tag = "d0" if l == 0 else "m2"
                norm(tag)
                if l == 0:
                    ffn(tag, M2, False)
                else:
                    route(tag, "route2")
                    route_rows(tag, E2)
                    ffn(tag, E2 * M2, True)
            norm("y")
            pe.wait_ge(S("normed"), nth("y"))
            for r in range(4):
                for s in range(2):
                    for c in range(2):
                        last = nc.tensor.transpose(PSB[4 + r][:, s * T + c * P:s * T + c * P + P],
                                                   H[:, 2 * r + c, s * P:s * P + P], ident)
                last.then_inc(S("y_tr"), 1)

        @block.scalar
        def _(act):
            fn = nc.scalar.activation

            def lin(name, i, out, func=ACT.Copy):
                act.wait_ge(S("a_used"), TILE0[name] + i + 1)
                fn(out, two(PSB[(LIN0[name] + i) % 2][:, :]), func).then_inc(S("lin_act"), 1)

            def norm(tag):
                _, dst, _, shift = NORMS[tag]
                act.wait_ge(S("mean_sq"), nth(tag))
                fn(RS[:, 0, :], PSB[3][:, 0:T], ACT.Sqrt, bias=con("eps")).then_inc(S("rms"), 1)
                if shift is not None:
                    for c in range(KC):
                        act.wait_ge(S("scaled"), shifted(tag) + c + 1)
                        last = fn(dst[:, c, :], SQ[:, c, :], ACT.Identity, bias=shift[:, c:c + 1])
                    last.then_inc(S("normed"), 1)

            def attend(tag):
                jobs = JOBS[tag]
                j0, t0, o0 = BEFORE[tag]
                def exps(j):
                    x = jobs[j]
                    act.wait_ge(S("masked"), j0 + j + 1)
                    if j >= 2:
                        act.wait_ge(S("weights"), j0 + j - 1)
                    for qt in range(2):
                        kk = x["keys"][qt]
                        if x["kind"] == "ml":
                            last = fn(PR[:, j % 2, qt, 0:kk], SM[:, j % 2, qt, 0:kk], ACT.Exp,
                                      bias=MCOL[:, 0, qt, x["h"]:x["h"] + 1])
                        else:
                            last = fn(PR[:, j % 2, qt, 0:kk], SM[:, j % 2, qt, 0:kk], ACT.Exp,
                                      bias=NM[:, j % 2, qt:qt + 1], accum_out=SUM[:, j % 2, qt:qt + 1])
                    last.then_inc(S("exps"), 1)

                def transposed(j):
                    x = jobs[j]
                    if not x["tr"]:
                        return
                    t_n = n_tr(jobs, j)
                    act.wait_ge(S("turned"), t0 + t_n)
                    if t_n > 2:
                        act.wait_ge(S("mixed"), t0 + t_n - 2)
                    bank = [PSB[6], PSB[2]][t_n % 2]
                    for kt, kr in enumerate(x["rows"]):
                        q0 = 0 if full(x, kt, 0) else P
                        last = fn(PT[0:kr, t_n % 2, kt, q0:T], bank[0:kr, kt * T + q0:kt * T + T], ACT.Copy)
                    last.then_inc(S("turned_out"), 1)

                def outputs(j):
                    x = jobs[j]
                    if not (x["tr"] and x["close"]):
                        return
                    act.wait_ge(S("mixed"), t0 + n_tr(jobs, j))
                    g = n_closed(jobs, j) - 1
                    fn(O[:, x["out"], :], OBANK[g % 2][:, 0:T], ACT.Copy).then_inc(S("outputs"), 1)

                exps(0)
                for j in range(len(jobs)):
                    if j + 1 < len(jobs):
                        exps(j + 1)
                    transposed(j)
                    if j:
                        outputs(j - 1)
                outputs(len(jobs) - 1)

            def group_mean(tag, n):
                for r in range(n):
                    act.wait_ge(S(f"gms_{tag}"), r + 1)
                    if r >= 1:
                        act.wait_ge(S(f"gd_{tag}"), r)
                    fn(RS[:, :, :], two(PSB[3][:, :]), ACT.Sqrt, bias=con("eps")).then_inc(S(f"gr_{tag}"), 1)

            def route(tag):
                act.wait_ge(S(f"re_{tag}"), 1)
                fn(RV[:, 6:8, :], RV[:, 4:6, :], ACT.Exp).then_inc(S(f"rx_{tag}"), 1)
                if tag != "m2":
                    act.wait_ge(S(f"rg_{tag}"), 1)
                    fn(R1[:, :, 0:4], R1[:, :, 0:4], ACT.Exp).then_inc(S(f"rx_{tag}"), 1)

            def route_rows(tag, ne):
                act.wait_ge(S(f"combt_{tag}"), 1)
                fn(COMBT[0:ne, :], PSB[3][0:ne, 0:T], ACT.Copy).then_inc(S(f"combr_{tag}"), 1)

            def ffn(tag, n):
                def silu(c, par, first=False):
                    act.wait_ge(S(f"gu_{tag}"), c + 1)
                    if not first:
                        act.wait_ge(S(f"up_{tag}"), c - 1)
                    fn(A1[:, par, :, :], two(PSB[2 * par][:, :]), ACT.Silu).then_inc(S(f"silu_{tag}"), 1)

                silu(0, 0, True)
                silu(1, 1, True)
                with act.Fori(0, (n - 2) // 2) as i:
                    for j in range(2):
                        silu(i * 2 + (2 + j), j)
                if n % 2:
                    silu(n - 1, (n - 1) % 2)

            act.wait_ge(S("con_in"), 16)
            act.wait_ge(S("cols_mm"), 1)
            for i in range(4):
                n = sum(k for _, k in ROW_TILES[i])
                last = fn(COLS[:, i * P:i * P + n], PSB[3][:, i * P:i * P + n], ACT.Copy)
            last.then_inc(S("cols"), 1)
            act.wait_ge(S("cols"), 1)
            fn(CACT[:, :], cols8("c"), ACT.Silu).then_inc(S("cact"), 1)
            for r in range(8):
                act.wait_ge(S("x_tr"), r + 1)
                dst = X if r < 4 else MEM
                fn(dst[:, 2 * (r % 4):2 * (r % 4) + 2, :], two(PSB[4 + r % 4][:, :]), ACT.Copy).then_inc(
                    S("x_cp"), 1)
            act.wait_ge(S("angle"), 2)
            fn(SIN[:, :], SM[:, 1, 0, :], ACT.Sin).then_inc(S("tables"), 1)
            fn(COS[:, :], SM[:, 0, 0, :], ACT.Sin, scale=-1.0, bias=con("halfpi")).then_inc(S("tables"), 1)
            act.wait_ge(S("lam_dot"), 1)
            fn(LAM[:, 2:4], LAM[:, 0:2], ACT.Exp).then_inc(S("lam_exp"), 1)

            norm("n0")
            for i in range(4):
                lin("diff_q", i, Q[:, 2 * i:2 * i + 2, :])
            for i in range(4):
                lin("diff_k", i, K[:, 2 * i:2 * i + 2, :])
            for i in range(4):
                lin("diff_v", i, V[:, :, i * NTILE:(i + 1) * NTILE])
            attend("a0")
            group_mean("g0", 4)
            norm("m0")
            route("m0")
            route_rows("m0", E1)
            ffn("m0", E1)

            norm("n1")
            for i in range(4):
                lin("nsa_q", i, Q[:, 2 * i:2 * i + 2, :])
            for i in range(3):
                lin("nsa_kv", i, K[:, 2 * i:2 * i + 2, :])
            act.wait_ge(S("gates_mm"), 1)
            for s in range(2):
                last = fn(GATE[:, s, :], PSB[2][:, s * 64:s * 64 + 48], ACT.Sigmoid)
            last.then_inc(S("gates"), 1)
            act.wait_ge(S("kvt_mm"), 1)
            fn(KVT[:, :, :, :].rearrange("p a b c -> p (a b c)"), PSB[7][:, :], ACT.Copy).then_inc(S("kvt"), 1)
            act.wait_ge(S("h1b"), 1)
            for kv in range(2):
                for s in range(2):
                    last = fn(H1G[:, kv, s, :], PSB[6][:, (2 * kv + s) * 32:(2 * kv + s) * 32 + 30],
                              ACT.Gelu_apprx_tanh, bias=H1[:, kv, s, 0:1])
            last.then_inc(S("h1g"), 1)
            attend("a1")
            norm("m1")
            route("m1")
            route_rows("m1", E1)
            ffn("m1", E1)
            norm("f1")

            for l in range(2):
                norm(f"x{l}")
                name = f"mix_in{l}"
                act.wait_ge(S(f"pads{l}"), 2)
                lin(name, 0, RAW[:, 0:2, 3:259])
                lin(name, 1, RAW[:, 2:4, 3:259])
                lin(name, 2, V[:, :, 0:256])
                lin(name, 3, Q[:, 2:4, :], ACT.Sigmoid)
                lin(name, 4, K[:, 2:4, :])
                lin(name, 5, LNM[:, :, :], ACT.Sigmoid)
                for i in range(2):
                    lin(name, 6 + i, Q[:, 4 + 2 * i:6 + 2 * i, :])
                for i in range(2):
                    lin(name, 8 + i, K[:, 4 + 2 * i:6 + 2 * i, :])
                for i in range(2):
                    lin(name, 10 + i, V[:, :, 512 + i * NTILE:512 + (i + 1) * NTILE])
                act.wait_ge(S(f"pre_mm{l}"), 1)
                act.wait_ge(S("pre_zero"), 1)
                for r, (rows, ps) in enumerate(((4, PSB[2][0:4, 0:T]), (4, PSB[2][0:4, T:2 * T]),
                                                (8, PSB[3][0:8, 0:T]))):
                    last = fn(PRE[0:rows, r, :], ps, ACT.Identity, bias=PB[0:rows, 3 * l + r:3 * l + r + 1])
                last.then_inc(S(f"pre{l}"), 1)
                act.wait_ge(S(f"pre_abs{l}"), 1)
                fn(PRE[:, 7:9, :], PRE[:, 7:9, :], ACT.Exp, scale=-1.0).then_inc(S(f"pre_ln{l}"), 1)
                act.wait_ge(S(f"pre_ln{l}"), 1)
                fn(PRE[:, 7:9, :], PRE[:, 7:9, :], ACT.Ln, bias=con("one", rows=8)).then_inc(S(f"pre_ln{l}"), 1)
                act.wait_ge(S(f"conv_ml{l}"), 1)
                fn(Q[:, 0:2, :], SM[:, 0, :, :], ACT.Silu)
                fn(K[:, 0:2, :], SM[:, 1, :, :], ACT.Silu).then_inc(S(f"qk_ml{l}"), 4)
                act.wait_ge(S(f"mcol_mm{l}"), 1)
                fn(MCOL[:, 0, :, :], PSB[6][:, 0:8].rearrange("p (s h) -> p s h", s=2), ACT.Copy,
                   scale=-1.0).then_inc(S(f"mcol{l}"), 1)
                fn(MCOL[:, 1, :, :], PSB[6][:, 8:16].rearrange("p (s h) -> p s h", s=2), ACT.Exp,
                   scale=-1.0).then_inc(S(f"mcol{l}"), 1)
                attend(f"mix{l}")
                group_mean(f"gm{l}", 1)
                act.wait_ge(S(f"ln_mm{l}"), 2)
                fn(RS[:, 0, :], PSB[2][:, 0:T], ACT.Sqrt, bias=con("eps")).then_inc(S(f"ln_rs{l}"), 1)
                act.wait_ge(S(f"ln_out{l}"), 1)
                for c in range(2):
                    last = fn(O[:, 2 + c, :], LNM[:, c, :], ACT.Silu, scale=col("ln_w", 2 * l + c),
                              bias=col("ln_b", 2 * l + c))
                last.then_inc(S(f"cat{l}"), 1)
                norm(f"mem{l}")
                norm(f"xa{l}")
                for i in range(2):
                    lin(f"x_q{l}", i, Q[:, 2 * i:2 * i + 2, :])
                for i in range(2):
                    lin(f"x_k{l}", i, K[:, 2 * i:2 * i + 2, :])
                for i in range(2):
                    lin(f"x_v{l}", i, V[:, :, i * NTILE:(i + 1) * NTILE])
                attend(f"xt{l}")
                tag = "d0" if l == 0 else "m2"
                norm(tag)
                if l == 0:
                    ffn(tag, M2)
                else:
                    route(tag)
                    route_rows(tag, E2)
                    ffn(tag, E2 * M2)
            norm("y")
            for r in range(4):
                act.wait_ge(S("y_tr"), r + 1)
                fn(YTOK[:, :, r * T:(r + 1) * T], two(PSB[4 + r][:, :]), ACT.Copy).then_inc(S("y_out"), 1)

        @block.gpsimd
        def _(pool):
            pool_n = [0]

            def link(ins):
                pool_n[0] += 1
                ins.then_inc(S("pool_done"), 1)
                pool.wait_ge(S("pool_done"), pool_n[0])

            def rows(tag, ne, k):
                pool.wait_ge(S(f"combr_{tag}"), 1)
                pool.dma_start(COMBD[k, 0:ne, :], COMBT[0:ne, :]).then_inc(S("comb_dram"), 16)
                pool.wait_ge(S("comb_dram"), 16 * (k + 1))
                pool.dma_start(CB[:, 0:ne, :], COMBD[k:k + 1, 0:ne, :].to_broadcast([P, ne, T])).then_inc(
                    S(f"cb_{tag}"), 16)

            nc.gpsimd.memset(PRE[:, :, :], 0.0).then_inc(S("pre_zero"), 1)
            rows("m0", E1, 0)
            rows("m1", E1, 1)
            for l in range(2):
                pool.wait_ge(S("lin_act"), emptied("act", LIN0[f"mix_in{l}"] + 5))
                pool.wait_ge(S("cols"), 1)
                link(nc.gpsimd.tensor_tensor(CPAD[:, :, 30:286], K[:, 2:4, :], LNM[:, :, :], ALU.mult))
                pool.wait_ge(S(f"pads{l}"), 2)
                for j in range(31):
                    taps = K[:, 2:4, :] if j else LNM[:, :, :]
                    for c in range(2):
                        w = col("conf_w", 62 * l + 2 * j + c)
                        if j == 0:
                            ins = nc.gpsimd.tensor_scalar(taps[:, c, :], CPAD[:, c, 0:T], w,
                                                          col("conf_b", 2 * l + c), ALU.mult, ALU.add)
                        else:
                            ins = nc.gpsimd.tensor_scalar(taps[:, c, :], CPAD[:, c, j:j + T], w, 0.0,
                                                          ALU.mult, ALU.add)
                    link(ins)
                    if j:
                        ins = nc.gpsimd.tensor_tensor(LNM[:, :, :], LNM[:, :, :], taps, ALU.add)
                        if j < 30:
                            link(ins)
                ins.then_inc(S(f"conv{l}"), 1)
            rows("m2", E2, 2)

        @block.vector
        def _(dve):
            done = [0]
            v = nc.vector

            def link(ins):
                done[0] += 1
                ins.then_inc(S("dve_done"), 1)
                dve.wait_ge(S("dve_done"), done[0])

            def norm(tag):
                src, dst, gain, shift = NORMS[tag]
                v.tensor_tensor(SQ[:, :, :], src[:, :, :], src[:, :, :], ALU.mult).then_inc(S("squares"), 1)
                dve.wait_ge(S("rms"), nth(tag))
                link(v.reciprocal(RS[:, 0, :], RS[:, 0, :]))
                for c in range(KC):
                    ins = v.scalar_tensor_tensor(out=(dst if shift is None else SQ)[:, c, :], in0=src[:, c, :],
                                                 scalar=gain[:, c:c + 1], in1=RS[:, 0, :],
                                                 op0=ALU.mult, op1=ALU.mult)
                    if shift is not None:
                        ins.then_inc(S("scaled"), 1)
                if shift is None:
                    ins.then_inc(S("normed"), 1)
                    dve.wait_ge(S("normed"), nth(tag))

            def rope(tag, pairs):
                for r, (x, _) in enumerate(pairs):
                    dve.wait_ge(S(f"rope_mm_{tag}"), r + 1)
                    v.tensor_tensor(PR[:, r % 2, :, :], two(PSB[4 + r % 2][:, :]), over2(SIN[:, :]), ALU.mult)
                    link(v.tensor_tensor(x, x, over2(COS[:, :]), ALU.mult))
                    v.tensor_tensor(x, x, PR[:, r % 2, :, :], ALU.add).then_inc(S(f"rope_use_{tag}"), 1)

            def attend(tag):
                jobs = JOBS[tag]
                j0, t0, o0 = BEFORE[tag]
                def front(j):
                    x = jobs[j]
                    dve.wait_ge(S("scores"), j0 + j + 1)
                    if j >= 2:
                        dve.wait_ge(S("exps"), j0 + j - 1)
                    bank = PSB[0] if x["kind"] == "ml" else PSB[4 + j % 2]
                    for qt in range(2):
                        kk = x["keys"][qt]
                        if x["kind"] == "ml":
                            ins = v.tensor_tensor(SM[:, j % 2, qt, 0:kk], bank[:, 0:kk], x["mask"][qt], ALU.add)
                        else:
                            ins = v.tensor_tensor_reduce(
                                out=SM[:, j % 2, qt, 0:kk], in0=bank[:, qt * T:qt * T + kk], in1=x["mask"][qt],
                                scale=x["scale"], scalar=-3e38, op0=ALU.add, op1=ALU.max,
                                accum_out=MX[:, j % 2, qt:qt + 1])
                    if x["kind"] != "ml":
                        link(ins)
                        ins = v.tensor_scalar(NM[:, j % 2, :], MX[:, j % 2, :], -1.0, None, ALU.mult)
                    ins.then_inc(S("masked"), 1)

                def back(j):
                    x = jobs[j]
                    dve.wait_ge(S("exps"), j0 + j + 1)
                    before = n_tr(jobs, j - 2) if j >= 2 else 0
                    if before:
                        dve.wait_ge(S("turned"), t0 + before)
                    f = FAC[:, j % 2, :]
                    if x["kind"] == "ml":
                        for qt in range(2):
                            kk = x["keys"][qt]
                            ins = v.tensor_tensor_reduce(
                                out=PN[:, j % 2, qt, 0:kk], in0=PSB[4 + j % 2][:, qt * T:qt * T + kk],
                                in1=PR[:, j % 2, qt, 0:kk], scale=x["scale"], scalar=0.0, op0=ALU.mult,
                                op1=ALU.add, accum_out=SUM[:, j % 2, qt:qt + 1])
                        link(ins)
                        link(v.scalar_tensor_tensor(out=f, in0=SUM[:, j % 2, :], scalar=-1.0,
                                                    in1=SUM[:, j % 2, :], op0=ALU.mult, op1=ALU.max))
                        link(v.tensor_tensor(f, f, MCOL[:, 1, :, x["h"]], ALU.max))
                        link(v.reciprocal(f, f))
                        src = PN
                    else:
                        link(v.reciprocal(f, SUM[:, j % 2, :]))
                        if x["kind"] == "diff1":
                            link(v.tensor_scalar(f, f, LAM[:, 4:5], None, ALU.mult))
                        if x["gate"] is not None:
                            link(v.tensor_tensor(f, f, GATE[:, :, x["gate"]], ALU.mult))
                        if x["kind"] == "cmp":
                            link(v.tensor_tensor(f, f, con("cmp_valid"), ALU.mult))
                        src = PR
                    for qt in range(2):
                        kk = x["keys"][qt]
                        if x["kind"] == "diff1":
                            ins = v.scalar_tensor_tensor(
                                out=PN[:, j % 2, qt, 0:kk], in0=PR[:, j % 2, qt, 0:kk], scalar=f[:, qt:qt + 1],
                                in1=PN[:, (j - 1) % 2, qt, 0:kk], op0=ALU.mult, op1=ALU.add)
                        else:
                            ins = v.tensor_scalar(PN[:, j % 2, qt, 0:kk], src[:, j % 2, qt, 0:kk],
                                                  f[:, qt:qt + 1], None, ALU.mult)
                    ins.then_inc(S("weights"), 1)
                    if x["kind"] == "diff0":
                        dve.wait_ge(S("weights"), j0 + j + 1)

                front(0)
                for j in range(len(jobs)):
                    if j + 1 < len(jobs):
                        front(j + 1)
                    back(j)

            def residual(name, i, gate=None):
                dve.wait_ge(S("a_used"), TILE0[name] + i + 1)
                bank = PSB[(LIN0[name] + i) % 2]
                if gate is None:
                    ins = v.tensor_tensor(X[:, 2 * i:2 * i + 2, :], two(bank[:, :]), X[:, 2 * i:2 * i + 2, :],
                                          ALU.add)
                else:
                    for s in range(2):
                        c = 2 * i + s
                        ins = v.scalar_tensor_tensor(out=X[:, c, :], in0=bank[:, s * T:s * T + T],
                                                     scalar=gate[:, c:c + 1], in1=X[:, c, :],
                                                     op0=ALU.mult, op1=ALU.add)
                ins.then_inc(S("lin_dve"), 1)
                dve.wait_ge(S("lin_dve"), emptied("dve", LIN0[name] + i))

            def group_squares(tag, n):
                for r in range(n):
                    v.tensor_tensor(SQ[:, 2 * r:2 * r + 2, :], O[:, 2 * r:2 * r + 2, :],
                                    O[:, 2 * r:2 * r + 2, :], ALU.mult).then_inc(S(f"gsq_{tag}"), 1)

            def first_max(x, mx, n, hot, tmp, low):
                b = mx.unsqueeze(2).to_broadcast([P, 2, n])
                link(v.tensor_tensor(tmp[:, :, 0:n], x, b, ALU.is_equal))
                link(v.scalar_tensor_tensor(out=tmp[:, :, 0:n], in0=tmp[:, :, 0:n], scalar=-1000.0,
                                            in1=con("iota", rows=P)[:, 0:n].unsqueeze(1).to_broadcast([P, 2, n]),
                                            op0=ALU.mult, op1=ALU.add))
                link(v.tensor_reduce(low, tmp[:, :, 0:n], AX.X, ALU.min))
                link(v.tensor_tensor(hot[:, :, 0:n], tmp[:, :, 0:n],
                                     low.unsqueeze(2).to_broadcast([P, 2, n]), ALU.is_equal))

            def route(tag, k, w):
                dve.wait_ge(S(f"rl_{tag}"), 1)
                link(v.tensor_tensor(LG[:, :, 0:w], PSB[2][:, 0:128].rearrange("p (s n) -> p s n", s=2)[:, :, 0:w],
                                     RB[:, k:k + 1, 0:w].to_broadcast([P, 2, w]), ALU.add))
                ne = E2 if tag == "m2" else E1
                if tag == "m2":
                    x = LG[:, :, 0:E2]
                else:
                    g4 = LG[:, :, 0:4]
                    link(v.tensor_reduce(RV[:, 0, :], g4, AX.X, ALU.max))
                    first_max(g4, RV[:, 0, :], 4, R2, R3, RV[:, 1, :])
                    v.tensor_tensor(R1[:, :, 0:4], g4, RV[:, 0, :].unsqueeze(2).to_broadcast([P, 2, 4]),
                                    ALU.subtract).then_inc(S(f"rg_{tag}"), 1)
                    link(v.tensor_scalar(R2[:, :, 0:4], R2[:, :, 0:4], 1e30, -1e30, ALU.mult, ALU.add))
                    for s in range(2):
                        ins = v.tensor_tensor(
                            R4[:, s, :].rearrange("p (g e) -> p g e", g=4),
                            LG[:, s, 4:36].rearrange("p (g e) -> p g e", g=4),
                            R2[:, s, 0:4].unsqueeze(2).to_broadcast([P, 4, 8]), ALU.add)
                    link(ins)
                    x = R4[:, :, :]
                link(v.tensor_reduce(RV[:, 2, :], x, AX.X, ALU.max))
                first_max(x, RV[:, 2, :], ne, R5, R3, RV[:, 1, :])
                link(v.scalar_tensor_tensor(out=R3[:, :, 0:ne], in0=R5[:, :, 0:ne], scalar=-1e32, in1=x,
                                            op0=ALU.mult, op1=ALU.add))
                link(v.tensor_reduce(RV[:, 3, :], R3[:, :, 0:ne], AX.X, ALU.max))
                first_max(R3[:, :, 0:ne], RV[:, 3, :], ne, R2, R2, RV[:, 1, :])
                v.memset(RV[:, 5, :], 0.0)
                v.tensor_tensor(RV[:, 4, :], RV[:, 3, :], RV[:, 2, :], ALU.subtract).then_inc(S(f"re_{tag}"), 1)
                dve.wait_ge(S(f"rx_{tag}"), 1 if tag == "m2" else 2)
                link(v.tensor_scalar(RV[:, 8, :], RV[:, 6, :], 1.0, None, ALU.add))
                if tag != "m2":
                    link(v.tensor_reduce(RV[:, 9, :], R1[:, :, 0:4], AX.X, ALU.add))
                    link(v.tensor_tensor(RV[:, 8, :], RV[:, 8, :], RV[:, 9, :], ALU.mult))
                link(v.reciprocal(RV[:, 9, :], RV[:, 8, :]))
                link(v.tensor_tensor(RV[:, 10, :], RV[:, 9, :], RV[:, 6, :], ALU.mult))
                bc = lambda r: RV[:, r, :].unsqueeze(2).to_broadcast([P, 2, ne])
                v.tensor_tensor(R5[:, :, 0:ne], R5[:, :, 0:ne], bc(9), ALU.mult)
                link(v.tensor_tensor(R2[:, :, 0:ne], R2[:, :, 0:ne], bc(10), ALU.mult))
                v.tensor_tensor(CTOK[:, :, 0:ne], R5[:, :, 0:ne], R2[:, :, 0:ne], ALU.add).then_inc(
                    S(f"comb_{tag}"), 1)

            def ffn(tag, n, weight, body, gate=None):
                def chunk(c, j, cb, first=False):
                    par = j % 2
                    dve.wait_ge(S(f"silu_{tag}"), c + 1)
                    if cb is None and not first:
                        dve.wait_ge(S(f"f_used_{tag}"), c - 1)
                    v.tensor_tensor(A2[:, par, :, :], A1[:, par, :, :], two(PSB[2 * par + 1][:, :]),
                                    ALU.mult).then_inc(S(f"up_{tag}"), 1)
                    if cb is not None:
                        dve.wait_ge(S(f"up_{tag}"), c + 1)
                        if not first:
                            dve.wait_ge(S(f"f_used_{tag}"), c - 1)
                        v.tensor_tensor(A3[:, par, :, :], A2[:, par, :, :], cb.to_broadcast([P, 2, T]),
                                        ALU.mult).then_inc(S(f"a3_{tag}"), 1)

                if weight:
                    dve.wait_ge(S(f"cb_{tag}"), 16)
                for c in range(body):
                    chunk(c, c, weight and CB[:, c:c + 1, :], c < 2)
                loops = n // body - 1
                with dve.Fori(0, loops) as i:
                    for j in range(body):
                        if weight == "fixed":
                            cb = CB[:, j:j + 1, :]
                        else:
                            cb = weight and CB[:, bass.ds(i * body + (body + j), 1), :]
                        chunk(i * body + (body + j), j, cb)
                for c in range((loops + 1) * body, n):
                    chunk(c, c, None)
                dve.wait_ge(S(f"f_used_{tag}"), n)
                for b in range(4):
                    if gate is None:
                        ins = v.tensor_tensor(X[:, 2 * b:2 * b + 2, :], two(PSB[4 + b][:, :]),
                                              X[:, 2 * b:2 * b + 2, :], ALU.add)
                    else:
                        for s in range(2):
                            c = 2 * b + s
                            ins = v.scalar_tensor_tensor(out=X[:, c, :], in0=PSB[4 + b][:, s * T:s * T + T],
                                                         scalar=gate[:, c:c + 1], in1=X[:, c, :],
                                                         op0=ALU.mult, op1=ALU.add)
                link(ins)

            dve.wait_ge(S("con_in"), 16)
            dve.wait_ge(S("small_in"), 96)
            link(v.tensor_copy(SM[:, 0, 1, :], SM[:, 0, 0, :].bitcast(I32)))
            link(v.tensor_scalar(SM[:, 1, 0, :], SM[:, 0, 1, :], con("invfreq"), None, ALU.mult))
            link(v.tensor_scalar(SM[:, 1, 1, :], SM[:, 1, 0, :], 1.0 / (2 * math.pi), None, ALU.mult))
            magic = 1.5 * 2.0 ** 23
            link(v.tensor_scalar(SM[:, 1, 1, :], SM[:, 1, 1, :], magic, None, ALU.add))
            link(v.tensor_scalar(SM[:, 1, 1, :], SM[:, 1, 1, :], magic, None, ALU.subtract))
            p1 = 6.28125
            p2 = round((2 * math.pi - p1) * 2 ** 20) / 2 ** 20
            for part in (p1, p2, 2 * math.pi - p1 - p2):
                link(v.scalar_tensor_tensor(out=SM[:, 1, 0, :], in0=SM[:, 1, 1, :], scalar=-part,
                                            in1=SM[:, 1, 0, :], op0=ALU.mult, op1=ALU.add))
            v.tensor_scalar(SM[:, 1, 0, :], SM[:, 1, 0, :], 3.141592, -3.141592, ALU.min, ALU.max).then_inc(
                S("angle"), 1)
            dve.wait_ge(S("angle"), 1)
            v.scalar_tensor_tensor(out=SM[:, 0, 0, :], in0=SM[:, 1, 0, :], scalar=-1.0, in1=SM[:, 1, 0, :],
                                   op0=ALU.mult, op1=ALU.max).then_inc(S("angle"), 1)
            for i in range(2):
                ins = v.tensor_tensor_reduce(out=PR[:, 0, i, 0:64], in0=LAMR[:, 128 * i:128 * i + 64],
                                             in1=LAMR[:, 128 * i + 64:128 * i + 128], scale=1.0, scalar=0.0,
                                             op0=ALU.mult, op1=ALU.add, accum_out=LAM[:, i:i + 1])
            ins.then_inc(S("lam_dot"), 1)
            dve.wait_ge(S("lam_exp"), 1)
            dve.wait_ge(S("cols"), 1)
            lam_init = 0.8 - 0.6 * math.exp(0.0)
            v.scalar_tensor_tensor(out=LAM[:, 4:5], in0=LAM[:, 3:4], scalar=-lam_init, in1=LAM[:, 2:3],
                                   op0=ALU.add, op1=ALU.subtract)
            v.tensor_scalar(LAM[:, 5:6], col("subln"), 1.0 - lam_init, None, ALU.mult)
            dve.wait_ge(S("a_used"), 48)
            link(v.tensor_tensor(MODS[:, :], PSB[2][:, 0:96], COLS[:, COL["ada_b"]:COL["ada_b"] + 96], ALU.add))
            for i in range(4):
                ins = v.scalar_tensor_tensor(out=AG[:, i, :], in0=mods(i // 2, 1 + 3 * (i % 2)), scalar=1.0,
                                             in1=cols8("norm_g", i), op0=ALU.add, op1=ALU.mult)
            link(ins)
            dve.wait_ge(S("x_cp"), 8)

            norm("n0")
            dve.wait_ge(S("tables"), 2)
            rope("r0", rope_pairs(0))
            attend("a0")
            dve.wait_ge(S("outputs"), outputs_of("a0", 8))
            group_squares("g0", 4)
            for r in range(4):
                dve.wait_ge(S("gr_g0"), r + 1)
                link(v.reciprocal(RS[:, :, :], RS[:, :, :]))
                for s in range(2):
                    c = 2 * r + s
                    ins = v.scalar_tensor_tensor(out=O[:, c, :], in0=O[:, c, :], scalar=LAM[:, 5:6],
                                                 in1=RS[:, s, :], op0=ALU.mult, op1=ALU.mult)
                ins.then_inc(S("gd_g0"), 1)
            for i in range(4):
                residual("diff_o", i, mods(0, 2))
            norm("m0")
            route("m0", 0, 36)
            ffn("m0", E1, "by chunk", 2, mods(0, 5))

            norm("n1")
            rope("r1", rope_pairs(1))
            dve.wait_ge(S("lin_act"), emptied("act", LIN0["nsa_kv"]))
            for kv in range(2):
                z = CMPZ[:, kv].rearrange("p a t -> p (a t)")[:, 0:496].rearrange("p (m n) -> p m n", m=16)
                for g in range(2):
                    src = K[64 * g:64 * g + 64, kv, :].rearrange("p (a r) -> p a r", r=16)
                    for par in range(2):
                        for mh in range(2):
                            v.tensor_copy(z[64 * par:64 * par + 64, 8 * mh:8 * mh + 8,
                                            15 * g:15 * g + 15].rearrange("p m n -> p n m"),
                                          src[:, mh:mh + 15, par:16:2])
                v.tensor_copy(z[:, :, 30:31], COLS[:, COL["cmp_pos"] + 16 * kv:COL["cmp_pos"] + 16 * kv + 16]
                              .unsqueeze(2)).then_inc(S("cmpz"), 1)
            dve.wait_ge(S("a_used"), TILE0["cmp"] + 4)
            v.tensor_tensor(H1[:, :, :, 0].rearrange("p a b -> p (a b)"), PSB[6][:, 30:128:32],
                            COLS[:, COL["cmp_b1"]:COL["cmp_b1"] + 4], ALU.add).then_inc(S("h1b"), 1)
            dve.wait_ge(S("cmp_out"), 1)
            for g in range(2):
                a = slice(64 * g, 64 * g + 64)
                v.tensor_copy(KCMP[a, 0:15], PSB[3][a, 15 * g:15 * g + 15])
            v.tensor_copy(VCMP[0:15, :, :], PSB[3][0:15, 64:192].rearrange("p (g d) -> p g d", g=2)).then_inc(
                S("cmp_kv"), 2)
            dve.wait_ge(S("gates"), 1)
            attend("a1")
            for i in range(4):
                residual("nsa_o", i, mods(1, 2))
            norm("m1")
            route("m1", 1, 36)
            ffn("m1", E1, "by chunk", 2, mods(1, 5))
            norm("f1")

            for l in range(2):
                norm(f"x{l}")
                v.memset(RAW[:, :, 0:3], 0.0).then_inc(S(f"pads{l}"), 1)
                v.memset(CPAD[:, :, 0:30], 0.0).then_inc(S(f"pads{l}"), 1)
                dve.wait_ge(S(f"pads{l}"), 2)
                dve.wait_ge(S("lin_act"), emptied("act", LIN0[f"mix_in{l}"] + 1))
                for j in range(4):
                    for c in range(4):
                        acc = SM[:, c // 2, c % 2, :]
                        w = col("ml_w", 16 * l + 4 * j + c)
                        if j == 0:
                            ins = v.tensor_scalar(acc, RAW[:, c, 0:T], w, col("ml_b", 4 * l + c),
                                                  ALU.mult, ALU.add)
                        else:
                            ins = v.scalar_tensor_tensor(out=acc, in0=RAW[:, c, j:j + T], scalar=w, in1=acc,
                                                         op0=ALU.mult, op1=ALU.add)
                    if j < 3:
                        link(ins)
                ins.then_inc(S(f"conv_ml{l}"), 1)
                dve.wait_ge(S(f"pre{l}"), 1)
                dve.wait_ge(S("pre_zero"), 1)
                z = PRE[:, 1:3, :]
                v.scalar_tensor_tensor(out=PRE[:, 7:9, :], in0=z, scalar=-1.0, in1=z, op0=ALU.mult,
                                       op1=ALU.max).then_inc(S(f"pre_abs{l}"), 1)
                dve.wait_ge(S(f"pre_ln{l}"), 2)
                link(v.scalar_tensor_tensor(out=z, in0=z, scalar=0.0, in1=PRE[:, 7:9, :], op0=ALU.min,
                                            op1=ALU.subtract))
                zero = con("zero", rows=8)
                v.tensor_tensor_scan(PRE[:, 7, :], PRE[:, 2, :], zero, 0.0, ALU.add, ALU.add)
                link(v.tensor_tensor_scan(PRE[0:4, 3, :], PRE[0:4, 1, :], zero[0:4, :], 0.0, ALU.add, ALU.add))
                v.tensor_scalar(PRE[:, 9, :], PRE[:, 7, :], -8.0, None, ALU.mult)
                link(v.tensor_tensor(PRE[0:4, 4, :], PRE[0:4, 0, :], PRE[0:4, 3, :], ALU.subtract))
                link(v.tensor_tensor_scan(PRE[0:4, 5, :], PRE[0:4, 4, :], PRE[0:4, 4, :], 0.0, ALU.max, ALU.max))
                v.tensor_tensor(PRE[0:4, 6, :], PRE[0:4, 3, :], PRE[0:4, 5, :], ALU.add).then_inc(
                    S(f"pre_rows{l}"), 1)
                dve.wait_ge(S(f"mcol{l}"), 2)
                dve.wait_ge(S(f"qk_ml{l}"), 4)
                attend(f"mix{l}")
                dve.wait_ge(S("outputs"), outputs_of(f"mix{l}", 2))
                group_squares(f"gm{l}", 1)
                dve.wait_ge(S(f"gr_gm{l}"), 1)
                link(v.reciprocal(RS[:, :, :], RS[:, :, :]))
                link(v.tensor_tensor(O[:, 0:2, :], O[:, 0:2, :], RS[:, :, :], ALU.mult))
                for c in range(2):
                    ins = v.scalar_tensor_tensor(out=O[:, c, :], in0=O[:, c, :], scalar=col("ml_norm", 2 * l + c),
                                                 in1=Q[:, 2 + c, :], op0=ALU.mult, op1=ALU.mult)
                ins.then_inc(S(f"cat{l}"), 1)
                dve.wait_ge(S(f"ln_mm{l}"), 1)
                link(v.tensor_tensor(LNM[:, :, :], LNM[:, :, :], over2(PSB[6][:, 0:T]), ALU.subtract))
                v.tensor_tensor(SQ[:, 6:8, :], LNM[:, :, :], LNM[:, :, :], ALU.mult).then_inc(S(f"ln_sq{l}"), 1)
                dve.wait_ge(S(f"ln_rs{l}"), 1)
                link(v.reciprocal(RS[:, 0, :], RS[:, 0, :]))
                v.tensor_tensor(LNM[:, :, :], LNM[:, :, :], over2(RS[:, 0, :]), ALU.mult).then_inc(
                    S(f"ln_out{l}"), 1)
                for i in range(4):
                    residual(f"mix_o{l}", i)
                norm(f"mem{l}")
                norm(f"xa{l}")
                attend(f"xt{l}")
                for i in range(4):
                    residual(f"x_o{l}", i)
                tag = "d0" if l == 0 else "m2"
                norm(tag)
                if l == 0:
                    ffn(tag, M2, None, 2)
                else:
                    route(tag, 2, E2)
                    ffn(tag, E2 * M2, "fixed", 8)
            norm("y")


def constants():
    c = {n: np.zeros((P, k), np.float32) for n, k in CONSTS}
    i = np.arange(P)
    c["ident"][i, i] = 1.0
    c["mean_d"][:] = 1.0 / D
    c["mean_128"][:] = 1.0 / 128
    c["mean_256"][:] = 1.0 / 256
    c["mean_64"][:] = (i[:, None] // 64 == i[None, :] // 64) / 64.0
    for p in range(P):
        r = p % 64
        if r < 8:
            c["rope"][p + 8, p] = -1.0
            c["invfreq"][p] = np.float32(500000.0) ** np.float32(-2.0 * r / 16)
        elif r < 16:
            c["rope"][p - 8, p] = 1.0
            c["invfreq"][p] = np.float32(500000.0) ** np.float32(-2.0 * (r - 8) / 16)
    diag = np.where(i[:, None] >= i[None, :], 0.0, NEG)
    c["causal"][:, 0:P] = diag
    c["causal"][:, 2 * P:3 * P] = diag
    for s in range(2):
        ok = 16 * np.arange(15)[None, :] + 31 <= (i + P * s)[:, None]
        c["cmp_mask"][:, 16 * s:16 * s + 15] = np.where(ok, 0.0, NEG)
        c["cmp_valid"][:, s] = ok.any(1)
    c["iota"][:] = np.arange(32)
    c["eps"][:] = EPS
    c["halfpi"][:] = math.pi / 2
    c["one"][:] = 1.0
    for h in range(8):
        c["sel"][h, h * P:(h + 1) * P] = 1.0
    return np.concatenate([c[n] for n, _ in CONSTS], axis=1)


def tiles(w, nc_=NTILE):
    k, n = w.shape
    return np.ascontiguousarray(w.reshape(k // P, P, n // nc_, nc_).transpose(2, 1, 0, 3)).reshape(
        n // nc_, P, k // P * nc_)


def small(w):
    return tiles(np.ascontiguousarray(w), w.shape[1])[0]


def ffn_chunks(gate, up, down):
    e, d, f = gate.shape
    m = f // HID
    out = np.empty((m, e, P, 3, NFREE), np.float32)
    for a, w in enumerate((gate, up)):
        out[:, :, :, a] = w.reshape(e, KC, P, m, HID).transpose(3, 0, 2, 1, 4).reshape(m, e, P, NFREE)
    out[:, :, :, 2] = down.reshape(e, m, 2, P, D).transpose(1, 0, 3, 2, 4).reshape(m, e, P, NFREE)
    return out.reshape(m * e, P, 3 * NFREE)


def lay_out(x):
    a = {}
    a["x"] = x["x"][0]
    a["mem"] = x["mem_2"][0]
    a["consts"] = constants()
    r = lambda v: np.asarray(v).reshape(-1, P)
    rows = {"ada_b": r(x["ada_b"]), "c": r(x["c"]), "cmp_b1": r(x["nsa_cmp_b1"]), "subln": r(x["diff_subln_g"]),
            "norm_g": r(x["norm_g"]), "final_g": r(x["final_g"]), "norm_mix": r(x["norm_mix_w_2"]),
            "norm_x": r(x["norm_xattn_w_2"]), "norm_mem": r(x["norm_mem_w_2"]), "norm_ffn": r(x["norm_ffn_w_2"]),
            "norm_final": r(x["norm_final_w_2"]), "conf_w": r(x["conf_conv_w_2"]), "ml_w": r(x["mlstm_conv_w_2"]),
            "ml_b": r(x["mlstm_conv_b_2"]), "conf_b": r(x["conf_conv_b_2"]), "ln_w": r(x["conf_ln_w_2"]),
            "ln_b": r(x["conf_ln_b_2"]), "ml_norm": r(x["mlstm_norm_w_2"]), "cmp_pos": r(x["nsa_cmp_pos"])}
    for i, names in enumerate(ROW_TILES):
        a[f"rows{i}"] = np.concatenate([rows[n] for n, _ in names])
    a["pos"] = np.asarray(x["positions"]).reshape(1, T)
    a["lam"] = x["diff_lambda"].reshape(1, 256)
    route_b = np.zeros((1, 108), np.float32)
    for l in range(2):
        route_b[0, 36 * l:36 * l + 4] = x["moe_b_group"][l]
        route_b[0, 36 * l + 4:36 * l + 36] = x["moe_b_expert"][l].reshape(-1)
    a["route_b"] = route_b
    pre_b = np.zeros((8, 6), np.float32)
    for l in range(2):
        pre_b[0:4, 3 * l] = x["mlstm_b_i_2"][l]
        pre_b[0:4, 3 * l + 1] = x["mlstm_b_f_2"][l]
        pre_b[0:8, 3 * l + 2] = x["fox_b_f_2"][l]
    a["pre_b"] = pre_b
    w2 = x["nsa_cmp_w2"][0].reshape(2, 2, P, 64)
    a["cmp_w2"] = np.concatenate([w2, w2], axis=3).transpose(2, 0, 1, 3).reshape(P, 512)
    nsa = x["nsa_w_in"][0]
    win = x["w_in_2"]
    group = [np.concatenate([x["moe_w_group"][l], x["moe_w_expert"][l].transpose(1, 0, 2).reshape(D, E1)], axis=1)
             for l in range(2)]
    a["small"] = np.concatenate(
        [small(nsa[:, 1792:1840]), small(group[0]), small(group[1]), small(x["router_w_2"][0])]
        + [small(np.concatenate([win[l][:, 1024:1032], win[l][:, 3080:3088]], axis=1)) for l in range(2)], axis=1)
    order = np.arange(1024).reshape(2, 8, 64).transpose(1, 0, 2).reshape(-1)
    parts = [tiles(x["ada_w"][0]), tiles(x["ada_w"][1]), tiles(x["diff_w_in"][0]), tiles(x["diff_w_out"][0]),
             tiles(nsa[:, 0:1024][:, order]), tiles(np.ascontiguousarray(nsa[:, 1024:1792]))]
    w1 = x["nsa_cmp_w1"][0].reshape(2, 2, 8, P, 256).transpose(0, 1, 3, 2, 4).reshape(4, P, NFREE)
    parts += [w1, tiles(x["nsa_w_out"][0][order])]
    for l in range(2):
        main = np.concatenate([win[l][:, 0:1024], win[l][:, 1032:3080]], axis=1)
        parts += [tiles(main), tiles(x["w_out_2"][l]), tiles(x["xattn_w_q_2"][l]), tiles(x["xattn_w_kv_2"][l])]
    a["wa"] = np.concatenate(parts)
    a["xo"] = np.concatenate([tiles(x["xattn_w_o_2"][l]) for l in range(2)])
    for l in range(2):
        a[f"wf{l}"] = ffn_chunks(x["moe_w_gate"][l], x["moe_w_up"][l], x["moe_w_down"][l])
    a["wf2"] = ffn_chunks(x["ffn_w_gate_2"], x["ffn_w_up_2"], x["ffn_w_down_2"])
    a["wf3"] = ffn_chunks(x["moe_w_gate_2"][0], x["moe_w_up_2"][0], x["moe_w_down_2"][0])
    return {k: np.ascontiguousarray(v) for k, v in a.items()}


def kernel(**inputs):
    import concourse.bacc as bacc
    from concourse.bass_utils import run_bass_kernel_spmd

    arrays = lay_out({k: np.asarray(v) for k, v in inputs.items()})
    nc = bacc.Bacc("TRN2", target_bir_lowering=False, num_devices=1, dynamic_dma_scratch_size=4096)
    t = {n: nc.dram_tensor(f"in_{n}", a.shape, mybir.dt.from_np(a.dtype), kind="ExternalInput").ap()
         for n, a in arrays.items()}
    t["out"] = nc.dram_tensor("out", (T, D), F32, kind="ExternalOutput").ap()
    build(nc, t)
    r = run_bass_kernel_spmd(nc, [{f"in_{n}": a for n, a in arrays.items()}], core_ids=[0])
    return r.results[0]["out"].reshape(1, T, D)
```

```python
import math
from contextlib import ExitStack

import numpy as np

import concourse.bass as bass
from concourse import mybir

P = 128
D = 1024
T = 256
KC = D // P
NTILE = 256
HID = 256
NEG = -1e30
EPS = 1e-6
RING_A = 3
RING_F = 3
E1 = 32
E2 = 8
FF2 = 2816
CAP = 96
G1 = 4
W1 = G1 + T // (CAP + 1)
M2 = FF2 // HID
W2 = E2 + 2 * T // (CAP + 1)
NFREE = 2048
ADA_R = 3
ADA_N = 2 * 6 * D // NTILE // ADA_R

F32 = mybir.dt.float32
I32 = mybir.dt.int32
ALU = mybir.AluOpType
ACT = mybir.ActivationFunctionType
AX = mybir.AxisListType

ROW_TILES = [
    [("ada_b", 96), ("c", 8), ("cmp_b1", 4), ("subln", 1)],
    [("norm_g", 32), ("final_g", 8), ("norm_mix", 16), ("norm_x", 16), ("norm_mem", 16),
     ("norm_ffn", 16), ("norm_final", 8)],
    [("conf_w", 124)],
    [("ml_w", 32), ("ml_b", 8), ("conf_b", 4), ("ln_w", 4), ("ln_b", 4), ("ml_norm", 4),
     ("cmp_pos", 32)],
]
COL = {}
for _t, _rows in enumerate(ROW_TILES):
    _at = 0
    for _name, _n in _rows:
        COL[_name] = _t * P + _at
        _at += _n

CONSTS = [("ident", P), ("mean_d", P), ("mean_128", P), ("mean_64", P), ("mean_256", P),
          ("rope", P), ("causal", 3 * P), ("zero", 2 * P), ("cmp_mask", 32), ("cmp_valid", 2),
          ("iota", 96), ("tri", P), ("ones", P), ("invfreq", 1), ("eps", 1), ("halfpi", 1), ("sel", 8 * P)]
CAT = {}
_at = 0
for _name, _n in CONSTS:
    CAT[_name] = _at
    _at += _n
NCONST = _at

SMALL = [("gates", 48), ("route0", 36), ("route1", 36), ("route2", 8), ("pre0", 16), ("pre1", 16)]
SAT = {}
_at = 0
for _name, _n in SMALL:
    SAT[_name] = (_at, _n)
    _at += KC * _n
NSMALL = _at

GROUPS = [("diff_q", 4, "act"), ("diff_k", 4, "act"), ("diff_v", 4, "act"),
          ("diff_o", 4, "dve"), ("nsa_kv", 3, "act"), ("nsa_q", 4, "act"), ("cmp", 4, None),
          ("nsa_o", 4, "dve")]
for _l in range(2):
    GROUPS += [(f"mix_in{_l}", 12, "act"), (f"mix_o{_l}", 4, "dve"), (f"x_q{_l}", 2, "act"),
               (f"x_k{_l}", 2, "act"), (f"x_v{_l}", 2, "act"), (f"x_o{_l}", 4, "dve")]
TILE0, LIN0, OWNER = {}, {}, []
_n = 0
for _name, _k, _who in GROUPS:
    TILE0[_name] = _n
    LIN0[_name] = len(OWNER)
    _n += _k
    if _who:
        OWNER += [_who] * _k
NT = _n
NTILES = {g[0]: g[1] for g in GROUPS}
WA_AT, XO_AT = {}, {}
for _name, _k, _who in GROUPS:
    for _i in range(_k):
        if _name.startswith("x_o"):
            XO_AT[TILE0[_name] + _i] = len(XO_AT)
        else:
            WA_AT[TILE0[_name] + _i] = len(WA_AT)


def emptied(who, lin):
    return sum(1 for w in OWNER[:lin + 1] if w == who)


def build(nc, t):
    ctx = ExitStack()
    with ctx:
        def sb(name, shape, dt=F32):
            return ctx.enter_context(nc.sbuf_tensor(name, shape, dt))

        sems = {}

        def S(name):
            if name not in sems:
                sems[name] = ctx.enter_context(nc.semaphore(name))
            return sems[name]

        CON = sb("CON", [P, NCONST])
        SMW = sb("SMW", [P, NSMALL])
        COLS = sb("COLS", [P, 4 * P])
        WA = [sb(f"WA{i}", [P, NFREE]) for i in range(RING_A)]
        WF = [sb(f"WF{i}", [P, 3, NFREE]) for i in range(RING_F)]
        X = sb("X", [P, KC, T])
        H = sb("H", [P, KC, T])
        MEM = sb("MEM", [P, KC, T])
        BIG = sb("BIG", [P, 4 * KC, T])
        Q = BIG[:, 0:KC, :]
        K = BIG[:, KC:2 * KC, :]
        V = BIG[:, 2 * KC:3 * KC, :].rearrange("p (s c) t -> p s (c t)", s=2)
        O = BIG[:, 3 * KC:4 * KC, :]
        OTOK = O.rearrange("p (s c) t -> p s (c t)", s=2)
        YTOK = Q.rearrange("p (s c) t -> p s (c t)", s=2)
        flat = BIG[:, :, :].rearrange("p c t -> p (c t)")
        HTOK = flat[:, 0:2048].rearrange("p (s d) -> p s d", s=2)
        HG = flat[:, 2048:2816].rearrange("p (k n) -> p k n", k=KC)
        CBG = flat[:, 2816:3584].rearrange("p (e n) -> p e n", e=8)
        PICK = flat[:, 3584:3776].rearrange("p (s n) -> p s n", s=2)
        PICKW = flat[:, 3776:3968].rearrange("p (s n) -> p s n", s=2)
        PICKE = flat[:, 3968:5504].rearrange("p (s e n) -> p s e n", s=2, e=8)
        YDS = flat[:, 5504:6272].rearrange("p (k n) -> p k n", k=KC)
        YTK = flat[:, 6272:7296]
        PUT = flat[:, 7296:7552]
        WRK = flat[:, 7552:8192]
        SQ = sb("SQ", [P, KC, T])
        SM = sb("SM", [P, 2, 2, T])
        PR = sb("PR", [P, 2, 2, T])
        PN = sb("PN", [P, 2, 2, T])
        PT = sb("PT", [P, 2, 2, T])
        FOLD = PT
        A1 = PR
        A2 = PN
        A3 = PT
        NTH = {"m0": 0, "m1": 1, "m2": 2}
        MOE = {"m0": (G1, 8, True), "m1": (G1, 8, True), "m2": (E2, M2, False)}
        COS = sb("COS", [P, T])
        SIN = sb("SIN", [P, T])
        RS = sb("RS", [P, 2, T])
        MODS = sb("MODS", [P, 96])
        AG = sb("AG", [P, 4, KC])
        CACT = sb("CACT", [P, KC])
        LAM = sb("LAM", [P, 16])
        LAMR = PN[:, 0, 0, :]
        GATE = sb("GATE", [P, 2, 48])
        KVT = sb("KVT", [P, 2, 2, P])
        ST = sb("ST", [P, 32])
        MX, NM, SUM, FAC = (ST[:, 4 * i:4 * i + 4].rearrange("p (j q) -> p j q", j=2) for i in range(4))
        RB = sb("RB", [P, 3, 36])
        LG = sb("LG", [P, 2, 36])
        R1, R2, R3, R4, R5 = (sb(f"R{i}", [P, 2, 32]) for i in range(1, 6))
        RV = sb("RV", [P, 12, 2])
        MASK = sb("MASK", [P, 2, 8])
        COMBL = sb("COMBL", [P, 2, 8])
        POS = sb("POS", [P, 2, 8])
        IPOS = sb("IPOS", [P, 2, W2 + 1])
        IWT = sb("IWT", [P, 2, W2 + 1])
        FIRST = sb("FIRST", [P, W2], I32)
        ITEMS = sb("ITEMS", [P, 1], I32)
        CTOK = sb("CTOK", [P, 2, 32])
        PB = sb("PB", [8, 6])
        PRE = sb("PRE", [8, 10, T])
        MCOL = sb("MCOL", [P, 2, 2, 4])
        H1 = sb("H1", [P, 2, 2, 31])
        H1G = sb("H1G", [P, 2, 2, 30])
        CMPZ = SM
        KCMP = sb("KCMP", [P, 16])
        VCMP = sb("VCMP", [16, 2, 64])
        W2D = sb("W2D", [P, 2, 2, P])
        LNM = sb("LNM", [P, 2, T])
        PSB = [ctx.enter_context(nc.psum_tensor(f"B{i}", [P, 512], F32)) for i in range(8)]

        OBANK = [PSB[7], PSB[3]]

        def con(name, n=None, rows=P):
            a = CAT[name]
            return CON[0:rows, a:a + (n or dict(CONSTS)[name])]

        def col(name, i=0):
            return COLS[:, COL[name] + i:COL[name] + i + 1]

        ident = con("ident")

        def two(ap):
            return ap.rearrange("p (s t) -> p s t", s=2)

        def over2(ap):
            return ap.unsqueeze(1).to_broadcast([P, 2, T])

        causal = [con("causal")[:, 0:P], con("causal")[:, P:3 * P]]
        nomask = [con("zero"), con("zero")]

        def job(**kw):
            j = dict(kind="std", scale=0.125, mask=causal, keys=[128, 256], tr=True, part=0, dv=64,
                     rows=[128, 128], first=True, last=True, gate=None)
            j.update(kw)
            return j

        def diff_jobs():
            out = []
            for h in range(8):
                for c in range(2):
                    a = slice(64 * c, 64 * c + 64)
                    out.append(job(kind=f"diff{c}", q=Q[a, h, :], k=K[a, h, :], tr=c == 1, dv=128,
                                   v=[V[:, kt, 128 * h:128 * h + 128] for kt in range(2)], out=h,
                                   close=True))
            return out

        def nsa_jobs():
            out = []
            for c in range(8):
                for g in range(2):
                    h = 8 * g + c
                    a = slice(64 * g, 64 * g + 64)
                    for b in range(3):
                        kw = dict(kind="nsa", q=Q[a, c, :], part=64 * g, out=c, first=b == 0,
                                  last=b == 2, gate=3 * h + b, close=g == 1 and b == 2)
                        if b == 0:
                            kw.update(kind="cmp", k=KCMP[a, 0:15], keys=[15, 15], rows=[15],
                                      mask=[con("cmp_mask")[:, 0:15], con("cmp_mask")[:, 16:31]],
                                      v=[VCMP[0:15, g, :]])
                        else:
                            kw.update(k=K[a, 2 + 2 * (b - 1), :],
                                      v=[KVT[:, b - 1, kt, 64 * g:64 * g + 64] for kt in range(2)])
                        out.append(job(**kw))
            return out

        def ml_jobs():
            out = []
            for h in range(4):
                a = slice(64 * (h % 2), 64 * (h % 2) + 64)
                out.append(job(kind="ml", h=h, q=Q[a, h // 2, :], k=K[a, h // 2, :], part=64 * (h % 2),
                               v=[V[:, kt, 64 * h:64 * h + 64] for kt in range(2)], out=h // 2,
                               close=h % 2 == 1))
            return out

        def fox_jobs():
            out = []
            for h in range(8):
                a = slice(64 * (h % 2), 64 * (h % 2) + 64)
                out.append(job(kind="fox", h=h, q=Q[a, 4 + h // 2, :], k=K[a, 4 + h // 2, :],
                               part=64 * (h % 2), out=4 + h // 2, close=h % 2 == 1,
                               v=[V[:, kt, 512 + 64 * h:576 + 64 * h] for kt in range(2)]))
            return out

        def x_jobs():
            return [job(q=Q[:, h, :], k=K[:, h, :], mask=nomask, keys=[256, 256], dv=128,
                        scale=128 ** -0.5, v=[V[:, kt, 128 * h:128 * h + 128] for kt in range(2)],
                        out=h, close=True) for h in range(4)]

        def n_tr(jobs, j):
            return sum(1 for x in jobs[:j + 1] if x["tr"])

        def n_closed(jobs, j):
            return sum(1 for x in jobs[:j + 1] if x["tr"] and x["close"])

        STAGES = [("a0", diff_jobs()), ("a1", nsa_jobs()), ("mix0", ml_jobs() + fox_jobs()), ("xt0", x_jobs()),
                  ("mix1", ml_jobs() + fox_jobs()), ("xt1", x_jobs())]
        JOBS = dict(STAGES)
        BEFORE, so_far = {}, (0, 0, 0)
        for name, jobs in STAGES:
            BEFORE[name] = so_far
            so_far = (so_far[0] + len(jobs), so_far[1] + n_tr(jobs, len(jobs)), so_far[2] + n_closed(jobs, len(jobs)))

        def outputs_of(tag, n):
            return BEFORE[tag][2] + n

        def full(j, kt, qt):
            return j["keys"][qt] > 128 * kt

        def rope_pairs(layer):
            if layer == 0:
                return ([(Q[:, 2 * i:2 * i + 2, :], emptied("act", LIN0["diff_q"] + i)) for i in range(4)]
                        + [(K[:, 2 * i:2 * i + 2, :], emptied("act", LIN0["diff_k"] + i)) for i in range(4)])
            return ([(K[:, 2 * i:2 * i + 2, :], emptied("act", LIN0["nsa_kv"] + i)) for i in (1, 2)]
                    + [(Q[:, 2 * i:2 * i + 2, :], emptied("act", LIN0["nsa_q"] + i)) for i in range(4)])

        def mods(layer, part, c=None):
            a = layer * 48 + part * KC
            return MODS[:, a:a + KC] if c is None else MODS[:, a + c:a + c + 1]

        def cols8(name, l=0):
            return COLS[:, COL[name] + l * KC:COL[name] + l * KC + KC]

        NORMS = {"n0": (X, H, AG[:, 0, :], mods(0, 0)), "m0": (X, H, AG[:, 1, :], mods(0, 3)),
                 "n1": (X, H, AG[:, 2, :], mods(1, 0)), "m1": (X, H, AG[:, 3, :], mods(1, 3)),
                 "f1": (X, X, cols8("final_g"), None), "y": (X, H, cols8("norm_final"), None),
                 "d0": (X, H, cols8("norm_ffn", 0), None), "m2": (X, H, cols8("norm_ffn", 1), None)}
        for l in range(2):
            NORMS[f"x{l}"] = (X, H, cols8("norm_mix", l), None)
            NORMS[f"xa{l}"] = (X, H, cols8("norm_x", l), None)
            NORMS[f"mem{l}"] = (MEM, O, cols8("norm_mem", l), None)
        ORDER = ["n0", "m0", "n1", "m1", "f1", "x0", "mem0", "xa0", "d0", "x1", "mem1", "xa1", "m2", "y"]

        def nth(tag):
            return ORDER.index(tag) + 1

        GROUPED = {"g0": 0, "gm0": 4, "gm1": 5}

        def shifted(tag):
            return KC * sum(1 for n in ORDER[:nth(tag) - 1] if NORMS[n][3] is not None)

        SQF = SQ[:, :, :].rearrange("p c t -> p (c t)")
        RAW = SQF[:, 0:4 * 260].rearrange("p (c t) -> p c t", c=4)
        CPAD = SQF[:, 1040:1040 + 2 * 286].rearrange("p (c t) -> p c t", c=2)

        block = ctx.enter_context(nc.Block())

        @block.sync
        def _(sp):
            sp.dma_start(CON[:, :], t["consts"]).then_inc(S("con_in"), 16)
            for i in range(4):
                n = sum(k for _, k in ROW_TILES[i])
                sp.dma_start(SQ[0:n, i, 0:P], t[f"rows{i}"]).then_inc(S("rows_in"), 16)
            sp.dma_start(SMW[:, :], t["small"]).then_inc(S("small_in"), 16)
            sp.dma_start(LAMR, t["lam"].to_broadcast([P, 256])).then_inc(S("small_in"), 16)
            sp.dma_start(SM[:, 0, 0, :].bitcast(I32), t["pos"].to_broadcast([P, T])).then_inc(S("small_in"), 16)
            sp.dma_start(RB[:, :, :].rearrange("p a b -> p (a b)"), t["route_b"].to_broadcast([P, 108])).then_inc(S("small_in"), 16)
            sp.dma_start(PB[:, :], t["pre_b"]).then_inc(S("small_in"), 16)
            sp.dma_start(W2D[:, :, :, :].rearrange("p a b c -> p (a b c)"), t["cmp_w2"]).then_inc(S("small_in"), 16)
            sp.dma_start(BIG[:, 16:24, :].rearrange("p (s c) t -> p s (c t)", s=2),
                         t["x"].rearrange("(s p) d -> p s d", p=P)).then_inc(S("x_in"), 16)
            sp.dma_start(BIG[:, 24:32, :].rearrange("p (s c) t -> p s (c t)", s=2),
                         t["mem"].rearrange("(s p) d -> p s d", p=P)).then_inc(S("x_in"), 16)

            def load_a(n):
                if n >= RING_A:
                    sp.wait_ge(S("a_used"), n - RING_A + 1)
                if n in XO_AT:
                    sp.dma_start(WA[n % RING_A][:, 0:1024], t["xo"][XO_AT[n]]).then_inc(
                        S(f"a_in{n % RING_A}"), 16)
                else:
                    sp.dma_start(WA[n % RING_A][:, :], t["wa"][WA_AT[n]]).then_inc(
                        S(f"a_in{n % RING_A}"), 16)

            for r in range(2):
                sp.dma_start(WF[r][:, :, :].rearrange("p a n -> p (a n)"), t["ada"][r]).then_inc(
                    S(f"ada_in{r}"), 16)
            with sp.Fori(1, ADA_N // 2) as i:
                for r in range(2):
                    sp.wait_ge(S("ada_cols"), (i - 1) * 2 + (r + 1))
                    sp.dma_start(WF[r][:, :, :].rearrange("p a n -> p (a n)"),
                                 t["ada"][bass.ds(i * 2 + r, 1)].rearrange("a p n -> p (a n)")
                                 ).then_inc(S(f"ada_in{r}"), 16)

            def load_group(name):
                for i in range(NTILES[name]):
                    load_a(TILE0[name] + i)

            def load_ffn(tag, src, n, before):
                if before:
                    sp.wait_ge(S(before[0]), before[1])
                for c in range(min(RING_F, n)):
                    sp.dma_start(WF[c][:, :, :].rearrange("p a n -> p (a n)"), src[c]).then_inc(
                        S(f"f_in_{tag}{c}"), 16)
                rounds = n // RING_F
                with sp.Fori(1, rounds) as i:
                    for j in range(RING_F):
                        sp.wait_ge(S(f"f_used_{tag}"), (i - 1) * RING_F + j + 1)
                        sp.dma_start(WF[j][:, :, :].rearrange("p a n -> p (a n)"),
                                     src[bass.ds(i * RING_F + j, 1)].rearrange("a p n -> p (a n)")
                                     ).then_inc(S(f"f_in_{tag}{j}"), 16)
                for c in range(rounds * RING_F, n):
                    sp.wait_ge(S(f"f_used_{tag}"), c - RING_F + 1)
                    sp.dma_start(WF[c % RING_F][:, :, :].rearrange("p a n -> p (a n)"),
                                 src[c]).then_inc(S(f"f_in_{tag}{c % RING_F}"), 16)

            def load_items(tag, src, before):
                sets, n, _ = MOE[tag]
                if before:
                    sp.wait_ge(S(before[0]), before[1])

                def load(c, chunk):
                    sp.dma_start(WF[c % RING_F][:, :, :].rearrange("p a n -> p (a n)"), chunk).then_inc(
                        S(f"f_in_{tag}{c % RING_F}"), 16)

                for c in range(n):
                    if c >= RING_F:
                        sp.wait_ge(S(f"f_used_{tag}"), c - RING_F + 1)
                    load(c, src[c])
                sp.wait_ge(S("plan"), NTH[tag] + 1)
                items = sp.value_load(ITEMS[0:1, 0:1], min_val=sets, max_val=W1 if n == 8 else W2)
                with sp.Fori(1, items) as w:
                    first = sp.value_load(FIRST[0:1, bass.ds(w, 1)], min_val=0, max_val=(sets - 1) * n)
                    for c in range(n):
                        if c >= RING_F:
                            sp.wait_ge(S(f"f_used_{tag}"), w * n + (c - RING_F + 1))
                        else:
                            last = max(k for k in range(n) if k % RING_F == c)
                            sp.wait_ge(S(f"f_used_{tag}"), (w - 1) * n + (last + 1))
                        load(c, src[bass.ds(first + c, 1)].rearrange("a p n -> p (a n)"))

            for name in ("diff_q", "diff_k", "diff_v", "diff_o"):
                load_group(name)
            load_items("m0", t["wf0"], ("ada_cols", ADA_N))
            for name in ("nsa_kv", "nsa_q", "cmp", "nsa_o"):
                load_group(name)
            load_items("m1", t["wf1"], ("moe_done", 1))
            for name in ("mix_in0", "mix_o0", "x_q0", "x_k0", "x_v0", "x_o0"):
                load_group(name)
            load_ffn("d0", t["wf2"], M2, ("moe_done", 2))
            for name in ("mix_in1", "mix_o1", "x_q1", "x_k1", "x_v1", "x_o1"):
                load_group(name)
            load_items("m2", t["wf3"], ("f_used_d0", M2))
            sp.wait_ge(S("y_out"), 4)
            sp.dma_start(t["out"].rearrange("(s p) d -> p s d", p=P),
                         BIG[:, 0:8, :].rearrange("p (s c) t -> p s (c t)", s=2)).then_inc(S("out_done"), 16)
            sp.wait_ge(S("out_done"), 16)

        @block.tensor
        def _(pe):
            def mm(out, lhsT, rhs, start, stop, **kw):
                return nc.tensor.matmul(out, lhsT, rhs, start=start, stop=stop, **kw)

            pe.wait_ge(S("con_in"), 16)
            pe.wait_ge(S("rows_in"), 64)
            for i in range(4):
                n = sum(k for _, k in ROW_TILES[i])
                last = nc.tensor.transpose(PSB[3][:, i * P:i * P + n], SQ[0:n, i, 0:P], ident[0:n, 0:n])
            last.then_inc(S("cols_mm"), 1)
            pe.wait_ge(S("x_in"), 32)
            for r in range(8):
                if r >= 4:
                    pe.wait_ge(S("x_cp"), r - 3)
                src = V if r < 4 else OTOK
                for c in range(2):
                    for s in range(2):
                        cc = 2 * (r % 4) + c
                        last = nc.tensor.transpose(PSB[4 + r % 4][:, c * T + s * P:c * T + s * P + P],
                                                   src[:, s, cc * P:cc * P + P], ident)
                last.then_inc(S("x_tr"), 1)
            pe.wait_ge(S("cact"), 1)
            with pe.Fori(0, ADA_N // 2) as i:
                for r in range(2):
                    pe.wait_ge(S(f"ada_in{r}"), i * 16 + 16)
                    w = WF[r][:, 2, :].rearrange("p (k n) -> p k n", k=KC)
                    for s in range(2):
                        for k in range(KC):
                            mm(PSB[1 + r][:, 4 + s:5 + s], w[:, k, s * P:s * P + P],
                               CACT[:, k:k + 1], k == 0, k == KC - 1)
                    pe.wait_ge(S("folds"), i * (4 * KC) + 2 * KC * (r + 1))
                    for j in range(2):
                        for s in range(2):
                            last = mm(PSB[1 + r][:, 2 * j + s:2 * j + s + 1],
                                      FOLD[:, r, j, s * P:s * P + P], con("ones")[:, 0:1], True, True)
                    last.then_inc(S("ada_cols"), 1)
                    pe.wait_ge(S("mods"), i * 2 + (r + 1))
            pe.wait_ge(S("mods"), ADA_N + 1)

            def tile(name, i, src, tokens=False, nk=KC, fresh=None):
                n, q = TILE0[name] + i, LIN0[name] + i
                pe.wait_ge(S(f"a_in{n % RING_A}"), 16 * (n // RING_A + 1))
                if q >= 2:
                    pe.wait_ge(S(f"lin_{OWNER[q - 2]}"), emptied(OWNER[q - 2], q - 2))
                w = WA[n % RING_A][:, 0:nk * NTILE].rearrange("p (k n) -> p k n", k=nk)
                for s in range(2):
                    for k in range(nk):
                        if fresh and s == 0:
                            pe.wait_ge(S("normed"), KC * (nth(fresh) - 1) + k + 1)
                        o = PSB[q % 2][:, s * T:s * T + T]
                        if tokens:
                            last = mm(o, src[:, k, s * P:s * P + P], w[:, k, :], k == 0, k == nk - 1)
                        else:
                            last = mm(o, w[:, k, s * P:s * P + P], src[:, k, :], k == 0, k == nk - 1)
                last.then_inc(S("a_used"), 1)

            def linear(name, src, tokens=False, nk=KC, fresh=None):
                for i in range(NTILES[name]):
                    tile(name, i, src, tokens, nk, fresh if i == 0 else None)

            def norm(tag):
                for k in range(KC):
                    if k % 2 == 0:
                        pe.wait_ge(S("squares"), 4 * (nth(tag) - 1) + k // 2 + 1)
                    last = mm(PSB[3][:, 0:T], con("mean_d"), SQ[:, k, :], k == 0, k == KC - 1)
                last.then_inc(S("mean_sq"), 1)

            def rope(tag, pairs, some):
                for r in some:
                    x, ready = pairs[r]
                    pe.wait_ge(S("lin_act"), ready)
                    if r >= 2:
                        pe.wait_ge(S(f"rope_use_{tag}"), r - 1)
                    mm(PSB[4 + r % 2][:, :], con("rope"), x.rearrange("p c t -> p (c t)"), True, True).then_inc(
                        S(f"rope_mm_{tag}"), 1)

            def attend(tag):
                jobs = JOBS[tag]
                j0, t0, o0 = BEFORE[tag]
                n = len(jobs)

                def scores(j):
                    x = jobs[j]
                    if j >= 2:
                        pe.wait_ge(S("weights" if jobs[j - 2]["kind"] == "ml" else "masked"), j0 + j - 1)
                    bank = PSB[4 + j % 2]
                    for qt in range(2):
                        kk = x["keys"][qt]
                        last = mm(bank[:, qt * T:qt * T + kk], x["q"][:, qt * P:qt * P + P],
                                  x["k"][:, 0:kk], True, x["kind"] != "fox")
                        if x["kind"] == "fox":
                            last = mm(bank[:, qt * T:qt * T + kk], con("sel", rows=8)[:, x["h"] * P:x["h"] * P + P],
                                      PRE[0:8, 9, 0:kk], False, True)
                    if x["kind"] == "ml":
                        if j >= 1:
                            pe.wait_ge(S("masked"), j0 + j)
                        last = mm(PSB[0][:, 0:T], con("sel", rows=4)[:, x["h"] * P:x["h"] * P + P],
                                  PRE[0:4, 4, :], True, True)
                    last.then_inc(S("scores"), 1)

                def turn(j):
                    x = jobs[j]
                    if not x["tr"]:
                        return
                    t_n = n_tr(jobs, j)
                    pe.wait_ge(S("weights"), j0 + j + 1)
                    if t_n > 2:
                        pe.wait_ge(S("turned_out"), t0 + t_n - 2)
                    bank = [PSB[6], PSB[2]][t_n % 2]
                    for kt, kr in enumerate(x["rows"]):
                        for qt in range(2):
                            if full(x, kt, qt):
                                last = nc.tensor.transpose(bank[0:kr, kt * T + qt * P:kt * T + qt * P + P],
                                                           PN[:, j % 2, qt, kt * P:kt * P + kr], ident)
                    last.then_inc(S("turned"), 1)

                def mix(j):
                    x = jobs[j]
                    if not x["tr"]:
                        return
                    t_n = n_tr(jobs, j)
                    pe.wait_ge(S("turned_out"), t0 + t_n)
                    g = n_closed(jobs, j - 1) if j else 0
                    if x["first"] and g >= 2:
                        pe.wait_ge(S("outputs"), o0 + g - 1)
                    for kt, kr in enumerate(x["rows"]):
                        q0 = 0 if full(x, kt, 0) else P
                        last = mm(OBANK[g % 2][x["part"]:x["part"] + x["dv"], q0:T],
                                  x["v"][kt], PT[0:kr, t_n % 2, kt, q0:T], x["first"] and kt == 0,
                                  x["last"] and kt == len(x["rows"]) - 1)
                    last.then_inc(S("mixed"), 1)

                scores(0)
                scores(1)
                for j in range(n):
                    if j + 2 < n:
                        scores(j + 2)
                    turn(j)
                    if j:
                        mix(j - 1)
                mix(n - 1)

            def group_mean(tag, matrix, n):
                for r in range(n):
                    pe.wait_ge(S("group_sq"), GROUPED[tag] + r + 1)
                    if r >= 1:
                        pe.wait_ge(S("group_rms"), 2 * (GROUPED[tag] + r) - 1)
                    mm(PSB[3][:, :], con(matrix), SQ[:, 2 * r:2 * r + 2, :].rearrange("p c t -> p (c t)"),
                       True, True).then_inc(S("group_mean"), 1)

            def route(tag, small):
                pe.wait_ge(S("normed"), KC * nth(tag))
                a, w = SAT[small]
                for s in range(2):
                    for k in range(KC):
                        last = mm(PSB[2][:, s * 64:s * 64 + w], H[:, k, s * P:s * P + P],
                                  SMW[:, a + k * w:a + k * w + w], k == 0, k == KC - 1)
                last.then_inc(S("rl"), 1)

            def moe(tag):
                sets, n, by_chunk = MOE[tag]
                for r in range(4):
                    for s in range(2):
                        for c in range(2):
                            last = nc.tensor.transpose(PSB[4 + r][:, s * T + c * P:s * T + c * P + P],
                                                       H[:, 2 * r + c, s * P:s * P + P], ident)
                    last.then_inc(S("htok_mm"), 1)
                pe.wait_ge(S("mask"), NTH[tag] + 1)
                mm(PSB[3][:, 0:sets], con("tri"), MASK[:, 0, 0:sets], True, True)
                mm(PSB[3][:, 8:8 + sets], con("ones"), MASK[:, 0, 0:sets], True, False)
                mm(PSB[3][:, 8:8 + sets], con("tri"), MASK[:, 1, 0:sets], False, True)
                mm(PSB[3][:, 16:16 + sets], con("ones"), MASK[:, 0, 0:sets], True, False)
                mm(PSB[3][:, 16:16 + sets], con("ones"), MASK[:, 1, 0:sets], False, True).then_inc(
                    S("count"), 1)
                pe.wait_ge(S("htok"), 4 * NTH[tag] + 4)
                pe.wait_ge(S("plan"), NTH[tag] + 1)
                items = pe.value_load(ITEMS[0:1, 0:1], min_val=sets, max_val=W1 if n == 8 else W2)

                def gate_up(w, c):
                    uses = len(range(c % RING_F, n, RING_F))
                    pe.wait_ge(S(f"f_in_{tag}{c % RING_F}"), (w * uses + (c // RING_F + 1)) * 16)
                    if c >= 2:
                        pe.wait_ge(S(f"up_{tag}"), w * n + (c - 1))
                    for half in range(2):
                        ww = WF[c % RING_F][:, half, :].rearrange("p (k n) -> p k n", k=KC)
                        for s in range(2):
                            for k in range(KC):
                                last = mm(PSB[2 * (c % 2) + half][:, s * CAP:s * CAP + CAP],
                                          ww[:, k, s * P:s * P + P], HG[:, k, :], k == 0, k == KC - 1)
                    last.then_inc(S(f"gu_{tag}"), 1)

                def gather(w):
                    pe.wait_ge(S(f"pick_{tag}"), w * 2 + 1)
                    for b in range(2):
                        for k in range(4):
                            for s in range(2):
                                last = mm(PSB[6 + b][:, k * CAP:k * CAP + CAP],
                                          HTOK[:, s, (4 * b + k) * P:(4 * b + k) * P + P], PICK[:, s, :],
                                          s == 0, s == 1)
                    last.then_inc(S(f"gath_{tag}"), 1)

                gather(0)
                with pe.Fori(0, items) as w:
                    pe.wait_ge(S(f"pick_{tag}"), w * 2 + 2)
                    for s in range(2):
                        last = nc.tensor.transpose(PSB[3][0:CAP, s * P:s * P + P],
                                                   (PICK if by_chunk else PICKW)[:, s, :], ident)
                    last.then_inc(S(f"put_mm_{tag}"), 1)
                    pe.wait_ge(S(f"item_in_{tag}"), w * 2 + 1)
                    gate_up(w, 0)
                    pe.wait_ge(S(f"added_{tag}"), w + 1)
                    if by_chunk:
                        for b in range(2):
                            for s in range(2):
                                last = mm(PSB[4 + b][:, 0:4 * CAP], con("ones"),
                                          PICKE[:, s, 4 * b:4 * b + 4, :].rearrange("p e n -> p (e n)"),
                                          s == 0, s == 1)
                        last.then_inc(S(f"cbg_mm_{tag}"), 1)
                    pe.wait_ge(S(f"item_in_{tag}"), w * 2 + 2)
                    for c in range(n):
                        if c + 1 < n:
                            gate_up(w, c + 1)
                        else:
                            gather(w + 1)
                        if c == 0 and by_chunk:
                            pe.wait_ge(S(f"cbg_{tag}"), w + 1)
                        pe.wait_ge(S(f"a3_{tag}" if by_chunk else f"up_{tag}"), w * n + (c + 1))
                        wd = WF[c % RING_F][:, 2, :].rearrange("p (s n) -> p s n", s=2)
                        for k in range(KC):
                            for s in range(2):
                                last = mm(PSB[4 + k // 4][:, (k % 4) * CAP:(k % 4) * CAP + CAP],
                                          wd[:, s, k * P:k * P + P],
                                          (A3 if by_chunk else A2)[:, c % 2, s, 0:CAP],
                                          c == 0 and k % 4 == 0 and s == 0, False, skip_group_check=True)
                        last.then_inc(S(f"f_used_{tag}"), 1)
                    pe.wait_ge(S(f"yds_{tag}"), w + 1)
                    for k in range(KC):
                        last = nc.tensor.transpose(PSB[6 + k // 4][0:CAP, (k % 4) * P:(k % 4) * P + P],
                                                   YDS[:, k, :], ident)
                    last.then_inc(S(f"ytk_mm_{tag}"), 1)
                    pe.wait_ge(S(f"ytk_{tag}"), w + 1)
                    for k in range(KC):
                        last = mm(PSB[4 + k // 2][:, (k % 2) * T:(k % 2) * T + T],
                                  YTK[0:CAP, k * P:k * P + P], PUT[0:CAP, :], True, True)
                    last.then_inc(S(f"spread_{tag}"), 1)

            def ffn(tag, n):
                def products(slot, par):
                    w = WF[slot]
                    for half in range(2):
                        ww = w[:, half, :].rearrange("p (k n) -> p k n", k=KC)
                        bank = PSB[2 * par + half]
                        for s in range(2):
                            for k in range(KC):
                                last = mm(bank[:, s * T:s * T + T], ww[:, k, s * P:s * P + P],
                                          H[:, k, :], k == 0, k == KC - 1)
                    last.then_inc(S(f"gu_{tag}"), 1)

                def down(slot, par):
                    w = WF[slot][:, 2, :].rearrange("p (s n) -> p s n", s=2)
                    for dch in range(KC):
                        for s in range(2):
                            last = mm(PSB[4 + dch // 2][:, (dch % 2) * T:(dch % 2) * T + T],
                                      w[:, s, dch * P:dch * P + P], A2[:, par, s, :],
                                      False, False, skip_group_check=True)
                    last.then_inc(S(f"f_used_{tag}"), 1)

                zero = con("zero")
                for b in range(4):
                    for s in range(2):
                        last = mm(PSB[4 + b][:, s * T:s * T + T], zero[:, 0:P], zero, s == 0, False,
                                  skip_group_check=True)

                def step(c, j, last):
                    if not last:
                        pe.wait_ge(S(f"f_in_{tag}{(j + 1) % RING_F}"),
                                   (c[0] + (j + 1) // RING_F) * 16 + 16)
                        if j >= 1:
                            pe.wait_ge(S(f"up_{tag}"), c[1])
                        products((j + 1) % RING_F, (j + 1) % 2)
                    pe.wait_ge(S(f"up_{tag}"), c[1] + 1)
                    down(j % RING_F, j % 2)

                pe.wait_ge(S("normed"), KC * nth(tag))
                pe.wait_ge(S(f"f_in_{tag}0"), 16)
                products(0, 0)
                step((0, 0), 0, False)
                body = 2 * RING_F
                loops = (n - 2) // body
                with pe.Fori(0, loops) as i:
                    for j in range(1, body + 1):
                        step((i * (body // RING_F), i * body + j), j, False)
                for c in range(1 + loops * body, n):
                    base = loops * body
                    step((base // RING_F, c), c - base, c == n - 1)

            def cmp_mlps():
                pe.wait_ge(S("cmpz"), 2)
                for kv in range(2):
                    for half in range(2):
                        n = TILE0["cmp"] + 2 * kv + half
                        pe.wait_ge(S(f"a_in{n % RING_A}"), 16 * (n // RING_A + 1))
                    for s in range(2):
                        for m in range(16):
                            n = TILE0["cmp"] + 2 * kv + m // 8
                            w = WA[n % RING_A][:, :].rearrange("p (k n) -> p k n", k=KC)
                            last = mm(PSB[6][:, (2 * kv + s) * 32:(2 * kv + s) * 32 + 31],
                                      w[:, m % 8, s * P:s * P + P],
                                      CMPZ[:, kv].rearrange("p a t -> p (a t)")[:, 0:496].rearrange(
                                          "p (m n) -> p m n", m=16)[:, m, :], m == 0, m == 15)
                            if s == 1 and m in (7, 15):
                                last.then_inc(S("a_used"), 1)
                pe.wait_ge(S("h1g"), 1)
                for s in range(2):
                    last = mm(PSB[3][:, 0:30], W2D[:, 0, s, :], H1G[:, 0, s, :], s == 0, s == 1)
                for g in range(2):
                    for s in range(2):
                        last = mm(PSB[3][0:15, 64 + 64 * g:128 + 64 * g], H1G[:, 1, s, 15 * g:15 * g + 15],
                                  W2D[:, 1, s, 0:64], s == 0, s == 1)
                last.then_inc(S("cmp_out"), 1)

            norm("n0")
            linear("diff_q", H, fresh="n0")
            linear("diff_k", H)
            for i in range(4):
                tile("diff_v", i, H, tokens=True)
                rope("r0", rope_pairs(0), (2 * i, 2 * i + 1))
            pe.wait_ge(S("rope_use_r0"), 8)
            pe.wait_ge(S("lin_act"), emptied("act", LIN0["diff_v"] + 3))
            attend("a0")
            group_mean("g0", "mean_128", 4)
            pe.wait_ge(S("group_done"), 4)
            linear("diff_o", O)
            norm("m0")
            route("m0", "route0")
            moe("m0")
            norm("n1")
            linear("nsa_kv", H, fresh="n1")
            for i in range(4):
                tile("nsa_q", i, H)
                if i:
                    rope("r1", rope_pairs(1), (i - 1, ))
            a, w = SAT["gates"]
            for s in range(2):
                for k in range(KC):
                    last = mm(PSB[2][:, s * 64:s * 64 + w], H[:, k, s * P:s * P + P],
                              SMW[:, a + k * w:a + k * w + w], k == 0, k == KC - 1)
            last.then_inc(S("gates_mm"), 1)
            rope("r1", rope_pairs(1), (3, 4, 5))
            cmp_mlps()
            pe.wait_ge(S("rope_use_r1"), 6)
            for b in range(2):
                for kt in range(2):
                    last = nc.tensor.transpose(PSB[7][:, (2 * b + kt) * P:(2 * b + kt) * P + P],
                                               K[:, 3 + 2 * b, kt * P:kt * P + P], ident)
            last.then_inc(S("kvt_mm"), 1)
            pe.wait_ge(S("cmp_kv"), 2)
            pe.wait_ge(S("kvt"), 1)
            attend("a1")
            pe.wait_ge(S("outputs"), outputs_of("a1", 8))
            linear("nsa_o", O)
            norm("m1")
            route("m1", "route1")
            moe("m1")
            norm("f1")
            for l in range(2):
                norm(f"x{l}")
                for i in range(12):
                    tile(f"mix_in{l}", i, H, tokens=i in (2, 10, 11), fresh=None if i else f"x{l}")
                a, w = SAT[f"pre{l}"]
                for r, (c0, c1) in enumerate(((0, 4), (4, 8), (8, 16))):
                    o = [PSB[2][0:4, 0:T], PSB[2][0:4, T:2 * T], PSB[3][0:8, 0:T]][r]
                    for k in range(KC):
                        last = mm(o, SMW[:, a + k * w + c0:a + k * w + c1], H[:, k, :], k == 0, k == KC - 1)
                last.then_inc(S("pre_mm"), 1)
                pe.wait_ge(S("pre_rows"), l + 1)
                for r in range(2):
                    for s in range(2):
                        last = nc.tensor.transpose(PSB[6][:, (2 * r + s) * 4:(2 * r + s) * 4 + 4],
                                                   PRE[0:4, 5 + r, s * P:s * P + P], ident[0:4, 0:4])
                last.then_inc(S("mcol_mm"), 1)
                pe.wait_ge(S("mcol"), 2 * l + 2)
                pe.wait_ge(S("qk_ml"), 4 * l + 4)
                pe.wait_ge(S("lin_act"), emptied("act", LIN0[f"mix_in{l}"] + 11))
                attend(f"mix{l}")
                pe.wait_ge(S("outputs"), outputs_of(f"mix{l}", 6))
                group_mean(f"gm{l}", "mean_64", 1)
                pe.wait_ge(S("conv"), l + 1)
                for c in range(2):
                    last = mm(PSB[6][:, 0:T], con("mean_256"), LNM[:, c, :], c == 0, c == 1)
                last.then_inc(S("ln_mm"), 1)
                pe.wait_ge(S("ln_sq"), l + 1)
                for c in range(2):
                    last = mm(PSB[2][:, 0:T], con("mean_256"), SQ[:, 6 + c, :], c == 0, c == 1)
                last.then_inc(S("ln_mm"), 1)
                pe.wait_ge(S("cat"), 2 * l + 2)
                linear(f"mix_o{l}", O)
                norm(f"mem{l}")
                norm(f"xa{l}")
                linear(f"x_q{l}", H, fresh=f"xa{l}")
                pe.wait_ge(S("normed"), KC * nth(f"mem{l}"))
                linear(f"x_k{l}", O)
                linear(f"x_v{l}", O, tokens=True)
                pe.wait_ge(S("lin_act"), emptied("act", LIN0[f"x_v{l}"] + 1))
                attend(f"xt{l}")
                pe.wait_ge(S("outputs"), outputs_of(f"xt{l}", 4))
                linear(f"x_o{l}", O, nk=4)
                tag = "d0" if l == 0 else "m2"
                norm(tag)
                if l == 0:
                    ffn(tag, M2)
                else:
                    route(tag, "route2")
                    moe(tag)
            norm("y")
            pe.wait_ge(S("normed"), KC * nth("y"))
            for r in range(4):
                for s in range(2):
                    for c in range(2):
                        last = nc.tensor.transpose(PSB[4 + r][:, s * T + c * P:s * T + c * P + P],
                                                   H[:, 2 * r + c, s * P:s * P + P], ident)
                last.then_inc(S("y_tr"), 1)

        @block.scalar
        def _(act):
            fn = nc.scalar.activation

            def lin(name, i, out, func=ACT.Copy):
                act.wait_ge(S("a_used"), TILE0[name] + i + 1)
                fn(out, two(PSB[(LIN0[name] + i) % 2][:, :]), func).then_inc(S("lin_act"), 1)

            def inverse_root(out, mean, name, count):
                fn(out, mean, ACT.Ln, bias=con("eps")).then_inc(S(name), 1)
                act.wait_ge(S(name), 2 * count - 1)
                fn(out, out, ACT.Exp, scale=-0.5).then_inc(S(name), 1)

            def norm(tag):
                _, dst, _, shift = NORMS[tag]
                act.wait_ge(S("mean_sq"), nth(tag))
                inverse_root(RS[:, 0, :], PSB[3][:, 0:T], "rms", nth(tag))
                if shift is not None:
                    for c in range(KC):
                        act.wait_ge(S("scaled"), shifted(tag) + c + 1)
                        fn(dst[:, c, :], SQ[:, c, :], ACT.Identity, bias=shift[:, c:c + 1]).then_inc(
                            S("normed"), 1)

            def attend(tag):
                jobs = JOBS[tag]
                j0, t0, o0 = BEFORE[tag]
                def exps(j):
                    x = jobs[j]
                    act.wait_ge(S("masked"), j0 + j + 1)
                    if j >= 2:
                        act.wait_ge(S("weights"), j0 + j - 1)
                    for qt in range(2):
                        kk = x["keys"][qt]
                        if x["kind"] == "ml":
                            last = fn(PR[:, j % 2, qt, 0:kk], SM[:, j % 2, qt, 0:kk], ACT.Exp,
                                      bias=MCOL[:, 0, qt, x["h"]:x["h"] + 1])
                        else:
                            last = fn(PR[:, j % 2, qt, 0:kk], SM[:, j % 2, qt, 0:kk], ACT.Exp,
                                      bias=NM[:, j % 2, qt:qt + 1], accum_out=SUM[:, j % 2, qt:qt + 1])
                    last.then_inc(S("exps"), 1)

                def transposed(j):
                    x = jobs[j]
                    if not x["tr"]:
                        return
                    t_n = n_tr(jobs, j)
                    act.wait_ge(S("turned"), t0 + t_n)
                    if t_n > 2:
                        act.wait_ge(S("mixed"), t0 + t_n - 2)
                    bank = [PSB[6], PSB[2]][t_n % 2]
                    for kt, kr in enumerate(x["rows"]):
                        q0 = 0 if full(x, kt, 0) else P
                        last = fn(PT[0:kr, t_n % 2, kt, q0:T], bank[0:kr, kt * T + q0:kt * T + T], ACT.Copy)
                    last.then_inc(S("turned_out"), 1)

                def outputs(j):
                    x = jobs[j]
                    if not (x["tr"] and x["close"]):
                        return
                    act.wait_ge(S("mixed"), t0 + n_tr(jobs, j))
                    g = n_closed(jobs, j) - 1
                    fn(O[:, x["out"], :], OBANK[g % 2][:, 0:T], ACT.Copy).then_inc(S("outputs"), 1)

                exps(0)
                for j in range(len(jobs)):
                    if j + 1 < len(jobs):
                        exps(j + 1)
                    transposed(j)
                    if j:
                        outputs(j - 1)
                outputs(len(jobs) - 1)

            def group_mean(tag, n):
                for r in range(n):
                    act.wait_ge(S("group_mean"), GROUPED[tag] + r + 1)
                    if r >= 1:
                        act.wait_ge(S("group_done"), GROUPED[tag] + r)
                    inverse_root(RS[:, :, :], two(PSB[3][:, :]), "group_rms", GROUPED[tag] + r + 1)

            def route(tag):
                act.wait_ge(S("re"), NTH[tag] + 1)
                fn(RV[:, 6:8, :], RV[:, 4:6, :], ACT.Exp).then_inc(S("rx"), 1)
                if tag != "m2":
                    act.wait_ge(S("rg"), NTH[tag] + 1)
                    fn(R1[:, :, 0:4], R1[:, :, 0:4], ACT.Exp).then_inc(S("rx"), 1)

            def moe(tag):
                sets, n, by_chunk = MOE[tag]
                for r in range(4):
                    act.wait_ge(S("htok_mm"), 4 * NTH[tag] + r + 1)
                    fn(HTOK[:, :, r * T:(r + 1) * T], two(PSB[4 + r][:, :]), ACT.Copy).then_inc(
                        S("htok"), 1)
                act.wait_ge(S("plan"), NTH[tag] + 1)
                items = act.value_load(ITEMS[0:1, 0:1], min_val=sets, max_val=W1 if n == 8 else W2)
                def gathered(w):
                    act.wait_ge(S(f"gath_{tag}"), w + 1)
                    for b in range(2):
                        last = fn(HG[:, 4 * b:4 * b + 4, :].rearrange("p k n -> p (k n)"),
                                  PSB[6 + b][:, 0:4 * CAP], ACT.Copy)
                    last.then_inc(S(f"item_in_{tag}"), 1)

                gathered(0)
                with act.Fori(0, items) as w:
                    act.wait_ge(S(f"put_mm_{tag}"), w + 1)
                    fn(PUT[0:CAP, :], PSB[3][0:CAP, 0:T], ACT.Copy).then_inc(S(f"item_in_{tag}"), 1)
                    for c in range(n):
                        act.wait_ge(S(f"gu_{tag}"), w * n + (c + 1))
                        if c >= 2:
                            act.wait_ge(S(f"up_{tag}"), w * n + (c - 1))
                        fn(A1[:, c % 2, :, 0:CAP], PSB[2 * (c % 2)][:, 0:2 * CAP].rearrange(
                            "p (s n) -> p s n", s=2), ACT.Silu).then_inc(S(f"silu_{tag}"), 1)
                    gathered(w + 1)
                    act.wait_ge(S(f"f_used_{tag}"), w * n + n)
                    for b in range(2):
                        last = fn(YDS[:, 4 * b:4 * b + 4, :].rearrange("p k n -> p (k n)"),
                                  PSB[4 + b][:, 0:4 * CAP], ACT.Copy)
                    last.then_inc(S(f"yds_{tag}"), 1)
                    act.wait_ge(S(f"ytk_mm_{tag}"), w + 1)
                    for b in range(2):
                        last = fn(YTK[0:CAP, b * 512:b * 512 + 512], PSB[6 + b][0:CAP, :], ACT.Copy)
                    last.then_inc(S(f"ytk_{tag}"), 1)

            def ffn(tag, n):
                def silu(c, par, first=False):
                    act.wait_ge(S(f"gu_{tag}"), c + 1)
                    if not first:
                        act.wait_ge(S(f"up_{tag}"), c - 1)
                    fn(A1[:, par, :, :], two(PSB[2 * par][:, :]), ACT.Silu).then_inc(S(f"silu_{tag}"), 1)

                silu(0, 0, True)
                silu(1, 1, True)
                with act.Fori(0, (n - 2) // 2) as i:
                    for j in range(2):
                        silu(i * 2 + (2 + j), j)
                if n % 2:
                    silu(n - 1, (n - 1) % 2)

            act.wait_ge(S("con_in"), 16)
            act.wait_ge(S("cols_mm"), 1)
            for i in range(4):
                n = sum(k for _, k in ROW_TILES[i])
                last = fn(COLS[:, i * P:i * P + n], PSB[3][:, i * P:i * P + n], ACT.Copy)
            last.then_inc(S("cols"), 1)
            act.wait_ge(S("cols"), 1)
            fn(CACT[:, :], cols8("c"), ACT.Silu).then_inc(S("cact"), 1)
            for r in range(8):
                act.wait_ge(S("x_tr"), r + 1)
                dst = X if r < 4 else MEM
                fn(dst[:, 2 * (r % 4):2 * (r % 4) + 2, :], two(PSB[4 + r % 4][:, :]), ACT.Copy).then_inc(
                    S("x_cp"), 1)
            act.wait_ge(S("angle"), 2)
            fn(SIN[:, :], SM[:, 1, 0, :], ACT.Sin).then_inc(S("tables"), 1)
            fn(COS[:, :], SM[:, 0, 0, :], ACT.Sin, scale=-1.0, bias=con("halfpi")).then_inc(S("tables"), 1)
            act.wait_ge(S("lam_dot"), 1)
            fn(LAM[:, 2:4], LAM[:, 0:2], ACT.Exp).then_inc(S("lam_exp"), 1)

            norm("n0")
            for i in range(4):
                lin("diff_q", i, Q[:, 2 * i:2 * i + 2, :])
            for i in range(4):
                lin("diff_k", i, K[:, 2 * i:2 * i + 2, :])
            for i in range(4):
                lin("diff_v", i, V[:, :, i * NTILE:(i + 1) * NTILE])
            attend("a0")
            group_mean("g0", 4)
            norm("m0")
            route("m0")
            moe("m0")

            norm("n1")
            for i in range(3):
                lin("nsa_kv", i, K[:, 2 * i:2 * i + 2, :])
            for i in range(4):
                lin("nsa_q", i, Q[:, 2 * i:2 * i + 2, :])
            act.wait_ge(S("gates_mm"), 1)
            for s in range(2):
                last = fn(GATE[:, s, :], PSB[2][:, s * 64:s * 64 + 48], ACT.Sigmoid)
            last.then_inc(S("gates"), 1)
            act.wait_ge(S("h1b"), 1)
            for kv in range(2):
                for s in range(2):
                    last = fn(H1G[:, kv, s, :], PSB[6][:, (2 * kv + s) * 32:(2 * kv + s) * 32 + 30],
                              ACT.Gelu_apprx_tanh, bias=H1[:, kv, s, 0:1])
            last.then_inc(S("h1g"), 1)
            act.wait_ge(S("kvt_mm"), 1)
            fn(KVT[:, :, :, :].rearrange("p a b c -> p (a b c)"), PSB[7][:, :], ACT.Copy).then_inc(S("kvt"), 1)
            attend("a1")
            norm("m1")
            route("m1")
            moe("m1")
            norm("f1")

            for l in range(2):
                norm(f"x{l}")
                name = f"mix_in{l}"
                act.wait_ge(S("pads"), 2 * l + 2)
                lin(name, 0, RAW[:, 0:2, 3:259])
                lin(name, 1, RAW[:, 2:4, 3:259])
                lin(name, 2, V[:, :, 0:256])
                lin(name, 3, Q[:, 2:4, :], ACT.Sigmoid)
                lin(name, 4, K[:, 2:4, :])
                lin(name, 5, LNM[:, :, :], ACT.Sigmoid)
                for i in range(2):
                    lin(name, 6 + i, Q[:, 4 + 2 * i:6 + 2 * i, :])
                for i in range(2):
                    lin(name, 8 + i, K[:, 4 + 2 * i:6 + 2 * i, :])
                for i in range(2):
                    lin(name, 10 + i, V[:, :, 512 + i * NTILE:512 + (i + 1) * NTILE])
                act.wait_ge(S("pre_mm"), l + 1)
                act.wait_ge(S("pre_zero"), 1)
                for r, (rows, ps) in enumerate(((4, PSB[2][0:4, 0:T]), (4, PSB[2][0:4, T:2 * T]),
                                                (8, PSB[3][0:8, 0:T]))):
                    last = fn(PRE[0:rows, r, :], ps, ACT.Identity, bias=PB[0:rows, 3 * l + r:3 * l + r + 1])
                last.then_inc(S("pre"), 1)
                act.wait_ge(S("pre_abs"), l + 1)
                fn(PRE[:, 7:9, :], PRE[:, 7:9, :], ACT.Exp, scale=-1.0).then_inc(S("pre_ln"), 1)
                act.wait_ge(S("pre_ln"), 2 * l + 1)
                fn(PRE[:, 7:9, :], PRE[:, 7:9, :], ACT.Ln, bias=con("ones", 1, rows=8)).then_inc(S("pre_ln"), 1)
                act.wait_ge(S("conv_ml"), l + 1)
                fn(Q[:, 0:2, :], SM[:, 0, :, :], ACT.Silu)
                fn(K[:, 0:2, :], SM[:, 1, :, :], ACT.Silu).then_inc(S("qk_ml"), 4)
                act.wait_ge(S("mcol_mm"), l + 1)
                fn(MCOL[:, 0, :, :], PSB[6][:, 0:8].rearrange("p (s h) -> p s h", s=2), ACT.Copy,
                   scale=-1.0).then_inc(S("mcol"), 1)
                fn(MCOL[:, 1, :, :], PSB[6][:, 8:16].rearrange("p (s h) -> p s h", s=2), ACT.Exp,
                   scale=-1.0).then_inc(S("mcol"), 1)
                attend(f"mix{l}")
                group_mean(f"gm{l}", 1)
                act.wait_ge(S("ln_mm"), 2 * l + 2)
                inverse_root(RS[:, 0, :], PSB[2][:, 0:T], "ln_rs", l + 1)
                act.wait_ge(S("ln_out"), l + 1)
                for c in range(2):
                    last = fn(O[:, 2 + c, :], LNM[:, c, :], ACT.Silu, scale=col("ln_w", 2 * l + c),
                              bias=col("ln_b", 2 * l + c))
                last.then_inc(S("cat"), 1)
                norm(f"mem{l}")
                norm(f"xa{l}")
                for i in range(2):
                    lin(f"x_q{l}", i, Q[:, 2 * i:2 * i + 2, :])
                for i in range(2):
                    lin(f"x_k{l}", i, K[:, 2 * i:2 * i + 2, :])
                for i in range(2):
                    lin(f"x_v{l}", i, V[:, :, i * NTILE:(i + 1) * NTILE])
                attend(f"xt{l}")
                tag = "d0" if l == 0 else "m2"
                norm(tag)
                if l == 0:
                    ffn(tag, M2)
                else:
                    route(tag)
                    moe(tag)
            norm("y")
            for r in range(4):
                act.wait_ge(S("y_tr"), r + 1)
                fn(YTOK[:, :, r * T:(r + 1) * T], two(PSB[4 + r][:, :]), ACT.Copy).then_inc(S("y_out"), 1)

        @block.gpsimd
        def _(pool):
            pool_n = [0]

            def link(ins):
                pool_n[0] += 1
                ins.then_inc(S("pool_done"), 1)
                pool.wait_ge(S("pool_done"), pool_n[0])

            nc.gpsimd.memset(PRE[:, :, :], 0.0).then_inc(S("pre_zero"), 1)
            for l in range(2):
                pool.wait_ge(S("lin_act"), emptied("act", LIN0[f"mix_in{l}"] + 5))
                pool.wait_ge(S("cols"), 1)
                link(nc.gpsimd.tensor_tensor(CPAD[:, :, 30:286], K[:, 2:4, :], LNM[:, :, :], ALU.mult))
                pool.wait_ge(S("pads"), 2 * l + 2)
                for j in range(31):
                    taps = K[:, 2:4, :] if j else LNM[:, :, :]
                    for c in range(2):
                        w = col("conf_w", 62 * l + 2 * j + c)
                        if j == 0:
                            ins = nc.gpsimd.tensor_scalar(taps[:, c, :], CPAD[:, c, 0:T], w,
                                                          col("conf_b", 2 * l + c), ALU.mult, ALU.add)
                        else:
                            ins = nc.gpsimd.tensor_scalar(taps[:, c, :], CPAD[:, c, j:j + T], w, 0.0,
                                                          ALU.mult, ALU.add)
                    link(ins)
                    if j:
                        ins = nc.gpsimd.tensor_tensor(LNM[:, :, :], LNM[:, :, :], taps, ALU.add)
                        if j < 30:
                            link(ins)
                ins.then_inc(S("conv"), 1)

        @block.vector
        def _(dve):
            done = [0]
            v = nc.vector

            def link(ins):
                done[0] += 1
                ins.then_inc(S("dve_done"), 1)
                dve.wait_ge(S("dve_done"), done[0])

            def norm(tag):
                src, dst, gain, shift = NORMS[tag]
                for c in range(0, KC, 2):
                    v.tensor_tensor(SQ[:, c:c + 2, :], src[:, c:c + 2, :], src[:, c:c + 2, :],
                                    ALU.mult).then_inc(S("squares"), 1)
                dve.wait_ge(S("rms"), 2 * nth(tag))
                for c in range(KC):
                    ins = v.scalar_tensor_tensor(out=(dst if shift is None else SQ)[:, c, :], in0=src[:, c, :],
                                                 scalar=gain[:, c:c + 1], in1=RS[:, 0, :],
                                                 op0=ALU.mult, op1=ALU.mult)
                    ins.then_inc(S("normed" if shift is None else "scaled"), 1)
                if shift is None:
                    dve.wait_ge(S("normed"), KC * nth(tag))

            def rope(tag, pairs):
                for r, (x, _) in enumerate(pairs):
                    dve.wait_ge(S(f"rope_mm_{tag}"), r + 1)
                    v.tensor_tensor(PR[:, r % 2, :, :], two(PSB[4 + r % 2][:, :]), over2(SIN[:, :]), ALU.mult)
                    link(v.tensor_tensor(x, x, over2(COS[:, :]), ALU.mult))
                    v.tensor_tensor(x, x, PR[:, r % 2, :, :], ALU.add).then_inc(S(f"rope_use_{tag}"), 1)

            def attend(tag):
                jobs = JOBS[tag]
                j0, t0, o0 = BEFORE[tag]
                def front(j):
                    x = jobs[j]
                    dve.wait_ge(S("scores"), j0 + j + 1)
                    if j >= 2:
                        dve.wait_ge(S("exps"), j0 + j - 1)
                    bank = PSB[0] if x["kind"] == "ml" else PSB[4 + j % 2]
                    for qt in range(2):
                        kk = x["keys"][qt]
                        if x["kind"] == "ml":
                            ins = v.tensor_tensor(SM[:, j % 2, qt, 0:kk], bank[:, 0:kk], x["mask"][qt], ALU.add)
                        else:
                            ins = v.tensor_tensor_reduce(
                                out=SM[:, j % 2, qt, 0:kk], in0=bank[:, qt * T:qt * T + kk], in1=x["mask"][qt],
                                scale=x["scale"], scalar=-3e38, op0=ALU.add, op1=ALU.max,
                                accum_out=MX[:, j % 2, qt:qt + 1])
                    if x["kind"] != "ml":
                        link(ins)
                        ins = v.tensor_scalar(NM[:, j % 2, :], MX[:, j % 2, :], -1.0, None, ALU.mult)
                    ins.then_inc(S("masked"), 1)

                def back(j):
                    x = jobs[j]
                    dve.wait_ge(S("exps"), j0 + j + 1)
                    before = n_tr(jobs, j - 2) if j >= 2 else 0
                    if before:
                        dve.wait_ge(S("turned"), t0 + before)
                    f = FAC[:, j % 2, :]
                    if x["kind"] == "ml":
                        for qt in range(2):
                            kk = x["keys"][qt]
                            ins = v.tensor_tensor_reduce(
                                out=PN[:, j % 2, qt, 0:kk], in0=PSB[4 + j % 2][:, qt * T:qt * T + kk],
                                in1=PR[:, j % 2, qt, 0:kk], scale=x["scale"], scalar=0.0, op0=ALU.mult,
                                op1=ALU.add, accum_out=SUM[:, j % 2, qt:qt + 1])
                        link(ins)
                        link(v.scalar_tensor_tensor(out=f, in0=SUM[:, j % 2, :], scalar=-1.0,
                                                    in1=SUM[:, j % 2, :], op0=ALU.mult, op1=ALU.max))
                        link(v.tensor_tensor(f, f, MCOL[:, 1, :, x["h"]], ALU.max))
                        link(v.reciprocal(f, f))
                        src = PN
                    else:
                        link(v.reciprocal(f, SUM[:, j % 2, :]))
                        if x["kind"] == "diff1":
                            link(v.tensor_scalar(f, f, LAM[:, 4:5], None, ALU.mult))
                        if x["gate"] is not None:
                            link(v.tensor_tensor(f, f, GATE[:, :, x["gate"]], ALU.mult))
                        if x["kind"] == "cmp":
                            link(v.tensor_tensor(f, f, con("cmp_valid"), ALU.mult))
                        src = PR
                    for qt in range(2):
                        kk = x["keys"][qt]
                        if x["kind"] == "diff1":
                            ins = v.scalar_tensor_tensor(
                                out=PN[:, j % 2, qt, 0:kk], in0=PR[:, j % 2, qt, 0:kk], scalar=f[:, qt:qt + 1],
                                in1=PN[:, (j - 1) % 2, qt, 0:kk], op0=ALU.mult, op1=ALU.add)
                        else:
                            ins = v.tensor_scalar(PN[:, j % 2, qt, 0:kk], src[:, j % 2, qt, 0:kk],
                                                  f[:, qt:qt + 1], None, ALU.mult)
                    ins.then_inc(S("weights"), 1)
                    if x["kind"] == "diff0":
                        dve.wait_ge(S("weights"), j0 + j + 1)

                front(0)
                front(1)
                for j in range(len(jobs)):
                    back(j)
                    if j + 2 < len(jobs):
                        front(j + 2)

            def residual(name, i, gate=None):
                dve.wait_ge(S("a_used"), TILE0[name] + i + 1)
                bank = PSB[(LIN0[name] + i) % 2]
                if gate is None:
                    ins = v.tensor_tensor(X[:, 2 * i:2 * i + 2, :], two(bank[:, :]), X[:, 2 * i:2 * i + 2, :],
                                          ALU.add)
                else:
                    for s in range(2):
                        c = 2 * i + s
                        ins = v.scalar_tensor_tensor(out=X[:, c, :], in0=bank[:, s * T:s * T + T],
                                                     scalar=gate[:, c:c + 1], in1=X[:, c, :],
                                                     op0=ALU.mult, op1=ALU.add)
                ins.then_inc(S("lin_dve"), 1)
                dve.wait_ge(S("lin_dve"), emptied("dve", LIN0[name] + i))

            def group_squares(tag, n):
                for r in range(n):
                    v.tensor_tensor(SQ[:, 2 * r:2 * r + 2, :], O[:, 2 * r:2 * r + 2, :],
                                    O[:, 2 * r:2 * r + 2, :], ALU.mult).then_inc(S("group_sq"), 1)

            def first_max(x, mx, n, hot, tmp, low):
                b = mx.unsqueeze(2).to_broadcast([P, 2, n])
                link(v.tensor_tensor(tmp[:, :, 0:n], x, b, ALU.is_equal))
                link(v.scalar_tensor_tensor(out=tmp[:, :, 0:n], in0=tmp[:, :, 0:n], scalar=-1000.0,
                                            in1=con("iota", rows=P)[:, 0:n].unsqueeze(1).to_broadcast([P, 2, n]),
                                            op0=ALU.mult, op1=ALU.add))
                link(v.tensor_reduce(low, tmp[:, :, 0:n], AX.X, ALU.min))
                link(v.tensor_tensor(hot[:, :, 0:n], tmp[:, :, 0:n],
                                     low.unsqueeze(2).to_broadcast([P, 2, n]), ALU.is_equal))

            def route(tag, k, w):
                dve.wait_ge(S("rl"), NTH[tag] + 1)
                link(v.tensor_tensor(LG[:, :, 0:w], PSB[2][:, 0:128].rearrange("p (s n) -> p s n", s=2)[:, :, 0:w],
                                     RB[:, k:k + 1, 0:w].to_broadcast([P, 2, w]), ALU.add))
                ne = E2 if tag == "m2" else E1
                if tag == "m2":
                    x = LG[:, :, 0:E2]
                else:
                    g4 = LG[:, :, 0:4]
                    link(v.tensor_reduce(RV[:, 0, :], g4, AX.X, ALU.max))
                    first_max(g4, RV[:, 0, :], 4, R2, R3, RV[:, 1, :])
                    v.tensor_copy(MASK[:, :, 0:4], R2[:, :, 0:4]).then_inc(S("mask"), 1)
                    v.tensor_tensor(R1[:, :, 0:4], g4, RV[:, 0, :].unsqueeze(2).to_broadcast([P, 2, 4]),
                                    ALU.subtract).then_inc(S("rg"), 1)
                    link(v.tensor_scalar(R2[:, :, 0:4], R2[:, :, 0:4], 1e30, -1e30, ALU.mult, ALU.add))
                    for s in range(2):
                        ins = v.tensor_tensor(
                            R4[:, s, :].rearrange("p (g e) -> p g e", g=4),
                            LG[:, s, 4:36].rearrange("p (g e) -> p g e", g=4),
                            R2[:, s, 0:4].unsqueeze(2).to_broadcast([P, 4, 8]), ALU.add)
                    link(ins)
                    x = R4[:, :, :]
                link(v.tensor_reduce(RV[:, 2, :], x, AX.X, ALU.max))
                first_max(x, RV[:, 2, :], ne, R5, R3, RV[:, 1, :])
                link(v.scalar_tensor_tensor(out=R3[:, :, 0:ne], in0=R5[:, :, 0:ne], scalar=-1e32, in1=x,
                                            op0=ALU.mult, op1=ALU.add))
                link(v.tensor_reduce(RV[:, 3, :], R3[:, :, 0:ne], AX.X, ALU.max))
                first_max(R3[:, :, 0:ne], RV[:, 3, :], ne, R2, R2, RV[:, 1, :])
                if tag == "m2":
                    v.tensor_tensor(MASK[:, :, :], R5[:, :, 0:E2], R2[:, :, 0:E2], ALU.add).then_inc(
                        S("mask"), 1)
                v.memset(RV[:, 5, :], 0.0)
                v.tensor_tensor(RV[:, 4, :], RV[:, 3, :], RV[:, 2, :], ALU.subtract).then_inc(S("re"), 1)
                dve.wait_ge(S("rx"), {"m0": 2, "m1": 4, "m2": 5}[tag])
                link(v.tensor_scalar(RV[:, 8, :], RV[:, 6, :], 1.0, None, ALU.add))
                if tag != "m2":
                    link(v.tensor_reduce(RV[:, 9, :], R1[:, :, 0:4], AX.X, ALU.add))
                    link(v.tensor_tensor(RV[:, 8, :], RV[:, 8, :], RV[:, 9, :], ALU.mult))
                link(v.reciprocal(RV[:, 9, :], RV[:, 8, :]))
                link(v.tensor_tensor(RV[:, 10, :], RV[:, 9, :], RV[:, 6, :], ALU.mult))
                bc = lambda r: RV[:, r, :].unsqueeze(2).to_broadcast([P, 2, ne])
                v.tensor_tensor(R5[:, :, 0:ne], R5[:, :, 0:ne], bc(9), ALU.mult)
                link(v.tensor_tensor(R2[:, :, 0:ne], R2[:, :, 0:ne], bc(10), ALU.mult))
                link(v.tensor_tensor(CTOK[:, :, 0:ne], R5[:, :, 0:ne], R2[:, :, 0:ne], ALU.add))

            def moe(tag, gate=None):
                sets, n, by_chunk = MOE[tag]
                wmax = W1 if by_chunk else W2
                if by_chunk:
                    link(v.tensor_reduce(COMBL[:, :, :], CTOK[:, :, :].rearrange("p s (g e) -> p s e g", g=4),
                                         AX.X, ALU.add))
                dve.wait_ge(S("count"), NTH[tag] + 1)
                dve.wait_ge(S("mask"), NTH[tag] + 1)
                pos = POS[:, :, 0:sets]
                link(v.tensor_tensor(pos, PSB[3][:, 0:16].rearrange("p (s n) -> p s n", s=2)[:, :, 0:sets],
                                     MASK[:, :, 0:sets], ALU.mult))
                link(v.tensor_scalar(pos, pos, -1.0, None, ALU.add))
                cnt, own, upto, before = (WRK[:, 8 * i:8 * i + sets] for i in range(4))
                sq = [WRK[:, 32 + 104 * i:32 + 104 * i + wmax * sets].rearrange("p (w s) -> p w s", w=wmax)
                      for i in range(5)]
                by_item = lambda ap: ap.unsqueeze(1).to_broadcast([P, wmax, sets])
                link(v.tensor_copy(cnt, PSB[3][:, 16:16 + sets]))
                link(v.tensor_scalar(own, cnt, float(CAP), 1.0, ALU.is_gt, ALU.add))
                link(v.scalar_tensor_tensor(out=own, in0=cnt, scalar=float(2 * CAP), in1=own, op0=ALU.is_gt,
                                            op1=ALU.add))
                link(v.tensor_tensor_scan(upto, own, con("zero")[:, 0:sets], 0.0, ALU.add, ALU.add))
                link(v.tensor_tensor(before, upto, own, ALU.subtract))
                link(v.tensor_tensor(sq[0], con("iota")[:, 0:wmax].unsqueeze(2).to_broadcast([P, wmax, sets]),
                                     by_item(before), ALU.subtract))
                link(v.tensor_tensor(sq[1], sq[0], by_item(own), ALU.is_lt))
                link(v.scalar_tensor_tensor(out=sq[1], in0=sq[0], scalar=0.0, in1=sq[1], op0=ALU.is_ge,
                                            op1=ALU.mult))
                link(v.scalar_tensor_tensor(out=sq[2], in0=sq[0], scalar=float(CAP), in1=sq[1], op0=ALU.mult,
                                            op1=ALU.mult))
                for s in range(2):
                    link(v.tensor_tensor(sq[3], sq[1], by_item(POS[:, s, 0:sets]), ALU.mult))
                    link(v.tensor_tensor(sq[3], sq[3], sq[2], ALU.subtract))
                    link(v.tensor_reduce(IPOS[:, s, 0:wmax], sq[3], AX.X, ALU.add))
                    if not by_chunk:
                        link(v.tensor_tensor(sq[4], sq[1], by_item(CTOK[:, s, 0:sets]), ALU.mult))
                        link(v.tensor_reduce(IWT[:, s, 0:wmax], sq[4], AX.X, ALU.add))
                link(v.tensor_tensor(sq[3], sq[1], by_item(con("iota")[:, 0:sets]), ALU.mult))
                link(v.tensor_reduce(WRK[:, 560:560 + wmax], sq[3], AX.X, ALU.add))
                v.tensor_scalar(FIRST[:, 0:wmax], WRK[:, 560:560 + wmax], float(n), None, ALU.mult)
                v.tensor_copy(ITEMS[:, :], upto[:, sets - 1:sets]).then_inc(S("plan"), 1)
                dve.wait_ge(S("plan"), NTH[tag] + 1)
                items = dve.value_load(ITEMS[0:1, 0:1], min_val=sets, max_val=wmax)

                v.memset(IPOS[:, :, wmax:wmax + 1], -1.0)
                if not by_chunk:
                    v.memset(IWT[:, :, wmax:wmax + 1], 0.0)
                v.memset(LAM[:, 8:9], 0.0).then_inc(S(f"added_{tag}"), 1)
                dve.wait_ge(S(f"added_{tag}"), 1)

                def pick(w):
                    at = slice(w, w + 1) if isinstance(w, int) else bass.ds(w, 1)
                    for s in range(2):
                        ins = v.tensor_scalar(PICK[:, s, :], con("iota"), IPOS[:, s, at], None,
                                              ALU.is_equal)
                    ins.then_inc(S(f"pick_{tag}"), 1)
                    dve.wait_ge(S(f"pick_{tag}"), w * 2 + 1)
                    for s in range(2):
                        if by_chunk:
                            ins = v.tensor_tensor(
                                PICKE[:, s, :, :], PICK[:, s, :].unsqueeze(1).to_broadcast([P, 8, CAP]),
                                COMBL[:, s, :].unsqueeze(2).to_broadcast([P, 8, CAP]), ALU.mult)
                        else:
                            ins = v.tensor_scalar(PICKW[:, s, :], PICK[:, s, :], IWT[:, s, at], None,
                                                  ALU.mult)
                    ins.then_inc(S(f"pick_{tag}"), 1)

                pick(0)
                with dve.Fori(0, items) as w:
                    if by_chunk:
                        dve.wait_ge(S(f"cbg_mm_{tag}"), w + 1)
                        for b in range(2):
                            ins = v.tensor_copy(CBG[:, 4 * b:4 * b + 4, :].rearrange("p e n -> p (e n)"),
                                                PSB[4 + b][:, 0:4 * CAP])
                        ins.then_inc(S(f"cbg_{tag}"), 1)
                        dve.wait_ge(S(f"cbg_{tag}"), w + 1)
                    for c in range(n):
                        if c == n - 1:
                            pick(w + 1)
                        dve.wait_ge(S(f"silu_{tag}"), w * n + (c + 1))
                        if c >= 2:
                            dve.wait_ge(S(f"f_used_{tag}"), w * n + (c - 1))
                        v.tensor_tensor(A2[:, c % 2, :, 0:CAP], A1[:, c % 2, :, 0:CAP],
                                        PSB[2 * (c % 2) + 1][:, 0:2 * CAP].rearrange("p (s n) -> p s n", s=2),
                                        ALU.mult).then_inc(S(f"up_{tag}"), 1)
                        if by_chunk:
                            dve.wait_ge(S(f"up_{tag}"), w * n + (c + 1))
                            v.tensor_tensor(A3[:, c % 2, :, 0:CAP], A2[:, c % 2, :, 0:CAP],
                                            CBG[:, c:c + 1, :].to_broadcast([P, 2, CAP]), ALU.mult).then_inc(
                                                S(f"a3_{tag}"), 1)
                    dve.wait_ge(S(f"spread_{tag}"), w + 1)
                    for b in range(4):
                        if gate is None:
                            ins = v.tensor_tensor(X[:, 2 * b:2 * b + 2, :], two(PSB[4 + b][:, :]),
                                                  X[:, 2 * b:2 * b + 2, :], ALU.add)
                        else:
                            for s in range(2):
                                c = 2 * b + s
                                ins = v.scalar_tensor_tensor(out=X[:, c, :], in0=PSB[4 + b][:, s * T:s * T + T],
                                                             scalar=gate[:, c:c + 1], in1=X[:, c, :],
                                                             op0=ALU.mult, op1=ALU.add)
                    ins.then_inc(S(f"added_{tag}"), 1)
                    dve.wait_ge(S(f"added_{tag}"), w + 2)
                v.memset(WRK[:, 0:1], 0.0).then_inc(S("moe_done"), 1)

            def ffn(tag, n):
                def chunk(c, par, first=False):
                    dve.wait_ge(S(f"silu_{tag}"), c + 1)
                    if not first:
                        dve.wait_ge(S(f"f_used_{tag}"), c - 1)
                    v.tensor_tensor(A2[:, par, :, :], A1[:, par, :, :], two(PSB[2 * par + 1][:, :]),
                                    ALU.mult).then_inc(S(f"up_{tag}"), 1)

                chunk(0, 0, True)
                chunk(1, 1, True)
                with dve.Fori(0, (n - 2) // 2) as i:
                    for j in range(2):
                        chunk(i * 2 + (2 + j), j)
                if n % 2:
                    chunk(n - 1, (n - 1) % 2)
                dve.wait_ge(S(f"f_used_{tag}"), n)
                for b in range(4):
                    ins = v.tensor_tensor(X[:, 2 * b:2 * b + 2, :], two(PSB[4 + b][:, :]),
                                          X[:, 2 * b:2 * b + 2, :], ALU.add)
                link(ins)

            dve.wait_ge(S("con_in"), 16)
            dve.wait_ge(S("small_in"), 96)
            link(v.tensor_copy(SM[:, 0, 1, :], SM[:, 0, 0, :].bitcast(I32)))
            link(v.tensor_scalar(SM[:, 1, 0, :], SM[:, 0, 1, :], con("invfreq"), None, ALU.mult))
            link(v.tensor_scalar(SM[:, 1, 1, :], SM[:, 1, 0, :], 1.0 / (2 * math.pi), None, ALU.mult))
            magic = 1.5 * 2.0 ** 23
            link(v.tensor_scalar(SM[:, 1, 1, :], SM[:, 1, 1, :], magic, None, ALU.add))
            link(v.tensor_scalar(SM[:, 1, 1, :], SM[:, 1, 1, :], magic, None, ALU.subtract))
            p1 = 6.28125
            p2 = round((2 * math.pi - p1) * 2 ** 20) / 2 ** 20
            for part in (p1, p2, 2 * math.pi - p1 - p2):
                link(v.scalar_tensor_tensor(out=SM[:, 1, 0, :], in0=SM[:, 1, 1, :], scalar=-part,
                                            in1=SM[:, 1, 0, :], op0=ALU.mult, op1=ALU.add))
            v.tensor_scalar(SM[:, 1, 0, :], SM[:, 1, 0, :], 3.141592, -3.141592, ALU.min, ALU.max).then_inc(
                S("angle"), 1)
            dve.wait_ge(S("angle"), 1)
            v.scalar_tensor_tensor(out=SM[:, 0, 0, :], in0=SM[:, 1, 0, :], scalar=-1.0, in1=SM[:, 1, 0, :],
                                   op0=ALU.mult, op1=ALU.max).then_inc(S("angle"), 1)
            for i in range(2):
                ins = v.tensor_tensor_reduce(out=PR[:, 0, i, 0:64], in0=LAMR[:, 128 * i:128 * i + 64],
                                             in1=LAMR[:, 128 * i + 64:128 * i + 128], scale=1.0, scalar=0.0,
                                             op0=ALU.mult, op1=ALU.add, accum_out=LAM[:, i:i + 1])
            ins.then_inc(S("lam_dot"), 1)
            dve.wait_ge(S("lam_exp"), 1)
            dve.wait_ge(S("cols"), 1)
            lam_init = 0.8 - 0.6 * math.exp(0.0)
            v.scalar_tensor_tensor(out=LAM[:, 4:5], in0=LAM[:, 3:4], scalar=-lam_init, in1=LAM[:, 2:3],
                                   op0=ALU.add, op1=ALU.subtract)
            v.tensor_scalar(LAM[:, 5:6], col("subln"), 1.0 - lam_init, None, ALU.mult)
            v.memset(LAM[:, 8:9], 0.0).then_inc(S("mods"), 1)
            dve.wait_ge(S("cact"), 1)

            def fold(i, r):
                dve.wait_ge(S(f"ada_in{r}"), i * 16 + 16)
                for k in range(KC):
                    for j in range(2):
                        if k:
                            dve.wait_ge(S("folds"), i * (4 * KC) + (2 * KC * r + 2 * k - 1 + j))
                        w, acc = WF[r][:, j, k * NTILE:(k + 1) * NTILE], FOLD[:, r, j, :]
                        if k == 0:
                            ins = v.tensor_scalar(acc, w, CACT[:, 0:1], None, ALU.mult)
                        else:
                            ins = v.scalar_tensor_tensor(out=acc, in0=w, scalar=CACT[:, k:k + 1], in1=acc,
                                                         op0=ALU.mult, op1=ALU.add)
                        ins.then_inc(S("folds"), 1)

            def take(i, r):
                dve.wait_ge(S("ada_cols"), i * 2 + (r + 1))
                a = i * (4 * ADA_R) + 2 * ADA_R * r
                b = a + COL["ada_b"]
                dst, bias = ((MODS[:, a:a + 2 * ADA_R], COLS[:, b:b + 2 * ADA_R]) if isinstance(i, int)
                             else (MODS[:, bass.ds(a, 2 * ADA_R)], COLS[:, bass.ds(b, 2 * ADA_R)]))
                v.tensor_tensor(dst, PSB[1 + r][:, 0:2 * ADA_R], bias, ALU.add).then_inc(S("mods"), 1)

            fold(0, 0)
            with dve.Fori(0, ADA_N // 2 - 1) as i:
                fold(i, 1)
                take(i, 0)
                fold(i + 1, 0)
                take(i, 1)
            last_pair = ADA_N // 2 - 1
            fold(last_pair, 1)
            take(last_pair, 0)
            take(last_pair, 1)
            dve.wait_ge(S("mods"), ADA_N + 1)
            for i in range(4):
                ins = v.scalar_tensor_tensor(out=AG[:, i, :], in0=mods(i // 2, 1 + 3 * (i % 2)), scalar=1.0,
                                             in1=cols8("norm_g", i), op0=ALU.add, op1=ALU.mult)
            link(ins)
            dve.wait_ge(S("x_cp"), 8)

            norm("n0")
            dve.wait_ge(S("tables"), 2)
            rope("r0", rope_pairs(0))
            attend("a0")
            dve.wait_ge(S("outputs"), outputs_of("a0", 8))
            group_squares("g0", 4)
            for r in range(4):
                dve.wait_ge(S("group_rms"), 2 * (r + 1))
                for s in range(2):
                    c = 2 * r + s
                    ins = v.scalar_tensor_tensor(out=O[:, c, :], in0=O[:, c, :], scalar=LAM[:, 5:6],
                                                 in1=RS[:, s, :], op0=ALU.mult, op1=ALU.mult)
                ins.then_inc(S("group_done"), 1)
            for i in range(4):
                residual("diff_o", i, mods(0, 2))
            norm("m0")
            route("m0", 0, 36)
            moe("m0", mods(0, 5))

            norm("n1")
            dve.wait_ge(S("lin_act"), emptied("act", LIN0["nsa_kv"]))
            for kv in range(2):
                z = CMPZ[:, kv].rearrange("p a t -> p (a t)")[:, 0:496].rearrange("p (m n) -> p m n", m=16)
                for g in range(2):
                    src = K[64 * g:64 * g + 64, kv, :].rearrange("p (a r) -> p a r", r=16)
                    for par in range(2):
                        for mh in range(2):
                            v.tensor_copy(z[64 * par:64 * par + 64, 8 * mh:8 * mh + 8,
                                            15 * g:15 * g + 15].rearrange("p m n -> p n m"),
                                          src[:, mh:mh + 15, par:16:2])
                v.tensor_copy(z[:, :, 30:31], COLS[:, COL["cmp_pos"] + 16 * kv:COL["cmp_pos"] + 16 * kv + 16]
                              .unsqueeze(2)).then_inc(S("cmpz"), 1)
            rope("r1", rope_pairs(1))
            dve.wait_ge(S("a_used"), TILE0["cmp"] + 4)
            v.tensor_tensor(H1[:, :, :, 0].rearrange("p a b -> p (a b)"), PSB[6][:, 30:128:32],
                            COLS[:, COL["cmp_b1"]:COL["cmp_b1"] + 4], ALU.add).then_inc(S("h1b"), 1)
            dve.wait_ge(S("cmp_out"), 1)
            for g in range(2):
                a = slice(64 * g, 64 * g + 64)
                v.tensor_copy(KCMP[a, 0:15], PSB[3][a, 15 * g:15 * g + 15])
            v.tensor_copy(VCMP[0:15, :, :], PSB[3][0:15, 64:192].rearrange("p (g d) -> p g d", g=2)).then_inc(
                S("cmp_kv"), 2)
            dve.wait_ge(S("gates"), 1)
            attend("a1")
            for i in range(4):
                residual("nsa_o", i, mods(1, 2))
            norm("m1")
            route("m1", 1, 36)
            moe("m1", mods(1, 5))
            norm("f1")

            for l in range(2):
                norm(f"x{l}")
                v.memset(RAW[:, :, 0:3], 0.0).then_inc(S("pads"), 1)
                v.memset(CPAD[:, :, 0:30], 0.0).then_inc(S("pads"), 1)
                dve.wait_ge(S("pads"), 2 * l + 2)
                dve.wait_ge(S("lin_act"), emptied("act", LIN0[f"mix_in{l}"] + 1))
                for j in range(4):
                    for c in range(4):
                        acc = SM[:, c // 2, c % 2, :]
                        w = col("ml_w", 16 * l + 4 * j + c)
                        if j == 0:
                            ins = v.tensor_scalar(acc, RAW[:, c, 0:T], w, col("ml_b", 4 * l + c),
                                                  ALU.mult, ALU.add)
                        else:
                            ins = v.scalar_tensor_tensor(out=acc, in0=RAW[:, c, j:j + T], scalar=w, in1=acc,
                                                         op0=ALU.mult, op1=ALU.add)
                    if j < 3:
                        link(ins)
                ins.then_inc(S("conv_ml"), 1)
                dve.wait_ge(S("pre"), l + 1)
                dve.wait_ge(S("pre_zero"), 1)
                z = PRE[:, 1:3, :]
                v.scalar_tensor_tensor(out=PRE[:, 7:9, :], in0=z, scalar=-1.0, in1=z, op0=ALU.mult,
                                       op1=ALU.max).then_inc(S("pre_abs"), 1)
                dve.wait_ge(S("pre_ln"), 2 * l + 2)
                link(v.scalar_tensor_tensor(out=z, in0=z, scalar=0.0, in1=PRE[:, 7:9, :], op0=ALU.min,
                                            op1=ALU.subtract))
                zero = con("zero", rows=8)
                v.tensor_tensor_scan(PRE[:, 7, :], PRE[:, 2, :], zero, 0.0, ALU.add, ALU.add)
                link(v.tensor_tensor_scan(PRE[0:4, 3, :], PRE[0:4, 1, :], zero[0:4, :], 0.0, ALU.add, ALU.add))
                v.tensor_scalar(PRE[:, 9, :], PRE[:, 7, :], -8.0, None, ALU.mult)
                link(v.tensor_tensor(PRE[0:4, 4, :], PRE[0:4, 0, :], PRE[0:4, 3, :], ALU.subtract))
                link(v.tensor_tensor_scan(PRE[0:4, 5, :], PRE[0:4, 4, :], PRE[0:4, 4, :], 0.0, ALU.max, ALU.max))
                v.tensor_tensor(PRE[0:4, 6, :], PRE[0:4, 3, :], PRE[0:4, 5, :], ALU.add).then_inc(
                    S("pre_rows"), 1)
                dve.wait_ge(S("mcol"), 2 * l + 2)
                dve.wait_ge(S("qk_ml"), 4 * l + 4)
                attend(f"mix{l}")
                dve.wait_ge(S("outputs"), outputs_of(f"mix{l}", 2))
                group_squares(f"gm{l}", 1)
                dve.wait_ge(S("group_rms"), 2 * (GROUPED[f"gm{l}"] + 1))
                link(v.tensor_tensor(O[:, 0:2, :], O[:, 0:2, :], RS[:, :, :], ALU.mult))
                for c in range(2):
                    ins = v.scalar_tensor_tensor(out=O[:, c, :], in0=O[:, c, :], scalar=col("ml_norm", 2 * l + c),
                                                 in1=Q[:, 2 + c, :], op0=ALU.mult, op1=ALU.mult)
                ins.then_inc(S("cat"), 1)
                dve.wait_ge(S("ln_mm"), 2 * l + 1)
                link(v.tensor_tensor(LNM[:, :, :], LNM[:, :, :], over2(PSB[6][:, 0:T]), ALU.subtract))
                v.tensor_tensor(SQ[:, 6:8, :], LNM[:, :, :], LNM[:, :, :], ALU.mult).then_inc(S("ln_sq"), 1)
                dve.wait_ge(S("ln_rs"), 2 * l + 2)
                v.tensor_tensor(LNM[:, :, :], LNM[:, :, :], over2(RS[:, 0, :]), ALU.mult).then_inc(
                    S("ln_out"), 1)
                for i in range(4):
                    residual(f"mix_o{l}", i)
                norm(f"mem{l}")
                norm(f"xa{l}")
                attend(f"xt{l}")
                for i in range(4):
                    residual(f"x_o{l}", i)
                tag = "d0" if l == 0 else "m2"
                norm(tag)
                if l == 0:
                    ffn(tag, M2)
                else:
                    route(tag, 2, E2)
                    moe(tag)
            norm("y")


def constants():
    c = {n: np.zeros((P, k), np.float32) for n, k in CONSTS}
    i = np.arange(P)
    c["ident"][i, i] = 1.0
    c["mean_d"][:] = 1.0 / D
    c["mean_128"][:] = 1.0 / 128
    c["mean_256"][:] = 1.0 / 256
    c["mean_64"][:] = (i[:, None] // 64 == i[None, :] // 64) / 64.0
    for p in range(P):
        r = p % 64
        if r < 8:
            c["rope"][p + 8, p] = -1.0
            c["invfreq"][p] = np.float32(500000.0) ** np.float32(-2.0 * r / 16)
        elif r < 16:
            c["rope"][p - 8, p] = 1.0
            c["invfreq"][p] = np.float32(500000.0) ** np.float32(-2.0 * (r - 8) / 16)
    diag = np.where(i[:, None] >= i[None, :], 0.0, NEG)
    c["causal"][:, 0:P] = diag
    c["causal"][:, 2 * P:3 * P] = diag
    for s in range(2):
        ok = 16 * np.arange(15)[None, :] + 31 <= (i + P * s)[:, None]
        c["cmp_mask"][:, 16 * s:16 * s + 15] = np.where(ok, 0.0, NEG)
        c["cmp_valid"][:, s] = ok.any(1)
    c["iota"][:] = np.arange(96)
    c["tri"][:] = i[:, None] <= i[None, :]
    c["ones"][:] = 1.0
    c["eps"][:] = EPS
    c["halfpi"][:] = math.pi / 2
    for h in range(8):
        c["sel"][h, h * P:(h + 1) * P] = 1.0
    return np.concatenate([c[n] for n, _ in CONSTS], axis=1)


def tiles(w, nc_=NTILE):
    k, n = w.shape
    return np.ascontiguousarray(w.reshape(k // P, P, n // nc_, nc_).transpose(2, 1, 0, 3)).reshape(
        n // nc_, P, k // P * nc_)


def small(w):
    return tiles(np.ascontiguousarray(w), w.shape[1])[0]


def ffn_chunks(gate, up, down):
    e, d, f = gate.shape
    m = f // HID
    out = np.empty((e, m, P, 3, NFREE), np.float32)
    for a, w in enumerate((gate, up)):
        out[:, :, :, a] = w.reshape(e, KC, P, m, HID).transpose(0, 3, 2, 1, 4).reshape(e, m, P, NFREE)
    out[:, :, :, 2] = down.reshape(e, m, 2, P, D).transpose(0, 1, 3, 2, 4).reshape(e, m, P, NFREE)
    return out.reshape(m * e, P, 3 * NFREE)


def lay_out(x):
    a = {}
    a["x"] = x["x"][0]
    a["mem"] = x["mem_2"][0]
    a["consts"] = constants()
    r = lambda v: np.asarray(v).reshape(-1, P)
    rows = {"ada_b": r(x["ada_b"]), "c": r(x["c"]), "cmp_b1": r(x["nsa_cmp_b1"]), "subln": r(x["diff_subln_g"]),
            "norm_g": r(x["norm_g"]), "final_g": r(x["final_g"]), "norm_mix": r(x["norm_mix_w_2"]),
            "norm_x": r(x["norm_xattn_w_2"]), "norm_mem": r(x["norm_mem_w_2"]), "norm_ffn": r(x["norm_ffn_w_2"]),
            "norm_final": r(x["norm_final_w_2"]), "conf_w": r(x["conf_conv_w_2"]), "ml_w": r(x["mlstm_conv_w_2"]),
            "ml_b": r(x["mlstm_conv_b_2"]), "conf_b": r(x["conf_conv_b_2"]), "ln_w": r(x["conf_ln_w_2"]),
            "ln_b": r(x["conf_ln_b_2"]), "ml_norm": r(x["mlstm_norm_w_2"]), "cmp_pos": r(x["nsa_cmp_pos"])}
    for i, names in enumerate(ROW_TILES):
        a[f"rows{i}"] = np.concatenate([rows[n] for n, _ in names])
    a["pos"] = np.asarray(x["positions"]).reshape(1, T)
    a["lam"] = x["diff_lambda"].reshape(1, 256)
    route_b = np.zeros((1, 108), np.float32)
    for l in range(2):
        route_b[0, 36 * l:36 * l + 4] = x["moe_b_group"][l]
        route_b[0, 36 * l + 4:36 * l + 36] = x["moe_b_expert"][l].reshape(-1)
    a["route_b"] = route_b
    pre_b = np.zeros((8, 6), np.float32)
    for l in range(2):
        pre_b[0:4, 3 * l] = x["mlstm_b_i_2"][l]
        pre_b[0:4, 3 * l + 1] = x["mlstm_b_f_2"][l]
        pre_b[0:8, 3 * l + 2] = x["fox_b_f_2"][l]
    a["pre_b"] = pre_b
    w2 = x["nsa_cmp_w2"][0].reshape(2, 2, P, 64)
    a["cmp_w2"] = np.concatenate([w2, w2], axis=3).transpose(2, 0, 1, 3).reshape(P, 512)
    nsa = x["nsa_w_in"][0]
    win = x["w_in_2"]
    group = [np.concatenate([x["moe_w_group"][l], x["moe_w_expert"][l].transpose(1, 0, 2).reshape(D, E1)], axis=1)
             for l in range(2)]
    a["small"] = np.concatenate(
        [small(nsa[:, 1792:1840]), small(group[0]), small(group[1]), small(x["router_w_2"][0])]
        + [small(np.concatenate([win[l][:, 1024:1032], win[l][:, 3080:3088]], axis=1)) for l in range(2)], axis=1)
    order = np.arange(1024).reshape(2, 8, 64).transpose(1, 0, 2).reshape(-1)
    parts = [tiles(x["diff_w_in"][0]), tiles(x["diff_w_out"][0]),
             tiles(np.ascontiguousarray(nsa[:, 1024:1792])), tiles(nsa[:, 0:1024][:, order])]
    w1 = x["nsa_cmp_w1"][0].reshape(2, 2, 8, P, 256).transpose(0, 1, 3, 2, 4).reshape(4, P, NFREE)
    parts += [w1, tiles(x["nsa_w_out"][0][order])]
    for l in range(2):
        main = np.concatenate([win[l][:, 0:1024], win[l][:, 1032:3080]], axis=1)
        parts += [tiles(main), tiles(x["w_out_2"][l]), tiles(x["xattn_w_q_2"][l]), tiles(x["xattn_w_kv_2"][l])]
    a["wa"] = np.concatenate(parts)
    ada = np.concatenate([tiles(x["ada_w"][0]), tiles(x["ada_w"][1])])
    a["ada"] = ada.reshape(ADA_N, ADA_R, P, NFREE).transpose(0, 2, 1, 3).reshape(ADA_N, P, ADA_R * NFREE)
    a["xo"] = np.concatenate([tiles(x["xattn_w_o_2"][l]) for l in range(2)])
    for l in range(2):
        a[f"wf{l}"] = ffn_chunks(x["moe_w_gate"][l], x["moe_w_up"][l], x["moe_w_down"][l])
    a["wf2"] = ffn_chunks(x["ffn_w_gate_2"], x["ffn_w_up_2"], x["ffn_w_down_2"])
    a["wf3"] = ffn_chunks(x["moe_w_gate_2"][0], x["moe_w_up_2"][0], x["moe_w_down_2"][0])
    return {k: np.ascontiguousarray(v) for k, v in a.items()}


def kernel(**inputs):
    import concourse.bacc as bacc
    from concourse.bass_utils import run_bass_kernel_spmd

    arrays = lay_out({k: np.asarray(v) for k, v in inputs.items()})
    nc = bacc.Bacc("TRN2", target_bir_lowering=False, num_devices=1, dynamic_dma_scratch_size=4096)
    t = {n: nc.dram_tensor(f"in_{n}", a.shape, mybir.dt.from_np(a.dtype), kind="ExternalInput").ap()
         for n, a in arrays.items()}
    t["out"] = nc.dram_tensor("out", (T, D), F32, kind="ExternalOutput").ap()
    build(nc, t)
    r = run_bass_kernel_spmd(nc, [{f"in_{n}": a for n, a in arrays.items()}], core_ids=[0])
    return r.results[0]["out"].reshape(1, T, D)
```
